# Optimizing a Trainium2 kernel written in Bass

```python
import jax, jax.numpy as jnp
from jax import lax
import numpy as np

D_MODEL = 1024
BATCH = 1
SEQ = 256
DEPTH = 2

GRID_W = 64
CTX_LEN = 256
N_EVEN = (DEPTH + 1) // 2
N_ODD = DEPTH // 2

MLA_HEADS = 8
QK_NOPE_DIM = 64
QK_ROPE_DIM = 32
QK_HEAD_DIM = QK_NOPE_DIM + QK_ROPE_DIM
V_HEAD_DIM = 64
Q_LORA_RANK = 384
KV_LORA_RANK = 256
QK_SCALE = QK_HEAD_DIM ** -0.5
ROPE_BASE = 10000.0
BLOCK_Q = 128
CONV_GROUPS = 8
CONV_GROUP_DIM = 64
CONV_DIM = CONV_GROUPS * CONV_GROUP_DIM
CONV_WIDTH = 3
CONV_OFFSET = Q_LORA_RANK + KV_LORA_RANK + QK_ROPE_DIM
IN_PROJ_DIM = CONV_OFFSET + 3 * CONV_DIM
MIX_OUT_DIM = MLA_HEADS * V_HEAD_DIM + CONV_DIM
FOURIER_GROUPS = 4
FOURIER_GROUP_DIM = D_MODEL // FOURIER_GROUPS
D_FF = ((8 * D_MODEL + 3 * 256 - 1) // (3 * 256)) * 256
EPS = 1e-6


def rmsnorm(x, g):
    xf = x.astype(jnp.float32)
    y = xf * lax.rsqrt(jnp.mean(xf * xf, axis=-1, keepdims=True) + EPS)
    return (y * g.astype(jnp.float32)).astype(x.dtype)

def axial_angles(T):
    rows = T // GRID_W
    row = jnp.broadcast_to(jnp.arange(rows)[:, None], (rows, GRID_W)).reshape(-1).astype(jnp.float32)
    col = jnp.broadcast_to(jnp.arange(GRID_W)[None, :], (rows, GRID_W)).reshape(-1).astype(jnp.float32)
    half = QK_ROPE_DIM // 2
    inv = 1.0 / (ROPE_BASE ** (jnp.arange(0, half, 2, dtype=jnp.float32) / half))
    return row[:, None] * inv, col[:, None] * inv

def rotate(x, ang):
    cos = jnp.cos(ang)[:, None, :].astype(x.dtype)
    sin = jnp.sin(ang)[:, None, :].astype(x.dtype)
    x1, x2 = jnp.split(x, 2, axis=-1)
    return jnp.concatenate([x1 * cos - x2 * sin, x2 * cos + x1 * sin], axis=-1)

def axial_rope(x, ang_row, ang_col):
    half = QK_ROPE_DIM // 2
    return jnp.concatenate([rotate(x[..., :half], ang_row), rotate(x[..., half:], ang_col)], axis=-1)

def mla_qkv(proj, q_norm_g, kv_norm_g, w_uq, w_ukv, q_gain, k_gain, angles):
    B, T, _ = proj.shape
    cq = proj[..., :Q_LORA_RANK]
    ckv = proj[..., Q_LORA_RANK:Q_LORA_RANK + KV_LORA_RANK]
    k_pe = proj[..., Q_LORA_RANK + KV_LORA_RANK:CONV_OFFSET]
    q = (rmsnorm(cq, q_norm_g) @ w_uq).reshape(B, T, MLA_HEADS, QK_HEAD_DIM)
    kv = (rmsnorm(ckv, kv_norm_g) @ w_ukv).reshape(B, T, MLA_HEADS, QK_NOPE_DIM + V_HEAD_DIM)
    k_nope, v = kv[..., :QK_NOPE_DIM], kv[..., QK_NOPE_DIM:]
    k = jnp.concatenate([k_nope, jnp.broadcast_to(k_pe[:, :, None, :], (B, T, MLA_HEADS, QK_ROPE_DIM))], axis=-1)
    q = rmsnorm(q, q_gain)
    k = rmsnorm(k, k_gain)
    if angles is not None:
        ang_row, ang_col = angles
        q = jnp.concatenate([q[..., :QK_NOPE_DIM], axial_rope(q[..., QK_NOPE_DIM:], ang_row, ang_col)], axis=-1)
        k = jnp.concatenate([k[..., :QK_NOPE_DIM], axial_rope(k[..., QK_NOPE_DIM:], ang_row, ang_col)], axis=-1)
    return q, k, v

def attend(q, k, v):
    s = jnp.einsum('bqhd,bkhd->bhqk', q, k, preferred_element_type=jnp.float32) * QK_SCALE
    p = jax.nn.softmax(s, axis=-1)
    return jnp.einsum('bhqk,bkhd->bqhd', p.astype(v.dtype), v)

def attend_blocked(q, k, v):
    B, S, H, D = q.shape
    nb = S // BLOCK_Q
    qb = q.reshape(B, nb, BLOCK_Q, H, D).transpose(1, 0, 2, 3, 4)
    ob = lax.map(lambda qi: attend(qi, k, v), qb)
    return ob.transpose(1, 0, 2, 3, 4).reshape(B, S, H * V_HEAD_DIM)

def short_conv(p, conv_w):
    b_gate, c_gate, u = jnp.split(p, 3, axis=-1)
    z = c_gate * u
    T = z.shape[1]
    zp = jnp.pad(z, ((0, 0), (1, 1), (0, 0)))
    y = zp[:, 0:T] * conv_w[0] + zp[:, 1:T + 1] * conv_w[1] + zp[:, 2:T + 2] * conv_w[2]
    return b_gate * y

def even_mixer(h_lat, h_ctx, w_in, q_norm_g, kv_norm_g, w_uq, w_ukv, q_gain, k_gain, conv_w, w_o, with_ctx_out):
    B, S, _ = h_lat.shape
    L = h_ctx.shape[1]
    p_lat = h_lat @ w_in
    p_ctx = h_ctx @ w_in
    q_l, k_l, v_l = mla_qkv(p_lat, q_norm_g, kv_norm_g, w_uq, w_ukv, q_gain, k_gain, axial_angles(S))
    q_c, k_c, v_c = mla_qkv(p_ctx, q_norm_g, kv_norm_g, w_uq, w_ukv, q_gain, k_gain, None)
    k_all = jnp.concatenate([k_l, k_c], axis=1)
    v_all = jnp.concatenate([v_l, v_c], axis=1)
    a_l = attend_blocked(q_l, k_all, v_all)
    s_l = short_conv(p_lat[..., CONV_OFFSET:], conv_w)
    out_l = jnp.concatenate([a_l, s_l], axis=-1) @ w_o
    if not with_ctx_out:
        return out_l, None
    a_c = attend(q_c, k_c, v_c).reshape(B, L, MLA_HEADS * V_HEAD_DIM)
    s_c = short_conv(p_ctx[..., CONV_OFFSET:], conv_w)
    out_c = jnp.concatenate([a_c, s_c], axis=-1) @ w_o
    return out_l, out_c

def fourier_mixer(h, w_f):
    B, T, _ = h.shape
    hg = h.astype(jnp.float32).reshape(B, T, FOURIER_GROUPS, FOURIER_GROUP_DIM)
    f = jnp.fft.fft2(hg, axes=(1, 3), norm="ortho").real
    return f.reshape(B, T, D_MODEL).astype(h.dtype) @ w_f

def swiglu(h, w1, w3, w2):
    return (jax.nn.silu(h @ w1) * (h @ w3)) @ w2

def ada(cvec, w, b):
    return jnp.split(jax.nn.silu(cvec) @ w + b, 6, axis=-1)

def first_inputs(seed: int = 0) -> dict:
    key = jax.random.key(seed)
    ks = jax.random.split(key, 24)
    nrm = jax.random.normal
    f32 = jnp.float32
    D = D_MODEL
    return {
        "x": nrm(ks[0], (BATCH, SEQ, D), f32),
        "c": nrm(ks[1], (BATCH, D), f32),
        "ctx": nrm(ks[2], (BATCH, CTX_LEN, D), f32),
        "c_ctx": nrm(ks[3], (D,), f32),
        "ada_w": nrm(ks[4], (DEPTH, D, 6 * D), f32) * D ** -0.5,
        "ada_b": nrm(ks[5], (DEPTH, 6 * D), f32) * 0.01,
        "norm1_g": 1.0 + 0.02 * nrm(ks[6], (DEPTH, D), f32),
        "norm2_g": 1.0 + 0.02 * nrm(ks[7], (DEPTH, D), f32),
        "w_in": nrm(ks[8], (N_EVEN, D, IN_PROJ_DIM), f32) * D ** -0.5,
        "q_norm_g": 1.0 + 0.02 * nrm(ks[9], (N_EVEN, Q_LORA_RANK), f32),
        "kv_norm_g": 1.0 + 0.02 * nrm(ks[10], (N_EVEN, KV_LORA_RANK), f32),
        "w_uq": nrm(ks[11], (N_EVEN, Q_LORA_RANK, MLA_HEADS * QK_HEAD_DIM), f32) * Q_LORA_RANK ** -0.5,
        "w_ukv": nrm(ks[12], (N_EVEN, KV_LORA_RANK, MLA_HEADS * (QK_NOPE_DIM + V_HEAD_DIM)), f32) * KV_LORA_RANK ** -0.5,
        "q_gain": 1.0 + 0.02 * nrm(ks[13], (N_EVEN, QK_HEAD_DIM), f32),
        "k_gain": 1.0 + 0.02 * nrm(ks[14], (N_EVEN, QK_HEAD_DIM), f32),
        "conv_w": nrm(ks[15], (N_EVEN, CONV_WIDTH, CONV_DIM), f32) * CONV_WIDTH ** -0.5,
        "w_o": nrm(ks[16], (N_EVEN, MIX_OUT_DIM, D), f32) * MIX_OUT_DIM ** -0.5,
        "w_fourier": nrm(ks[17], (N_ODD, D, D), f32) * D ** -0.5,
        "ffn_w1": nrm(ks[18], (DEPTH, D, D_FF), f32) * D ** -0.5,
        "ffn_w3": nrm(ks[19], (DEPTH, D, D_FF), f32) * D ** -0.5,
        "ffn_w2": nrm(ks[20], (DEPTH, D_FF, D), f32) * D_FF ** -0.5,
    }

def first_block(x, c, ctx, c_ctx, ada_w, ada_b, norm1_g, norm2_g, w_in, q_norm_g, kv_norm_g, w_uq, w_ukv,
              q_gain, k_gain, conv_w, w_o, w_fourier, ffn_w1, ffn_w3, ffn_w2):
    for i in range(DEPTH):
        last = i == DEPTH - 1
        j = i // 2
        sh1, sc1, g1, sh2, sc2, g2 = [m[:, None, :] for m in ada(c, ada_w[i], ada_b[i])]
        csh1, csc1, cg1, csh2, csc2, cg2 = ada(c_ctx, ada_w[i], ada_b[i])
        h_l = rmsnorm(x, norm1_g[i]) * (1 + sc1) + sh1
        if i % 2 == 0:
            h_c = rmsnorm(ctx, norm1_g[i]) * (1 + csc1) + csh1
            out_l, out_c = even_mixer(h_l, h_c, w_in[j], q_norm_g[j], kv_norm_g[j], w_uq[j], w_ukv[j],
                                      q_gain[j], k_gain[j], conv_w[j], w_o[j], not last)
        else:
            out_l = fourier_mixer(h_l, w_fourier[j])
            out_c = None
            if not last:
                h_c = rmsnorm(ctx, norm1_g[i]) * (1 + csc1) + csh1
                out_c = fourier_mixer(h_c, w_fourier[j])
        x = x + g1 * out_l
        x = x + g2 * swiglu(rmsnorm(x, norm2_g[i]) * (1 + sc2) + sh2, ffn_w1[i], ffn_w3[i], ffn_w2[i])
        if not last:
            ctx = ctx + cg1 * out_c
            ctx = ctx + cg2 * swiglu(rmsnorm(ctx, norm2_g[i]) * (1 + csc2) + csh2, ffn_w1[i], ffn_w3[i], ffn_w2[i])
    return x


DEPTH_2 = 1

MIX_WIDTH = D_MODEL
HEAD_DIM = 64
ATTN_WIDTH = MIX_WIDTH // 2
N_Q_HEADS = ATTN_WIDTH // HEAD_DIM
N_KV_HEADS = 2
KV_GROUP = N_Q_HEADS // N_KV_HEADS
KV_WIDTH = N_KV_HEADS * HEAD_DIM
WINDOW = 128
ATTN_BLOCK = 128
LRU_WIDTH = MIX_WIDTH - ATTN_WIDTH
LRU_BLOCKS = 8
LRU_BLOCK_W = LRU_WIDTH // LRU_BLOCKS
CONV_WIDTH_2 = 4
LRU_C = 8.0
IN_SPLITS = [ATTN_WIDTH, ATTN_WIDTH + KV_WIDTH, ATTN_WIDTH + 2 * KV_WIDTH, ATTN_WIDTH + 2 * KV_WIDTH + LRU_WIDTH]
IN_COLS = ATTN_WIDTH + 2 * KV_WIDTH + 2 * LRU_WIDTH
N_EXPERTS = 32
TOP_K = 4
D_EXPERT = D_MODEL
SWIGLU_LIMIT = 7.0
SWIGLU_ALPHA = 1.702
MOE_BLOCK = 256


def rms_norm(x, g):
    xf = x.astype(jnp.float32)
    y = xf * lax.rsqrt(jnp.mean(xf * xf, axis=-1, keepdims=True) + EPS)
    return (y * g.astype(jnp.float32)).astype(x.dtype)

def causal_depthwise_conv(x, w, b):
    y = lax.conv_general_dilated(
        x, w[:, None, :].astype(x.dtype), window_strides=(1,),
        padding=[(CONV_WIDTH_2 - 1, 0)], dimension_numbers=("NWC", "WIO", "NWC"),
        feature_group_count=x.shape[-1])
    return y + b

def rg_lru(x, w_a, b_a, w_x, b_x, lam):
    B, S, C = x.shape
    xf = x.astype(jnp.float32)
    xh = xf.reshape(B, S, LRU_BLOCKS, LRU_BLOCK_W)
    r = jax.nn.sigmoid(jnp.einsum("bshi,hij->bshj", xh, w_a.astype(jnp.float32)) + b_a).reshape(B, S, C)
    i = jax.nn.sigmoid(jnp.einsum("bshi,hij->bshj", xh, w_x.astype(jnp.float32)) + b_x).reshape(B, S, C)
    log_a = LRU_C * r * jax.nn.log_sigmoid(lam.astype(jnp.float32))
    a = jnp.exp(log_a)
    mult = jnp.sqrt(jnp.maximum(-jnp.expm1(2.0 * log_a), 0.0))
    u = mult * (i * xf)

    def combine(left, right):
        a1, b1 = left
        a2, b2 = right
        return a1 * a2, a2 * b1 + b2

    _, h = lax.associative_scan(combine, (a, u), axis=1)
    return h.astype(x.dtype)

def sliding_window_sink_attention(q, k, v, sinks):
    B, S = q.shape[0], q.shape[1]
    nblk = S // ATTN_BLOCK
    qb = q.reshape(B, nblk, ATTN_BLOCK, N_KV_HEADS, KV_GROUP, HEAD_DIM)

    def band(t):
        tp = jnp.pad(t, ((0, 0), (ATTN_BLOCK, 0), (0, 0), (0, 0)))
        prev = tp[:, :S].reshape(B, nblk, ATTN_BLOCK, N_KV_HEADS, HEAD_DIM)
        cur = t.reshape(B, nblk, ATTN_BLOCK, N_KV_HEADS, HEAD_DIM)
        return jnp.concatenate([prev, cur], axis=2)

    kw, vw = band(k), band(v)
    scores = jnp.einsum("bnqkgd,bnskd->bnkgqs", qb, kw).astype(jnp.float32) * (HEAD_DIM ** -0.5)
    qi = jnp.arange(ATTN_BLOCK)[:, None]
    sj = jnp.arange(2 * ATTN_BLOCK)[None, :]
    rel = qi + ATTN_BLOCK - sj
    key_pos = jnp.arange(nblk)[:, None, None] * ATTN_BLOCK - ATTN_BLOCK + sj[None]
    mask = ((rel >= 0) & (rel < WINDOW))[None] & (key_pos >= 0)
    scores = jnp.where(mask[None, :, None, None], scores, jnp.finfo(jnp.float32).min)
    sink = jnp.broadcast_to(sinks.astype(jnp.float32).reshape(1, 1, N_KV_HEADS, KV_GROUP, 1, 1),
                            scores.shape[:-1] + (1,))
    probs = jax.nn.softmax(jnp.concatenate([scores, sink], axis=-1), axis=-1)[..., :-1]
    out = jnp.einsum("bnkgqs,bnskd->bnqkgd", probs.astype(v.dtype), vw)
    return out.reshape(B, S, N_Q_HEADS * HEAD_DIM)

def parallel_mixer(h, w_in, conv_w, conv_b, w_rg_a, b_rg_a, w_rg_x, b_rg_x, lru_lambda,
                   sinks, g_attn_out, g_lru_out, w_out):
    B, S, _ = h.shape
    p = h @ w_in
    q, k, v, xr, xg = jnp.split(p, IN_SPLITS, axis=-1)
    attn = sliding_window_sink_attention(
        q.reshape(B, S, N_Q_HEADS, HEAD_DIM), k.reshape(B, S, N_KV_HEADS, HEAD_DIM),
        v.reshape(B, S, N_KV_HEADS, HEAD_DIM), sinks)
    xc = causal_depthwise_conv(xr, conv_w, conv_b)
    lru = rg_lru(xc, w_rg_a, b_rg_a, w_rg_x, b_rg_x, lru_lambda) * jax.nn.gelu(xg)
    merged = jnp.concatenate([rms_norm(attn, g_attn_out), rms_norm(lru, g_lru_out)], axis=-1)
    return merged @ w_out

def moe_ffn(h, w_router, b_router, w_gu, b_gu, w_down, b_down):
    B, S, D = h.shape
    T = B * S
    A = T * TOP_K
    R = ((A + N_EXPERTS * (MOE_BLOCK - 1) + MOE_BLOCK - 1) // MOE_BLOCK) * MOE_BLOCK
    nb = R // MOE_BLOCK
    hf = h.reshape(T, D)
    logits = (hf @ w_router + b_router).astype(jnp.float32)
    top_vals, top_idx = lax.top_k(logits, TOP_K)
    gates = jax.nn.softmax(top_vals, axis=-1)
    flat_e = top_idx.reshape(A).astype(jnp.int32)
    flat_tok = jnp.repeat(jnp.arange(T, dtype=jnp.int32), TOP_K)
    flat_w = gates.reshape(A)
    order = jnp.argsort(flat_e)
    se = flat_e[order]
    sizes = jnp.bincount(flat_e, length=N_EXPERTS)
    padded = ((sizes + MOE_BLOCK - 1) // MOE_BLOCK) * MOE_BLOCK
    pad_end = jnp.cumsum(padded)
    pad_start = pad_end - padded
    start = jnp.cumsum(sizes) - sizes
    dest = pad_start[se] + (jnp.arange(A, dtype=jnp.int32) - start[se])
    row_tok = jnp.zeros((R,), jnp.int32).at[dest].set(flat_tok[order])
    row_w = jnp.zeros((R,), jnp.float32).at[dest].set(flat_w[order])
    blk_e = jnp.minimum(jnp.searchsorted(pad_end, jnp.arange(nb) * MOE_BLOCK, side="right"),
                        N_EXPERTS - 1).astype(jnp.int32)
    xs = hf[row_tok].reshape(nb, MOE_BLOCK, D)

    def expert_block(args):
        xb, e = args
        gu = xb @ w_gu[e] + b_gu[e]
        gate = jnp.minimum(gu[:, :D_EXPERT], SWIGLU_LIMIT)
        up = jnp.clip(gu[:, D_EXPERT:], -SWIGLU_LIMIT, SWIGLU_LIMIT)
        glu = gate * jax.nn.sigmoid(SWIGLU_ALPHA * gate)
        return ((up + 1.0) * glu) @ w_down[e] + b_down[e]

    ys = lax.map(expert_block, (xs, blk_e)).reshape(R, D)
    ys = ys.astype(jnp.float32) * row_w[:, None]
    out = jax.ops.segment_sum(ys, row_tok, num_segments=T)
    return out.reshape(B, S, D).astype(h.dtype)

def second_inputs(seed: int = 0) -> dict:
    key = jax.random.key(seed)
    ks = jax.random.split(key, 26)
    L, D, E, F = DEPTH_2, D_MODEL, N_EXPERTS, D_EXPERT
    nrm = lambda k, shape, s: jax.random.normal(k, shape, jnp.float32) * s
    a0 = jax.random.uniform(ks[13], (L, LRU_WIDTH), jnp.float32, minval=0.9, maxval=0.999)
    root = a0 ** (1.0 / LRU_C)
    return {
        "x": nrm(ks[0], (BATCH, SEQ, D), 1.0),
        "c": nrm(ks[1], (BATCH, D), 1.0),
        "w_ada": nrm(ks[2], (L, D, 6 * D), 0.5 * D ** -0.5),
        "b_ada": nrm(ks[3], (L, 6 * D), 0.02),
        "g_mix": 1.0 + nrm(ks[4], (L, D), 0.05),
        "w_in": nrm(ks[5], (L, D, IN_COLS), D ** -0.5),
        "conv_w": nrm(ks[6], (L, CONV_WIDTH_2, LRU_WIDTH), CONV_WIDTH_2 ** -0.5),
        "conv_b": nrm(ks[7], (L, LRU_WIDTH), 0.02),
        "w_rg_a": nrm(ks[8], (L, LRU_BLOCKS, LRU_BLOCK_W, LRU_BLOCK_W), LRU_BLOCK_W ** -0.5),
        "b_rg_a": nrm(ks[9], (L, LRU_BLOCKS, LRU_BLOCK_W), 0.02),
        "w_rg_x": nrm(ks[10], (L, LRU_BLOCKS, LRU_BLOCK_W, LRU_BLOCK_W), LRU_BLOCK_W ** -0.5),
        "b_rg_x": nrm(ks[11], (L, LRU_BLOCKS, LRU_BLOCK_W), 0.02),
        "lru_lambda": jnp.log(root) - jnp.log1p(-root),
        "sinks": nrm(ks[12], (L, N_Q_HEADS), 0.5),
        "g_attn_out": 1.0 + nrm(ks[14], (L, ATTN_WIDTH), 0.05),
        "g_lru_out": 1.0 + nrm(ks[15], (L, LRU_WIDTH), 0.05),
        "w_out": nrm(ks[16], (L, MIX_WIDTH, D), MIX_WIDTH ** -0.5),
        "g_ffn": 1.0 + nrm(ks[17], (L, D), 0.05),
        "w_router": nrm(ks[18], (L, D, E), D ** -0.5),
        "b_router": nrm(ks[19], (L, E), 0.01),
        "w_gu": nrm(ks[20], (L, E, D, 2 * F), D ** -0.5),
        "b_gu": nrm(ks[21], (L, E, 2 * F), 0.02),
        "w_down": nrm(ks[22], (L, E, F, D), F ** -0.5),
        "b_down": nrm(ks[23], (L, E, D), 0.02),
        "g_final": 1.0 + nrm(ks[24], (D,), 0.05),
    }

def second_block(x, c, w_ada, b_ada, g_mix, w_in, conv_w, conv_b, w_rg_a, b_rg_a, w_rg_x, b_rg_x,
              lru_lambda, sinks, g_attn_out, g_lru_out, w_out, g_ffn, w_router, b_router,
              w_gu, b_gu, w_down, b_down, g_final):
    for l in range(DEPTH_2):
        mod = (c @ w_ada[l] + b_ada[l])[:, None, :]
        sh1, sc1, gt1, sh2, sc2, gt2 = jnp.split(mod, 6, axis=-1)
        h = rms_norm(x, g_mix[l]) * (1.0 + sc1) + sh1
        x = x + gt1 * parallel_mixer(h, w_in[l], conv_w[l], conv_b[l], w_rg_a[l], b_rg_a[l],
                                     w_rg_x[l], b_rg_x[l], lru_lambda[l], sinks[l],
                                     g_attn_out[l], g_lru_out[l], w_out[l])
        h = rms_norm(x, g_ffn[l]) * (1.0 + sc2) + sh2
        x = x + gt2 * moe_ffn(h, w_router[l], b_router[l], w_gu[l], b_gu[l], w_down[l], b_down[l])
    return rms_norm(x, g_final)


def setup_inputs(seed=0):
    out = dict(first_inputs(seed))
    for name, value in second_inputs(seed + 1).items():
        if name != "x":
            out[name + "_2"] = value
    return out


def reference(
    x, c, ctx, c_ctx, ada_w, ada_b, norm1_g, norm2_g, w_in, q_norm_g, kv_norm_g, w_uq, w_ukv,
    q_gain, k_gain, conv_w, w_o, w_fourier, ffn_w1, ffn_w3, ffn_w2, c_2, w_ada_2, b_ada_2,
    g_mix_2, w_in_2, conv_w_2, conv_b_2, w_rg_a_2, b_rg_a_2, w_rg_x_2, b_rg_x_2, lru_lambda_2,
    sinks_2, g_attn_out_2, g_lru_out_2, w_out_2, g_ffn_2, w_router_2, b_router_2, w_gu_2,
    b_gu_2, w_down_2, b_down_2, g_final_2,
):
    x = first_block(
        x, c, ctx, c_ctx, ada_w, ada_b, norm1_g, norm2_g, w_in, q_norm_g, kv_norm_g, w_uq,
        w_ukv, q_gain, k_gain, conv_w, w_o, w_fourier, ffn_w1, ffn_w3, ffn_w2,
    )
    return second_block(
        x, c_2, w_ada_2, b_ada_2, g_mix_2, w_in_2, conv_w_2, conv_b_2, w_rg_a_2, b_rg_a_2,
        w_rg_x_2, b_rg_x_2, lru_lambda_2, sinks_2, g_attn_out_2, g_lru_out_2, w_out_2, g_ffn_2,
        w_router_2, b_router_2, w_gu_2, b_gu_2, w_down_2, b_down_2, g_final_2,
    )


_drawn_inputs = setup_inputs


def setup_inputs(seed=0):
    import zlib

    import numpy as np

    out = dict(_drawn_inputs(seed))
    spreads = {}
    factors = {'ctx': 2.976,
     'norm2_g': 2.867,
     'q_norm_g': 8.0,
     'kv_norm_g': 8.0,
     'q_gain': 8.0,
     'k_gain': 8.0,
     'g_mix_2': 3.084,
     'conv_b_2': 16.395,
     'b_rg_a_2': 64.0,
     'b_rg_x_2': 63.091,
     'sinks_2': 64.0,
     'g_attn_out_2': 25.178,
     'g_lru_out_2': 26.847,
     'b_router_2': 44.168,
     'b_gu_2': 60.262,
     'b_down_2': 64.0,
     'b_ada_2': 2.77,
     'g_ffn_2': 8.0}
    for name, (base, spread) in spreads.items():
        noise = np.random.default_rng([zlib.crc32(name.encode()), seed]).standard_normal(out[name].shape)
        drawn = base * np.exp(spread * noise) if base else spread * noise
        out[name] = __import__('jax').numpy.asarray(drawn.astype(out[name].dtype))
    for name, factor in factors.items():
        out[name] = (out[name] * factor).astype(out[name].dtype)
    return out
```

```python
import numpy as np
import concourse.bass as bass
from concourse import mybir
from concourse.alu_op_type import AluOpType as ALU
from contextlib import ExitStack

P = 128
D = 1024
DJ = D // P
T = 256
TT = T // P
TC = 256
EPS = 1e-6
QR, KVR, ROPE, NOPE, VD, HEADS = 384, 256, 32, 64, 64, 8
QD = NOPE + ROPE
QK_SCALE = QD ** -0.5
CONV = 512
CJ = CONV // P
FF = 2816
NF = FF // P
FA = 2 * D
HD = 64
Q_SCALE2 = HD ** -0.5
NEXP, TOPK = 32, 4
CAP = 128
PASSES = T // CAP
LIMIT, ALPHA = 7.0, 1.702
NEG = -3.0e38
B_Q, B_KV, B_KPE, B_CB, B_CC, B_CU = 0, 3, 5, 6, 10, 14
B_O, B_F = 18, 26
B_Q2, B_K2, B_XR, B_XG, B_V2 = 34, 38, 39, 43, 47
B_OUT2 = 48
NB = 56
NRAW, NSPLIT = 3, 6
AG = 1024
NGRP = 18
GU_CH, DN_CH = D // P, D // (2 * P)
CH = GU_CH + DN_CH
MRAW = 4
POOL_LO = (1, 4, 7, 10)

_V = {}
_n = 0
for _name, _m in [("c", 8), ("cx", 8), ("c2", 8), ("ada_b", 18 * 8), ("n1", 16), ("n2", 16), ("gmix", 8), ("gffn", 8),
                  ("gfin", 8), ("qg", 3), ("kvg", 2), ("qgain", 1), ("kgain", 1), ("conv", 12), ("conv2", 16),
                  ("conv2b", 4), ("ba", 4), ("bx", 4), ("lam", 4), ("gattn", 4), ("glru", 4), ("sink", 8),
                  ("eps", 1), ("brout", 32)]:
    _V[_name] = _n
    _n += _m
NV = _n
_C = {}
_n = 0
for _name, _m in [("ident", 128), ("ones", 128), ("triu", 128), ("iota", 128), ("iota32", 32), ("head8", 64),
                  ("bcast8", 8 * QD), ("cos", T), ("sin", T), ("rot", ROPE), ("mask", 2 * P), ("eye64", NEXP + 1)]:
    _C[_name] = _n
    _n += _m
NC_ = _n


def build(nc, xT_d, xc_d, vec_d, con_d, tab_d, ada_d, blk_d, uq_d, uk_d, ffna_d, ffnb_d, rga_d, rgx_d, rout_d,
          gu_d, bgu_d, dn_d, bdn_d, out_d):
    F32, F32R, I32 = mybir.dt.float32, mybir.dt.float32r, mybir.dt.int32
    ACT = mybir.ActivationFunctionType
    AX = mybir.AxisListType.X
    ctx = ExitStack()
    with ctx:
        def sb(name, shape, dt=F32, stack=ctx):
            return stack.enter_context(nc.sbuf_tensor(name, shape, dt))

        def sem(name):
            return ctx.enter_context(nc.semaphore(name))

        x = sb("x", [P, DJ, T])
        work = sb("work", [P, DJ, 2 * T])
        ah = sb("ah", [P, DJ * 2 * T], F32R)
        al = sb("al", [P, DJ * 2 * T], F32R)
        ah3 = ah[:, :].rearrange("p (j t) -> p j t", j=DJ)
        al3 = al[:, :].rearrange("p (j t) -> p j t", j=DJ)
        raw = sb("raw", [P, 8192])
        wh = sb("wh", [P, 6144], F32R)
        wl = sb("wl", [P, 6144], F32R)
        mh = sb("mh", [P, 1024], F32R)
        ml = sb("ml", [P, 1024], F32R)
        con = sb("con", [P, NC_])
        vec = sb("vec", [P, NV])
        mod = sb("mod", [P, NGRP * 8])
        gs = sb("gs", [P, 8])
        gsx = sb("gsx", [P, 8])
        rt = sb("rt", [P, 2 * T])
        rstd = sb("rstd", [P, 2 * T])
        csil = sb("csil", [P, 16])
        modx = sb("modx", [P, 16])
        srow = sb("srow", [P, 2, 8])
        flag = sb("flag", [1, 1], I32)

        def C(name, w, rows=P):
            return con[0:rows, _C[name]:_C[name] + w]

        def V(name, i=0, rows=P):
            return vec[0:rows, _V[name] + i:_V[name] + i + 1]

        ident, ones = C("ident", P), C("ones", P)

        ph = ExitStack()
        acc = sb("acc", [P, AG], F32, ph)
        araw = sb("araw", [P, 2, AG], F32, ph)
        base = ExitStack()
        xc = sb("xc", [P, DJ * TC], F32, base)
        kbuf = sb("kbuf", [P, HEADS * 2 * T], F32, base)
        pbuf = sb("pbuf", [P, 2, 2 * T], F32, base)
        sqb = sb("sqb", [P, 2, 2 * T], F32, base)
        kpe = sb("kpe", [P, 2 * T], F32, base)
        diag = sb("diag", [P, 2, P], F32, base)
        base.close()
        base = ExitStack()
        sg = sb("sg", [P, 2, T], F32, base)
        mm_ = sb("mm_", [P, 2, T], F32, base)
        tabs = sb("tabs", [P, 2, 3, T], F32, base)
        vdft = sb("vdft", [P, TT, 4, 2 * T], F32, base)
        base.close()
        base = ExitStack()
        q2 = sb("q2", [P, 4, T], F32, base)
        k2 = sb("k2", [P, T], F32, base)
        v2 = sb("v2", [P, TT, P], F32, base)
        xr = sb("xr", [P, 4, T + 3], F32, base)
        xg = sb("xg", [P, 4, T], F32, base)
        xcv = sb("xcv", [P, 4, T], F32, base)
        rga = sb("rga", [P, 4, P], F32, base)
        rgx = sb("rgx", [P, 4, P], F32, base)
        atn = sb("atn", [P, 4, T], F32, base)
        p2 = sb("p2", [P, 2, T], F32, base)
        e2 = sb("e2", [P, 2, T], F32, base)
        pt2 = sb("pt2", [P, 2, T], F32, base)
        dg2 = sb("dg2", [P, 2, P], F32, base)
        lam = sb("lam", [P, 8, 4], F32, base)
        base.close()
        ph.close()
        mo = ExitStack()
        oacc = sb("oacc", [P, TT, D], F32, mo)
        wh4 = sb("wh4", [P, 2048], F32R, mo)
        wl4 = sb("wl4", [P, 2048], F32R, mo)
        sone = sb("sone", [P, TT, CAP], F32R, mo)
        stwo = sb("stwo", [P, TT, CAP], F32, mo)
        stt = sb("stt", [P, T], F32R, mo)
        sel = sb("sel", [64, P], F32R, mo)
        bgu = sb("bgu", [64, 2 * D], F32R, mo)
        gcol = sb("gcol", [P, 1], F32, mo)
        rout = sb("rout", [P, DJ, NEXP], F32, mo)
        logit = sb("logit", [P, TT, NEXP], F32, mo)
        gatew = sb("gatew", [P, TT, NEXP], F32, mo)
        pos = sb("pos", [P, TT, NEXP + 1], F32, mo)
        mask_ = sb("mask_", [P, TT, NEXP], F32, mo)
        rsc = sb("rsc", [P, 64], F32, mo)
        ridx = sb("ridx", [P, TT, 8], mybir.dt.uint32, mo)
        gT = sb("gT", [NEXP, T], F32, mo)
        bdn = sb("bdn", [NEXP, D], F32, mo)
        mo.close()

        psum = ctx.enter_context(nc.psum_tensor("psum", [P, 8, 512], F32))
        ps = [psum[:, i, :] for i in range(8)]
        ps45, ps67 = [psum[:, i:i + 2, :].rearrange("p a n -> p (a n)") for i in (4, 6)]

        uq = raw[:, 3072:3072 + 3 * HEADS * QD].rearrange("p (k n) -> p k n", k=3)
        uk = raw[:, 5376:5376 + 2 * D].rearrange("p (k n) -> p k n", k=2)
        ukn = uk.rearrange("p k (a h d) -> p k a h d", a=2, h=HEADS)
        qb = work[:, 0:4, :].rearrange("p a (b t) -> p (a b) t", b=2)
        vb = work[:, 4:8, :]
        cq = xc[:, 0:768].rearrange("p (j t) -> p j t", j=3)
        ckv = xc[:, 768:1792].rearrange("p (j t) -> p j t", j=2)
        pt = xc[:, :].rearrange("p (s k t) -> p s k t", s=2, k=4)
        kb = kbuf[:, :].rearrange("p (h t) -> p h t", h=HEADS)
        cbg = kbuf[:, 0:1024].rearrange("p (j t) -> p j t", j=4)
        ccg = kbuf[:, 1024:2048].rearrange("p (j t) -> p j t", j=4)
        czp = kbuf[:, 2048:2048 + 4 * (T + 2)].rearrange("p (j t) -> p j t", j=4)
        sqf = sqb[:, :, :].rearrange("p a t -> p (a t)")
        hth = ah[:, 0:2048].rearrange("p (a n) -> p a n", a=TT)
        htl = al[:, 0:2048].rearrange("p (a n) -> p a n", a=TT)
        xsh, xsl = ah[:, 2048:3072], al[:, 2048:3072]
        ath, atl = ah[:, 3072:4096], al[:, 3072:4096]
        wflat = work[:, :, :].rearrange("p j t -> p (j t)")
        gate_c, up_c, sig_c, act_c = [wflat[:, i * D:(i + 1) * D] for i in range(4)]
        mwh = [wh[:, i * 2048:(i + 1) * 2048] for i in range(3)] + [wh4[:, :]]
        mwl = [wl[:, i * 2048:(i + 1) * 2048] for i in range(3)] + [wl4[:, :]]
        accx = kbuf[:, 0:AG]
        bgr = oacc[0:64, :, :].rearrange("p a n -> p (a n)")
        gl = acc[:, :].rearrange("p (j t) -> p j t", j=4)

        s_con, s_xin, s_xcin, s_out = [sem(n) for n in ("consts_loaded", "x_loaded", "ctx_loaded", "out_stored")]
        s_par = sem("parameters_loaded")
        MLA_IN, DFT_IN, LRU_IN, EXP_IN = 32, 48, 48 + 256, 48 + 256 + 64
        s_raw = [sem(f"block_loaded{i}") for i in range(NRAW)]
        s_hi, s_lo, s_blk, s_ev = [sem(n) for n in ("block_hi", "block_lo", "block_product", "block_evacuated")]
        s_araw = [sem(f"ada_loaded{i}") for i in range(2)]
        s_ada, s_adx, s_acol, s_mod = [sem(n) for n in ("ada_acc", "ada_ctx_acc", "ada_columns", "mod_ready")]
        s_sil = sem("c_sigmoid")
        s_x = sem("x_chunk")
        s_nt, s_zp, s_pos = sem("norm_scaled"), sem("conv_pads"), sem("places_cleared")
        s_sq, s_sum, s_rt, s_h, s_hh, s_hl = [sem(n) for n in (
            "norm_squares", "norm_sums", "norm_root", "h_chunk", "h_hi", "h_lo")]
        s_dve, s_act = sem("dve_chain"), sem("act_chain")
        s_cqs, s_cqsum, s_cqrt, s_cqn = [sem(n) for n in ("lora_squares", "lora_sums", "lora_root", "lora_normed")]
        s_qk, s_qkc, s_qksq, s_qks8, s_qk8r, s_qkr8, s_qkbc, s_qkn, s_rot, s_qrope = [sem(n) for n in (
            "qk_product", "qk_copied", "qk_squares", "qk_sums", "qk_root", "qk_rstd", "qk_rstd_spread", "qk_normed",
            "rope_turned", "rope_done")]
        s_v, s_vc = sem("v_product"), sem("v_copied")
        s_sc, s_nm, s_pe_, s_dg, s_pt, s_ptc, s_pv, s_ao = [sem(n) for n in (
            "scores", "row_max", "probs", "diag_ready", "probs_turned", "probs_copied", "pv_product", "attn_hi")]
        s_aol, s_cs, s_csh, s_csl = [sem(n) for n in ("attn_lo", "conv_out", "conv_hi", "conv_lo")]
        s_fraw = [sem(f"ffn_loaded{i}") for i in range(2)]
        s_fbraw = [sem(f"ffn_down_loaded{i}") for i in range(2)]
        s_fbhi, s_fblo, s_fhi, s_flo, s_fgu, s_fsig, s_ft, s_fm, s_fmh, s_fml, s_fdn = [sem(f"ffn_{n}") for n in (
            "down_hi", "down_lo", "hi", "lo", "gate_up", "sigmoid", "gate", "mul", "mul_hi", "mul_lo", "down")]
        s_v1, s_v1c, s_f2, s_f2h, s_f2l = [sem(n) for n in (
            "dft_features", "dft_features_copied", "dft_tokens", "dft_hi", "dft_lo")]
        s_th, s_lruo = sem("lru_tanh"), sem("lru_out")
        s_zero = sem("pads_cleared")
        s_xcv, s_rg1, s_sgm, s_lru, s_ex, s_mul2, s_sq2, s_gel, s_gelt = [sem(n) for n in (
            "lru_conv", "lru_gates", "lru_sigmoids", "lru_log", "lru_exp", "lru_mult", "lru_root", "gelu_arg", "gelu_tanh")]
        s_ms2, s_ex2, s_at2 = [sem(n) for n in ("win_masked", "win_probs", "win_out")]
        s_msq, s_msum, s_mrt, s_mn, s_mnh, s_mnl = [sem(n) for n in (
            "merge_squares", "merge_sums", "merge_root", "merged", "merged_hi", "merged_lo")]
        s_lg, s_tk, s_tke, s_mask, s_cum, s_route, s_ht, s_hth, s_htl, s_flag = [sem(n) for n in (
            "logits", "top_values", "top_exp", "chosen", "slot_counts", "routed", "h_turned", "h_tok_hi", "h_tok_lo",
            "overflow_known")]
        s_cumr = sem("slot_counts_read")
        s_gtt, s_gtc, s_bd, s_oi, s_bgh, s_bgl = [sem(n) for n in (
            "gates_turned", "gates_copied", "down_bias_sum", "out_started", "gu_bias_hi", "gu_bias_lo")]
        MOE = {"hi": 12 * NEXP, "lo_dve": 8 * NEXP, "lo_pool": 4 * NEXP, "chunk": 12 * NEXP, "onehot": NEXP + 1,
               "onehot2": NEXP, "select": NEXP + 1, "gathered": 2 * NEXP + 2, "xs_hi": 2 * NEXP + 2, "xs_lo": 2 * NEXP + 2,
               "gu": NEXP, "gate": NEXP, "sig": NEXP, "glu": NEXP, "act": NEXP, "turned": 2 * NEXP, "at_hi": 2 * NEXP,
               "at_lo": 2 * NEXP, "slots": NEXP, "stt": NEXP, "gcol": NEXP, "y_hi": 2 * NEXP, "y_lo": 2 * NEXP,
               "combined": 2 * NEXP, "added": 4 * NEXP}
        m = {n: sem("moe_" + n) for n in MOE}
        s_mraw = [sem(f"moe_loaded{i}") for i in range(MRAW)]
        MOE_RAW = 16 * CH * NEXP // MRAW
        s_ot, s_fy = sem("out_turned"), sem("final_chunk")

        block = ctx.enter_context(nc.Block())

        def lo_before(q):
            n = q + 24
            pool = sum(1 for k in range(4, n) if k % CH in POOL_LO)
            return (n - 4 - pool) - 16, pool - 8

        def wait(eng, s, value):
            if not isinstance(value, int) or value > 0:
                eng.wait_ge(s, value)

        def moe_wait(eng, p_, name, value):
            if p_ or not isinstance(value, int) or value > 0:
                eng.wait_ge(m[name], value + p_ * MOE[name])

        def ada_chunk_ap(g, j):
            return ada_d[g // 6, j * P:(j + 1) * P, (g % 6) * AG:(g % 6 + 1) * AG]

        ADA_FIRST = 2 * 8

        @block.sync
        def _(sp):
            sp.dma_start(con[:, :], con_d).then_inc(s_con, 16)
            sp.dma_start(vec[:, :], vec_d).then_inc(s_con, 16)
            sp.dma_start(x[:, :, :], xT_d).then_inc(s_xin, 16)
            sp.dma_start(xc[:, :], xc_d).then_inc(s_xcin, 16)

            def ada(n):
                if n >= 2:
                    sp.wait_ge(s_ada, n - 1)
                    if n - 2 < ADA_FIRST:
                        sp.wait_ge(s_adx, n - 1)
                sp.dma_start(araw[:, n % 2, :], ada_chunk_ap(n // 8, n % 8)).then_inc(s_araw[n % 2], 16)

            def blk(b):
                if b >= NRAW:
                    sp.wait_ge(s_hi, b - NRAW + 1)
                    sp.wait_ge(s_lo, b - NRAW + 1)
                sp.dma_start(raw[:, (b % NRAW) * D:(b % NRAW + 1) * D], blk_d[b]).then_inc(s_raw[b % NRAW], 16)

            for n in range(ADA_FIRST):
                ada(n)
                if n >= 10 and n % 2 == 0:
                    blk((n - 10) // 2)
            for n in range(8):
                ada(ADA_FIRST + n)
                blk(3 + n)
            sp.dma_start(uq, uq_d).then_inc(s_par, 16)
            sp.dma_start(uk, uk_d).then_inc(s_par, 16)
            for b in range(11, B_O + 3):
                blk(b)
            for n in range(24, 48):
                ada(n)
            for b in range(B_O + 3, B_F):
                blk(b)

            def ffn_a(l, slot, src):
                sp.dma_start(raw[:, slot * FA:(slot + 1) * FA], src).then_inc(s_fraw[slot], 16)

            def ffn_b(l, slot, src):
                sp.dma_start(raw[:, 2 * FA + slot * D:2 * FA + (slot + 1) * D], src).then_inc(s_fbraw[slot], 16)

            def ffn(l):
                sp.wait_ge(s_lo, B_F if l == 0 else B_Q2)
                if l == 0:
                    sp.wait_ge(s_v, 4)
                for f in range(2):
                    ffn_a(l, f, ffna_d[l, f])
                    ffn_b(l, f, ffnb_d[l, f])
                base_n = 48 + 48 * l
                for j in range(8):
                    ada(base_n + j)
                with sp.Fori(0, (NF - 2) // 4) as i:
                    f0 = sp.snap(i * 4)
                    g0 = sp.snap(i * AG + AG)
                    ada_done = sp.snap(i * 8 + (base_n + 7))
                    for u in range(4):
                        f, split = sp.snap(f0 + (2 + u)), sp.snap(f0 + (l * NF + 1 + u))
                        sp.wait_ge(s_flo, split)
                        ffn_a(l, u % 2, ffna_d[l, bass.ds(f, 1), :, :].rearrange("a p n -> p (a n)"))
                        sp.wait_ge(s_fblo, split)
                        ffn_b(l, u % 2, ffnb_d[l, bass.ds(f, 1), :, :].rearrange("a p n -> p (a n)"))
                        for j in (2 * u, 2 * u + 1):
                            summed = sp.snap(ada_done + j)
                            sp.wait_ge(s_ada, summed)
                            sp.dma_start(araw[:, j % 2, :], ada_d[l + 1, j * P:(j + 1) * P, bass.ds(g0, AG)]
                                         ).then_inc(s_araw[j % 2], 16)

            ffn(0)
            sp.wait_ge(s_flo, NF)
            sp.wait_ge(s_pv, HEADS)
            sp.dma_start(tabs[:, :, :, :], tab_d).then_inc(s_par, 16)
            for b in range(B_F, B_Q2):
                blk(b)
            ffn(1)
            sp.wait_ge(s_flo, 2 * NF)
            sp.wait_ge(s_f2, 8)
            sp.wait_ge(s_fml, 2 * NF)
            sp.wait_ge(s_zero, 3)
            for c_ in range(4):
                for hb in range(2):
                    sl = slice(64 * hb, 64 * hb + 64)
                    sp.dma_start(rga[sl, c_, 64 * hb:64 * hb + 64], rga_d[2 * c_ + hb]).then_inc(s_par, 16)
                    sp.dma_start(rgx[sl, c_, 64 * hb:64 * hb + 64], rgx_d[2 * c_ + hb]).then_inc(s_par, 16)
            for b in range(B_Q2, NB):
                blk(b)
            sp.wait_ge(s_mnl, 8)
            sp.dma_start(rout[:, :, :], rout_d).then_inc(s_par, 16)
            sp.dma_start(bgr[0:NEXP, :], bgu_d).then_inc(s_par, 16)
            sp.dma_start(bgr[NEXP:2 * NEXP, :], bgu_d).then_inc(s_par, 16)
            sp.dma_start(bdn[:, :], bdn_d).then_inc(s_par, 16)
            sp.wait_ge(s_lo, NB)

            def experts(p_):

                def load(q, e, static):
                    slot = raw[:, (q % MRAW) * 2048:(q % MRAW + 1) * 2048]
                    if q < GU_CH:
                        src = gu_d[e, q * P:(q + 1) * P, :] if static else \
                            gu_d[bass.ds(e, 1), q * P:(q + 1) * P, :].rearrange("a p n -> p (a n)")
                    else:
                        c_ = q - GU_CH
                        src = dn_d[e - 1] if static else dn_d[bass.ds(e - 1, 1), :, :].rearrange("a k n -> (a k) n")
                        src = src[c_ * 256:(c_ + 1) * 256, :].rearrange("(i p) n -> p i n", p=P)
                        slot = slot.rearrange("p (i n) -> p i n", i=2)
                    sp.dma_start(slot, src).then_inc(s_mraw[q % MRAW], 16)

                def chunk(e, q, e8, e4, static, kind=None):
                    d_, l_ = lo_before(q - MRAW + 1)
                    name, value = ("lo_pool", e4 + l_) if (q - MRAW) % CH in POOL_LO else ("lo_dve", e8 + d_)
                    if not static or 12 * e - 4 + q >= MRAW:
                        if not static:
                            value = sp.snap(value + p_ * MOE[name])
                            sp.wait_ge(m[name], value)
                        else:
                            moe_wait(sp, p_, name, value)
                    load(q if kind is None else kind, e, static)

                for q in range(4, 12):
                    chunk(0, q, 0, 0, True, q - 4)
                with sp.Fori(1, NEXP) as e:
                    e8, e4, ev = sp.snap(e * 8), sp.snap(e * 4), sp.snap(e + 0)
                    for q in range(CH):
                        chunk(ev, q, e8, e4, False)
                for q in range(DN_CH):
                    chunk(NEXP, q, 8 * NEXP, 4 * NEXP, True, GU_CH + q)

            experts(0)
            sp.wait_ge(s_flag, 1)
            over = sp.value_load(flag[0:1, 0:1], min_val=0, max_val=1)
            with sp.If(over > 0):
                sp.wait_ge(m["added"], MOE["added"])
                experts(1)
            sp.end_ifs()
            for j in range(DJ):
                sp.wait_ge(s_fy, j + 1)
                sp.dma_start(out_d[:, j, :], work[:, j, 0:T]).then_inc(s_out, 16)
            sp.wait_ge(s_out, 16 * DJ)

        @block.tensor
        def _(pe):
            mm = nc.tensor.matmul

            def ada_columns(g):
                pe.wait_ge(s_ada, 8 * (g + 1))
                wait(pe, s_mod, g)
                if g < 2:
                    pe.wait_ge(s_adx, 8 * (g + 1))
                    for i in range(8):
                        mm(ps[2][:, 8 + i:9 + i], accx[:, i * P:(i + 1) * P], ones[:, 0:1], start=True, stop=True)
                for i in range(8):
                    last = mm(ps[2][:, i:i + 1], acc[:, i * P:(i + 1) * P], ones[:, 0:1], start=True, stop=True)
                last.then_inc(s_acol, 1)

            def norm_sums(n, width=T):
                for j in range(DJ):
                    pe.wait_ge(s_sq, DJ * n + j + 1)
                    last = mm(ps[3][:, 0:width], ones, work[:, j, 0:width], start=(j == 0), stop=(j == DJ - 1))
                last.then_inc(s_sum, 1)

            def block_product(b, width=T):
                pe.wait_ge(s_lo, b + 1)
                wait(pe, s_ev, b - 1)
                w0 = (b % NSPLIT) * D
                for j in range(DJ):
                    w = slice(w0 + j * P, w0 + (j + 1) * P)
                    o = ps[b % 2][:, 0:width]
                    mm(o, wh[:, w], ah3[:, j, 0:width], start=(j == 0), stop=False)
                    mm(o, wh[:, w], al3[:, j, 0:width], start=False, stop=False)
                    last = mm(o, wl[:, w], ah3[:, j, 0:width], start=False, stop=(j == DJ - 1))
                last.then_inc(s_blk, 1)

            def h_ready(n):
                pe.wait_ge(s_hl, DJ * (n + 1))

            pe.wait_ge(s_con, 32)
            ada_columns(0)
            ada_columns(1)
            norm_sums(0, 2 * T)
            h_ready(0)
            for b in range(B_CB):
                block_product(b, T if b < B_KV else 2 * T)
            for b in range(B_CB, B_CC):
                block_product(b)
            for j in range(3):
                pe.wait_ge(s_cqs, j + 1)
                last = mm(ps[3][:, 0:T], ones, sqf[:, j * T:(j + 1) * T], start=(j == 0), stop=(j == 2))
            last.then_inc(s_cqsum, 1)
            for j in range(2):
                pe.wait_ge(s_cqs, 4 + j)
                last = mm(ps[4][:, :], ones, pbuf[:, j, :], start=(j == 0), stop=(j == 1))
            last.then_inc(s_cqsum, 1)
            for b in range(B_CC, B_O):
                block_product(b)
            ada_columns(2)

            pe.wait_ge(s_par, MLA_IN)
            pe.wait_ge(s_cqn, 5)

            def qk_product(u):
                wait(pe, s_qkc, u - 3)
                if u < 4:
                    for h in (2 * u, 2 * u + 1):
                        for k in range(3):
                            last = mm(ps[4 + u % 4][0:QD, (h % 2) * T:(h % 2 + 1) * T], uq[:, k, h * QD:(h + 1) * QD],
                                      cq[:, k, :], start=(k == 0), stop=(k == 2))
                else:
                    for k in range(2):
                        last = mm(ps[4 + u % 4][0:NOPE, :], ukn[:, k, 0, u - 4, :], ckv[:, k, :], start=(k == 0),
                                  stop=(k == 1))
                last.then_inc(s_qk, 1)

            def qk_sums(u):
                pe.wait_ge(s_qksq, u + 1)
                if u < 4:
                    for h in (2 * u, 2 * u + 1):
                        last = mm(ps[3][0:8, 0:T], C("head8", 64, QD)[:, 8 * h:8 * h + 8],
                                  sqb[0:QD, u % 2, (h % 2) * T:(h % 2 + 1) * T], start=(h == 0), stop=(h == HEADS - 1))
                else:
                    h = u - 4
                    if h == 0:
                        pe.wait_ge(s_ev, B_O)
                    last = mm(ps[1][0:8, :], C("head8", 64, QD)[:, 8 * h:8 * h + 8], sqb[0:QD, u % 2, :],
                              start=(h == 0), stop=(h == HEADS - 1))
                last.then_inc(s_qks8, 1)

            qk_product(0)
            qk_product(1)
            for u in range(12):
                if u + 2 < 12:
                    qk_product(u + 2)
                qk_sums(u)
            pe.wait_ge(s_qkc, 12)
            for t in range(4):
                for k in range(2):
                    last = mm(ps[4 + t][:, :], ckv[:, k, t * P:(t + 1) * P], uk[:, k, 512:1024], start=(k == 0), stop=(k == 1))
                last.then_inc(s_v, 1)
            def spread(u):
                pe.wait_ge(s_qkr8, 1 if u < 4 else 2)
                if u < 4:
                    pe.wait_ge(s_vc, u + 1)
                else:
                    pe.wait_ge(s_qrope, u - 3)
                for h in (2 * u, 2 * u + 1) if u < 4 else (u - 4,):
                    o = ps[4 + u % 4][0:QD, (h % 2) * T:(h % 2 + 1) * T] if u < 4 else ps[4 + u % 4][0:QD, :]
                    last = mm(o, C("bcast8", 768, 8)[:, h * QD:(h + 1) * QD], rstd[0:8, 0:T] if u < 4 else rt[0:8, :],
                              start=True, stop=True)
                last.then_inc(s_qkbc, 1)

            def rope_turn(u):
                pe.wait_ge(s_qkn, u + 1)
                if u < 4:
                    moving = qb[NOPE:QD, 2 * u:2 * u + 2, :].rearrange("p a t -> p (a t)")
                else:
                    moving = kb[NOPE:QD, u - 4, 0:T]
                mm(ps[4 + u % 4][NOPE:QD, 0:2 * T if u < 4 else T], con[NOPE:QD, _C["rot"]:_C["rot"] + ROPE], moving,
                   start=True, stop=True).then_inc(s_rot, 1)

            spread(0)
            for u in range(12):
                if u + 1 < 12:
                    spread(u + 1)
                rope_turn(u)

            pe.wait_ge(s_qrope, 12)

            def scores(i):
                wait(pe, s_pe_, i - 1)
                mm(ps[4 + i % 2][:, :], qb[0:QD, i // 2, (i % 2) * P:(i % 2 + 1) * P], kb[0:QD, i // 2, :],
                   start=True, stop=True).then_inc(s_sc, 1)

            def turn(i):
                pe.wait_ge(s_dg, i + 1)
                wait(pe, s_ptc, i - 1)
                for k in range(4):
                    last = mm(ps[6 + i % 2][:, k * P:(k + 1) * P], pbuf[:, i % 2, k * P:(k + 1) * P], diag[:, i % 2, :],
                              start=True, stop=True)
                last.then_inc(s_pt, 1)

            def times_v(h):
                pe.wait_ge(s_ptc, 2 * h + 2)
                pe.wait_ge(s_qkr8, 2)
                c = h // 2
                if h % 2 == 0:
                    wait(pe, s_aol, c - 1)
                for k in range(4):
                    last = mm(ps[c % 2][64 * (h % 2):64 * (h % 2) + 64, 0:T], vb[:, k, h * VD:(h + 1) * VD],
                              pt[:, h % 2, k, :], start=(k == 0), stop=(k == 3))
                last.then_inc(s_pv, 1)

            scores(0)
            scores(1)
            for i in range(2 * HEADS):
                turn(i)
                if i + 2 < 2 * HEADS:
                    scores(i + 2)
                if i % 2:
                    if i // 2 >= 1:
                        times_v(i // 2 - 1)
                if i in (3, 7, 11):
                    ada_columns(3 + (i - 3) // 4)
            times_v(HEADS - 1)

            pe.wait_ge(s_aol, 4)
            pe.wait_ge(s_csl, 4)
            for b in range(B_O, B_F):
                block_product(b)

            def ffn(l):
                def gate_up(f, fv):
                    wait(pe, s_flo, f + (l * NF + 1))
                    wait(pe, s_fm, f + (l * NF - 1))
                    for half in range(2):
                        for j in range(DJ):
                            w0 = (fv % 2) * FA + half * D + j * P
                            o = ps[fv % 2][:, half * T:(half + 1) * T]
                            mm(o, wh[:, w0:w0 + P], ah3[:, j, 0:T], start=(j == 0), stop=False)
                            mm(o, wh[:, w0:w0 + P], al3[:, j, 0:T], start=False, stop=False)
                            last = mm(o, wl[:, w0:w0 + P], ah3[:, j, 0:T], start=False, stop=(j == DJ - 1))
                    last.then_inc(s_fgu, 1)

                def down(f, fv, first=False, end=False):
                    wait(pe, s_fblo, f + (l * NF + 1))
                    wait(pe, s_fml, f + (l * NF + 1))
                    for j in range(DJ):
                        w0 = 2 * FA + (fv % 2) * D + j * P
                        o = ps[4 + j // 2][:, (j % 2) * T:(j % 2 + 1) * T]
                        a, b_ = mh[:, (fv % 2) * T:(fv % 2 + 1) * T], ml[:, (fv % 2) * T:(fv % 2 + 1) * T]
                        mm(o, wh[:, w0:w0 + P], a, start=first and j % 2 == 0, stop=False, skip_group_check=True)
                        mm(o, wh[:, w0:w0 + P], b_, start=False, stop=False, skip_group_check=True)
                        last = mm(o, wl[:, w0:w0 + P], a, start=False, stop=end, skip_group_check=True)
                    last.then_inc(s_fdn, 1)

                gate_up(0, 0)
                gate_up(1, 1)
                down(0, 0, first=True)
                ada_columns(6 + 6 * l)
                with pe.Fori(0, (NF - 2) // 4) as i:
                    f0 = pe.snap(i * 4)
                    for u in range(4):
                        gate_up(f0 + (2 + u), u)
                        down(f0 + (1 + u), u + 1)
                    pe.wait_ge(s_ada, i * 8 + (8 * (8 + 6 * l)))
                    pe.wait_ge(s_mod, i + (7 + 6 * l))
                    for k in range(8):
                        last = mm(ps[2][:, k:k + 1], acc[:, k * P:(k + 1) * P], ones[:, 0:1], start=True, stop=True)
                    last.then_inc(s_acol, 1)
                down(NF - 1, NF - 1, end=True)

            norm_sums(1)
            h_ready(1)
            ffn(0)

            norm_sums(2)
            pe.wait_ge(s_par, DFT_IN)
            pe.wait_ge(s_h, DJ * 3)
            for i in range(8):
                t, g = i // 4, i % 4
                wait(pe, s_v1c, i - 3)
                for k in range(2):
                    last = mm(ps[4 + i % 4][:, :], work[:, 2 * g + k, t * P:(t + 1) * P],
                              tabs[:, k, 0:2, :].rearrange("p a n -> p (a n)"), start=(k == 0), stop=(k == 1))
                last.then_inc(s_v1, 1)
            for c in range(8):
                g, half = c // 2, c % 2
                if c == 0:
                    pe.wait_ge(s_v1c, 8)
                wait(pe, s_f2l, c - 1)
                for t in range(TT):
                    for part in range(2):
                        last = mm(ps[c % 2][:, 0:T], vdft[:, t, g, part * T + half * P:part * T + (half + 1) * P],
                                  tabs[:, t, 2 * part, :], start=(t + part == 0), stop=(t + part == 2))
                last.then_inc(s_f2, 1)
            pe.wait_ge(s_f2l, 8)
            for b in range(B_F, B_Q2):
                block_product(b)
            norm_sums(3)
            h_ready(2)
            ffn(1)

            norm_sums(4)
            h_ready(3)
            for b in range(B_Q2, B_V2):
                block_product(b)
            pe.wait_ge(s_lo, B_V2 + 1)
            pe.wait_ge(s_ev, B_V2 - 1)
            for t in range(TT):
                for j in range(DJ):
                    w = slice((B_V2 % NSPLIT) * D + j * P, (B_V2 % NSPLIT) * D + (j + 1) * P)
                    tok = slice(t * P, (t + 1) * P)
                    o = ps[B_V2 % 2][:, tok]
                    mm(o, ah3[:, j, tok], wh[:, w], start=(j == 0), stop=False)
                    mm(o, al3[:, j, tok], wh[:, w], start=False, stop=False)
                    last = mm(o, ah3[:, j, tok], wl[:, w], start=False, stop=(j == DJ - 1))
            last.then_inc(s_blk, 1)
            pe.wait_ge(s_par, LRU_IN)
            for c in range(4):
                pe.wait_ge(s_xcv, c + 1)
                wait(pe, s_sgm, 2 * (c - 1))
                mm(ps[2 + c % 2][:, 0:T], rga[:, c, :], xcv[:, c, :], start=True, stop=True)
                mm(ps[2 + c % 2][:, T:2 * T], rgx[:, c, :], xcv[:, c, :], start=True, stop=True).then_inc(s_rg1, 1)
            pe.wait_ge(s_ev, B_V2 + 1)

            def win_scores(i):
                h, qb_ = i // 2, i % 2
                kv = slice(64 * (h // 4), 64 * (h // 4) + 64)
                wait(pe, s_ms2, i - 1)
                mm(ps[4 + i % 2][:, 0:(1 + qb_) * P], q2[kv, h % 4, qb_ * P:(qb_ + 1) * P], k2[kv, 0:(1 + qb_) * P],
                   start=True, stop=True).then_inc(s_sc, 1)

            def win_turn(i):
                pe.wait_ge(s_dg, 2 * HEADS + i + 1)
                wait(pe, s_ptc, 2 * HEADS + i - 1)
                for k in range(1 + i % 2):
                    last = mm(ps[6 + i % 2][:, k * P:(k + 1) * P], e2[:, i % 2, k * P:(k + 1) * P], dg2[:, i % 2, :],
                              start=True, stop=True)
                last.then_inc(s_pt, 1)

            def win_pv(i):
                h = i // 2
                kv = slice(64 * (h // 4), 64 * (h // 4) + 64)
                pe.wait_ge(s_ptc, 2 * HEADS + i + 1)
                wait(pe, s_at2, i - 1)
                n = 1 + i % 2
                for k in range(n):
                    last = mm(ps[i % 2][kv, 0:P], v2[:, k, kv], pt2[:, i % 2, k * P:(k + 1) * P],
                              start=(k == 0), stop=(k == n - 1))
                last.then_inc(s_pv, 1)

            win_scores(0)
            win_scores(1)
            for i in range(16):
                win_turn(i)
                if i + 2 < 16:
                    win_scores(i + 2)
                if i >= 1:
                    win_pv(i - 1)
            win_pv(15)
            for half in range(2):
                for c in range(4):
                    pe.wait_ge(s_msq, 4 * half + c + 1)
                    last = mm(ps[2 + half][:, 0:T], ones, work[:, 4 * half + c, T:2 * T], start=(c == 0), stop=(c == 3))
                last.then_inc(s_msum, 1)
            pe.wait_ge(s_mnl, 8)
            for b in range(B_OUT2, NB):
                block_product(b)

            norm_sums(5)
            pe.wait_ge(s_h, DJ * 6)
            pe.wait_ge(s_par, EXP_IN)
            for t in range(TT):
                for j in range(DJ):
                    last = mm(ps[4 + t][:, 0:NEXP], work[:, j, t * P:(t + 1) * P], rout[:, j, :], start=(j == 0),
                              stop=(j == DJ - 1))
                last.then_inc(s_lg, 1)
            pe.wait_ge(s_ev, NB)
            for i in range(4):
                wait(pe, s_htl, i - 1)
                for k in range(4):
                    j = (i % 2) * 4 + k
                    last = nc.tensor.transpose(ps[i % 2][:, k * P:(k + 1) * P], work[:, j, (i // 2) * P:(i // 2 + 1) * P],
                                               ident)
                last.then_inc(s_ht, 1)
            pe.wait_ge(s_mask, 2)
            mm(ps[6][:, 0:NEXP], C("triu", P), mask_[:, 0, :], start=True, stop=True)
            mm(ps[6][:, 32:64], ones, mask_[:, 0, :], start=True, stop=False)
            mm(ps[6][:, 32:64], C("triu", P), mask_[:, 1, :], start=False, stop=True)
            mm(ps[6][:, 64:96], ones, mask_[:, 0, :], start=True, stop=False)
            mm(ps[6][:, 64:96], ones, mask_[:, 1, :], start=False, stop=True).then_inc(s_cum, 1)
            pe.wait_ge(s_route, 2)
            for t in range(TT):
                last = nc.tensor.transpose(ps[7][0:NEXP, t * P:(t + 1) * P], gatew[:, t, :], ident)
            last.then_inc(s_gtt, 1)
            pe.wait_ge(s_gtc, 1)
            for i in range(4):
                if i >= 2:
                    pe.wait_ge(s_cumr, 1)
                last = mm(ps[4 + i][:, :], gT[:, (i // 2) * P:(i // 2 + 1) * P], bdn[:, (i % 2) * 512:(i % 2 + 1) * 512],
                          start=True, stop=True)
            last.then_inc(s_bd, 1)
            pe.wait_ge(s_htl, 4)
            pe.wait_ge(s_bgl, 1)

            def experts(p_):
                if p_:
                    pe.wait_ge(m["added"], MOE["added"])

                def gather(e, half):
                    moe_wait(pe, p_, "onehot", e + 2)
                    if half == 0:
                        moe_wait(pe, p_, "at_lo", 2 * e)
                    else:
                        moe_wait(pe, p_, "xs_lo", 2 * e + 3)
                    for src, bank in ((hth, 2), (htl, 3)):
                        for k in range(4):
                            f = slice((4 * half + k) * P, (4 * half + k + 1) * P)
                            for t in range(TT):
                                last = mm(ps[bank][:, k * P:(k + 1) * P], src[:, t, f], sone[:, t, :], start=(t == 0),
                                          stop=(t == TT - 1))
                    last.then_inc(m["gathered"], 1)

                def chunk_ready(e, q):
                    d_, l_ = lo_before(q + 1)
                    if q % CH in POOL_LO:
                        moe_wait(pe, p_, "lo_pool", e * 4 + l_)
                    else:
                        moe_wait(pe, p_, "lo_dve", e * 8 + d_)

                def first_product(e, q, k):
                    chunk_ready(e, q)
                    w_h, w_l = mwh[q % MRAW], mwl[q % MRAW]
                    s = slice(k * P, (k + 1) * P)
                    for stat, mov, end in ((xsh, w_h, False), (xsh, w_l, False), (xsl, w_h, k == GU_CH - 1)):
                        for n in range(4):
                            last = mm(ps[4 + n][:, :], stat[:, s], mov[:, n * 512:(n + 1) * 512], start=False, stop=end)
                    last.then_inc(m["chunk"], 1)

                def second_product(e, q, c):
                    chunk_ready(e, q)
                    w_h, w_l = mwh[q % MRAW], mwl[q % MRAW]
                    for i in range(2):
                        k = 2 * c + i
                        s = slice(k * P, (k + 1) * P)
                        for step, (stat, mov) in enumerate(((ath, w_h), (ath, w_l), (atl, w_h))):
                            for n in range(2):
                                last = mm(ps[n][:, :], stat[:, s], mov[:, i * D + n * 512:i * D + (n + 1) * 512],
                                          start=(k == 0 and step == 0), stop=(k == 7 and step == 2))
                    last.then_inc(m["chunk"], 1)

                def combine(e, t):
                    if t == 0:
                        moe_wait(pe, p_, "stt", e - 1)
                        moe_wait(pe, p_, "y_lo", 2 * (e - 1))
                    else:
                        moe_wait(pe, p_, "added", 4 * (e - 1) - 2)
                    for n in range(2):
                        mm(ps[n][:, :], stt[:, t * P:(t + 1) * P], mh[:, n * 512:(n + 1) * 512], start=True, stop=False)
                        last = mm(ps[n][:, :], stt[:, t * P:(t + 1) * P], ml[:, n * 512:(n + 1) * 512], start=False,
                                  stop=True)
                    last.then_inc(m["combined"], 1)

                def slots(e, col):
                    moe_wait(pe, p_, "xs_lo", 2 * e + 4)
                    moe_wait(pe, p_, "onehot2", e)
                    for t in range(TT):
                        nc.tensor.transpose(ps[2][:, t * P:(t + 1) * P], stwo[:, t, :], ident)
                    for t in range(TT):
                        last = mm(ps[2][:, T:T + 1], stwo[:, t, :], gatew[:, t, col], start=(t == 0), stop=(t == TT - 1))
                    last.then_inc(m["slots"], 1)

                def body(e, gu=True, dn=True, cmb=True, first=False):
                    if gu:
                        moe_wait(pe, p_, "select", e + 1)
                        moe_wait(pe, p_, "xs_lo", 2 * e + 2)
                        moe_wait(pe, p_, "gu", e)
                        for n in range(4):
                            mm(ps[4 + n][:, :], sel[:, :], bgu[:, n * 512:(n + 1) * 512], start=True, stop=False)
                    for k in range(GU_CH):
                        if gu:
                            first_product(e, k + 4 if first else k, k)
                        if cmb and k in (1, 4):
                            combine(e, 0 if k == 1 else 1)
                    if gu:
                        gather(e, 0)
                    if dn:
                        moe_wait(pe, p_, "at_lo", 2 * e)
                        if cmb:
                            moe_wait(pe, p_, "added", 4 * (e - 1))
                        shift = 0 if gu else GU_CH
                        second_product(e, 8 - shift, 0)
                        second_product(e, 9 - shift, 1)
                    if gu:
                        gather(e, 1)
                    if dn:
                        second_product(e, 10 - shift, 2)
                        if isinstance(e, int):
                            col = slice(e - 1, e)
                        else:
                            col = bass.ds(e - 1, 1)
                        if not gu:
                            moe_wait(pe, p_, "at_lo", 2 * e)
                        slots(e, col) if gu else slots_last(e, col)
                        second_product(e, 11 - shift, 3)
                    if gu:
                        moe_wait(pe, p_, "act", e + 1)
                        if dn:
                            moe_wait(pe, p_, "gcol", e)
                        else:
                            moe_wait(pe, p_, "xs_lo", 2 * e + 4)
                        for half in range(2):
                            for k in range(4):
                                f = (4 * half + k) * P
                                last = nc.tensor.transpose(ps[2 + half][:, k * P:(k + 1) * P], act_c[:, f:f + P], ident)
                            last.then_inc(m["turned"], 1)

                def slots_last(e, col):
                    moe_wait(pe, p_, "onehot2", e)
                    for t in range(TT):
                        nc.tensor.transpose(ps[2][:, t * P:(t + 1) * P], stwo[:, t, :], ident)
                    for t in range(TT):
                        last = mm(ps[2][:, T:T + 1], stwo[:, t, :], gatew[:, t, col], start=(t == 0), stop=(t == TT - 1))
                    last.then_inc(m["slots"], 1)

                gather(-1, 0)
                gather(-1, 1)
                body(0, dn=False, cmb=False, first=True)
                body(1, cmb=False)
                with pe.Fori(2, NEXP) as e:
                    body(e)
                body(NEXP, gu=False)
                combine(NEXP + 1, 0)
                combine(NEXP + 1, 1)
                pe.wait_ge(m["added"], (p_ + 1) * MOE["added"])

            experts(0)
            pe.wait_ge(s_flag, 1)
            over = pe.value_load(flag[0:1, 0:1], min_val=0, max_val=1)
            with pe.If(over > 0):
                experts(1)
            pe.end_ifs()
            for j in range(DJ):
                if j >= 4:
                    pe.wait_ge(s_x, 2 * DJ + j - 3)
                for t in range(TT):
                    last = nc.tensor.transpose(ps[4 + j % 4][:, t * P:(t + 1) * P], oacc[:, t, j * P:(j + 1) * P], ident)
                last.then_inc(s_ot, 1)
            norm_sums(6)

        @block.scalar
        def _(act):
            A = nc.scalar.activation
            chain = [0]

            def link(ins):
                chain[0] += 1
                ins.then_inc(s_act, 1)
                act.wait_ge(s_act, chain[0])

            def block_hi(b):
                act.wait_ge(s_raw[b % NRAW], 16 * (b // NRAW + 1))
                wait(act, s_blk, b - NSPLIT + 1)
                A(wh[:, (b % NSPLIT) * D:(b % NSPLIT + 1) * D], raw[:, (b % NRAW) * D:(b % NRAW + 1) * D], ACT.Copy
                  ).then_inc(s_hi, 1)

            def norm_squares(n, ready):
                for j in range(DJ):
                    ready(j)
                    A(work[:, j, 0:T], x[:, j, :], ACT.Square).then_inc(s_sq, 1)

            def norm_root(n, width=T):
                act.wait_ge(s_sum, n + 1)
                A(rt[:, 0:width], ps[3][:, 0:width], ACT.Sqrt, bias=V("eps"), scale=1.0 / D).then_inc(s_rt, 1)

            def h_hi(n, width=T):
                for j in range(DJ):
                    act.wait_ge(s_h, DJ * n + j + 1)
                    A(ah3[:, j, 0:width], work[:, j, 0:width], ACT.Copy).then_inc(s_hh, 1)

            act.wait_ge(s_con, 32)
            A(csil[:, :], vec[:, 0:16], ACT.Sigmoid).then_inc(s_sil, 1)
            act.wait_ge(s_xin, 16)
            act.wait_ge(s_xcin, 16)
            for j in range(DJ):
                link(A(work[:, j, 0:T], x[:, j, :], ACT.Square))
                A(work[:, j, T:2 * T], xc[:, j * TC:(j + 1) * TC], ACT.Square).then_inc(s_sq, 1)
            norm_root(0, 2 * T)
            for b in range(3):
                block_hi(b)
            h_hi(0, 2 * T)
            for b in range(3, 10):
                block_hi(b)
            for j in range(5):
                act.wait_ge(s_ev, j + 1)
                if j < 3:
                    A(sqf[:, j * T:(j + 1) * T], cq[:, j, :], ACT.Square).then_inc(s_cqs, 1)
                else:
                    A(pbuf[:, j - 3, :], ckv[:, j - 3, :], ACT.Square).then_inc(s_cqs, 1)
            for b in range(10, 13):
                block_hi(b)
            act.wait_ge(s_cqsum, 1)
            A(rt[:, 0:T], ps[3][:, 0:T], ACT.Sqrt, bias=V("eps"), scale=1.0 / QR).then_inc(s_cqrt, 1)
            act.wait_ge(s_cqsum, 2)
            act.wait_ge(s_cqn, 3)
            A(rt[:, :], ps[4][:, :], ACT.Sqrt, bias=V("eps"), scale=1.0 / KVR).then_inc(s_cqrt, 1)
            for b in range(13, B_O):
                block_hi(b)
            for c in range(CJ):
                act.wait_ge(s_cs, c + 1)
                act.wait_ge(s_blk, B_O)
                A(ah3[:, 4 + c, 0:T], work[:, 4 + c, T:2 * T], ACT.Copy).then_inc(s_csh, 1)
            for b in range(B_O, B_O + 3):
                block_hi(b)
            for u in range(12):
                act.wait_ge(s_qkc, u + 1)
                wait(act, s_qks8, u - 1)
                src = qb[0:QD, 2 * u:2 * u + 2, :].rearrange("p a t -> p (a t)") if u < 4 else kb[0:QD, u - 4, :]
                A(sqb[0:QD, u % 2, :], src, ACT.Square).then_inc(s_qksq, 1)
                if u == 5:
                    act.wait_ge(s_qks8, 4)
                    A(rstd[0:8, T:2 * T], ps[3][0:8, 0:T], ACT.Sqrt, bias=V("eps", 0, 8), scale=1.0 / QD
                      ).then_inc(s_qk8r, 1)
            act.wait_ge(s_qks8, 12)
            A(kpe[0:8, :], ps[1][0:8, :], ACT.Sqrt, bias=V("eps", 0, 8), scale=1.0 / QD).then_inc(s_qk8r, 1)
            for t in range(4):
                act.wait_ge(s_v, t + 1)
                A(vb[:, t, :], ps[4 + t][:, :], ACT.Copy).then_inc(s_vc, 1)

            def probs(i):
                act.wait_ge(s_nm, i + 1)
                wait(act, s_pt, i - 1)
                A(pbuf[:, i % 2, :], ps[4 + i % 2][:, :], ACT.Exp, bias=srow[:, i % 2, 1:2], scale=QK_SCALE,
                  accum_out=srow[:, i % 2, 2:3]).then_inc(s_pe_, 1)

            def probs_copy(i):
                act.wait_ge(s_pt, i + 1)
                h = i // 2
                wait(act, s_pv, h - 1)
                A(pt[:, h % 2, :, (i % 2) * P:(i % 2 + 1) * P], ps[6 + i % 2][:, :].rearrange("p (k t) -> p k t", k=4),
                  ACT.Copy).then_inc(s_ptc, 1)

            probs(0)
            for i in range(2 * HEADS):
                if i + 1 < 2 * HEADS:
                    probs(i + 1)
                probs_copy(i)
                if i % 4 == 3 and i >= 7:
                    attn_hi = (i - 7) // 4
                    act.wait_ge(s_pv, 2 * attn_hi + 2)
                    A(ah3[:, attn_hi, 0:T], ps[attn_hi % 2][:, 0:T], ACT.Copy).then_inc(s_ao, 1)
            act.wait_ge(s_pv, HEADS)
            A(ah3[:, 3, 0:T], ps[1][:, 0:T], ACT.Copy).then_inc(s_ao, 1)
            for b in range(B_O + 3, B_F):
                block_hi(b)

            def x_by_blocks(b):
                return lambda j: act.wait_ge(s_ev, b + j + 1)

            def x_by_ffn(k):
                return lambda j: act.wait_ge(s_x, DJ * k + j + 1)

            def ffn_hi(l, slot, loaded):
                act.wait_ge(s_fraw[slot], loaded + l * NF * 8)
                w = slice(slot * FA, (slot + 1) * FA)
                A(wh[:, w], raw[:, w], ACT.Copy).then_inc(s_fhi, 1)

            def ffn(l):
                def rest(f, slot, loaded):
                    wait(act, s_fgu, f + (l * NF + 1))
                    wait(act, s_fm, f + (l * NF - 1))
                    A(sg[:, slot, :], ps[slot][:, 0:T], ACT.Sigmoid).then_inc(s_fsig, 1)
                    act.wait_ge(s_fbraw[slot], loaded + l * NF * 8)
                    wait(act, s_fdn, f + (l * NF - 1))
                    w = slice(2 * FA + slot * D, 2 * FA + (slot + 1) * D)
                    A(wh[:, w], raw[:, w], ACT.Copy).then_inc(s_fbhi, 1)
                    wait(act, s_fm, f + (l * NF + 1))
                    A(mh[:, slot * T:(slot + 1) * T], mm_[:, slot, :], ACT.Copy).then_inc(s_fmh, 1)

                rest(0, 0, 16)
                with act.Fori(0, (NF - 2) // 4) as i:
                    f0 = act.snap(i * 4)
                    r0 = act.snap(i * 32)
                    for u in range(4):
                        wait(act, s_fgu, f0 + (l * NF + u + 1))
                        ffn_hi(l, u % 2, r0 + 16 * (u // 2 + 2))
                        rest(f0 + (1 + u), (1 + u) % 2, r0 + 16 * ((1 + u) // 2 + 1))
                rest(NF - 1, (NF - 1) % 2, 16 * ((NF - 1) // 2 + 1))

            norm_squares(1, x_by_blocks(B_O))
            norm_root(1)
            act.wait_ge(s_blk, B_F)
            ffn_hi(0, 0, 16)
            h_hi(1)
            ffn_hi(0, 1, 16)
            ffn(0)

            norm_squares(2, x_by_ffn(0))
            norm_root(2)
            act.wait_ge(s_fdn, NF)
            for i in range(8):
                act.wait_ge(s_v1, i + 1)
                A(vdft[:, i // 4, i % 4, :], ps[4 + i % 4][:, :], ACT.Copy).then_inc(s_v1c, 1)
            for b in range(B_F, B_F + NSPLIT):
                block_hi(b)
            for c in range(8):
                act.wait_ge(s_f2, c + 1)
                A(ah3[:, c, 0:T], ps[c % 2][:, 0:T], ACT.Copy).then_inc(s_f2h, 1)
            for b in range(B_F + NSPLIT, B_Q2):
                block_hi(b)
            norm_squares(3, x_by_blocks(B_F))
            norm_root(3)
            act.wait_ge(s_blk, B_Q2)
            ffn_hi(1, 0, 16)
            h_hi(3)
            ffn_hi(1, 1, 16)
            ffn(1)

            norm_squares(4, x_by_ffn(1))
            norm_root(4)
            act.wait_ge(s_fdn, 2 * NF)
            for b in range(B_Q2, B_Q2 + NSPLIT):
                block_hi(b)
            h_hi(4)
            for b in range(B_Q2 + NSPLIT, B_OUT2 + 5):
                block_hi(b)
            act.wait_ge(s_lru, 1)
            A(lam[:, 1, :], lam[:, 0, :], ACT.Exp, scale=-1.0).then_inc(s_lru, 1)
            for c in range(4):
                act.wait_ge(s_rg1, c + 1)
                A(work[:, c, 0:T], ps[2 + c % 2][:, 0:T], ACT.Sigmoid, bias=V("ba", c)).then_inc(s_sgm, 1)
                A(work[:, 4 + c, 0:T], ps[2 + c % 2][:, T:2 * T], ACT.Sigmoid, bias=V("bx", c)).then_inc(s_sgm, 1)

            def win_probs(i):
                n = (1 + i % 2) * P
                act.wait_ge(s_nm, 2 * HEADS + i + 1)
                wait(act, s_pt, 2 * HEADS + i - 1)
                A(e2[:, i % 2, 0:n], p2[:, i % 2, 0:n], ACT.Exp, bias=srow[:, i % 2, 1:2],
                  accum_out=srow[:, i % 2, 2:3]).then_inc(s_ex2, 1)
                A(srow[:, i % 2, 3:4], V("sink", i // 2), ACT.Exp, bias=srow[:, i % 2, 1:2]).then_inc(s_ex2, 1)

            def win_copy(i):
                n = (1 + i % 2) * P
                act.wait_ge(s_pt, 2 * HEADS + i + 1)
                wait(act, s_pv, HEADS + i - 1)
                A(pt2[:, i % 2, 0:n], ps[6 + i % 2][:, 0:n], ACT.Copy).then_inc(s_ptc, 1)

            act.wait_ge(s_lru, 3)
            for c in range(4):
                act.wait_ge(s_sgm, 8)
                A(work[:, c, T:2 * T], work[:, c, 0:T], ACT.Exp, scale=lam[:, 6, c:c + 1]).then_inc(s_ex, 1)
            for c in range(4):
                act.wait_ge(s_ex, 4)
                A(work[:, 4 + c, T:2 * T], work[:, c, 0:T], ACT.Tanh, scale=lam[:, 7, c:c + 1]).then_inc(s_th, 1)
            act.wait_ge(s_th, 4)
            for c in range(4):
                act.wait_ge(s_gel, 1)
                A(work[:, c, 0:T], gl[:, c, :], ACT.Tanh, scale=0.7978845608028654
                  ).then_inc(s_gelt, 1)
            win_probs(0)
            for i in range(16):
                if i + 1 < 16:
                    win_probs(i + 1)
                win_copy(i)
            for c in range(4):
                act.wait_ge(s_mul2, 1)
                A(work[:, 4 + c, T:2 * T], work[:, 4 + c, T:2 * T], ACT.Sqrt).then_inc(s_sq2, 1)
            for c in range(8):
                if c < 4:
                    act.wait_ge(s_at2, 16)
                    act.wait_ge(s_lruo, 4)
                    A(work[:, c, T:2 * T], atn[:, c, :], ACT.Square).then_inc(s_msq, 1)
                else:
                    A(work[:, c, T:2 * T], xcv[:, c - 4, :], ACT.Square).then_inc(s_msq, 1)
            for half in range(2):
                act.wait_ge(s_msum, half + 1)
                A(rt[:, half * T:(half + 1) * T], ps[2 + half][:, 0:T], ACT.Sqrt, bias=V("eps"), scale=1.0 / 512
                  ).then_inc(s_mrt, 1)
            for c in range(8):
                act.wait_ge(s_mn, c + 1)
                act.wait_ge(s_blk, B_V2 + 1)
                A(ah3[:, c, 0:T], work[:, c, 0:T], ACT.Copy).then_inc(s_mnh, 1)
            for b in range(B_OUT2 + 5, NB):
                block_hi(b)

            norm_squares(5, x_by_blocks(B_OUT2))
            norm_root(5)
            for i in range(4):
                act.wait_ge(s_ht, i + 1)
                act.wait_ge(s_blk, NB)
                A(hth[:, i // 2, (i % 2) * 512:(i % 2 + 1) * 512], ps[i % 2][:, :], ACT.Copy).then_inc(s_hth, 1)
            act.wait_ge(s_par, EXP_IN)
            A(bgu[:, :], bgr[:, :], ACT.Copy).then_inc(s_bgh, 1)
            for t in range(TT):
                act.wait_ge(s_tk, t + 1)
                A(rsc[:, t * 32 + 8:t * 32 + 12], rsc[:, t * 32:t * 32 + 4], ACT.Exp, bias=rsc[:, t * 32 + 16:t * 32 + 17],
                  accum_out=rsc[:, t * 32 + 17:t * 32 + 18]).then_inc(s_tke, 1)
            act.wait_ge(s_gtt, 1)
            A(gT[:, :], ps[7][0:NEXP, 0:T], ACT.Copy).then_inc(s_gtc, 1)

            def experts(p_):
                if p_:
                    act.wait_ge(m["added"], MOE["added"])
                else:
                    act.wait_ge(s_blk, NB)

                def hi(e, q):
                    n_ = e * 12 + (q - 4)
                    wait(act, s_mraw[q % MRAW], e * 48 + 16 * (q // 4) + p_ * MOE_RAW)
                    moe_wait(act, p_, "chunk", n_ - 3)
                    A(mwh[q % MRAW], raw[:, (q % MRAW) * 2048:(q % MRAW + 1) * 2048], ACT.Copy).then_inc(m["hi"], 1)

                def xs_hi(e, half):
                    moe_wait(act, p_, "gathered", 2 * e + 3 + half)
                    A(xsh[:, half * 512:(half + 1) * 512], ps[2][:, :], ACT.Copy).then_inc(m["xs_hi"], 1)

                def y_hi(e):
                    moe_wait(act, p_, "chunk", MOE["chunk"] if isinstance(e, int) and e > NEXP else 12 * (e - 1) + 8)
                    moe_wait(act, p_, "gcol", e - 1)
                    for n in range(2):
                        A(mh[:, n * 512:(n + 1) * 512], ps[n][:, :], ACT.Copy, scale=gcol[:, 0:1]).then_inc(m["y_hi"], 1)

                def body(e, gu=True, dn=True, cmb=True, q0=2):
                    if cmb:
                        y_hi(e)
                    for q in range(q0, 12 if gu else 4):
                        if q == 10 and dn and gu:
                            xs_hi(e, 0)
                        hi(e, q)
                    if gu:
                        if not dn:
                            xs_hi(e, 0)
                        moe_wait(act, p_, "gate", e + 1)
                        moe_wait(act, p_, "act", e)
                        A(sig_c, gate_c, ACT.Sigmoid, scale=ALPHA).then_inc(m["sig"], 1)
                        xs_hi(e, 1)
                        hi(e, 12)
                    if dn:
                        moe_wait(act, p_, "slots", e)
                        A(stt[:, :], ps[2][:, 0:T], ACT.Copy).then_inc(m["stt"], 1)
                    if gu:
                        hi(e, 13)
                        for half in range(2):
                            moe_wait(act, p_, "turned", 2 * e + 1 + half)
                            A(ath[:, half * 512:(half + 1) * 512], ps[2 + half][:, :], ACT.Copy).then_inc(m["at_hi"], 1)

                for q in range(4, 8):
                    hi(0, q)
                xs_hi(-1, 0)
                xs_hi(-1, 1)
                body(0, dn=False, cmb=False, q0=8)
                body(1, cmb=False)
                with act.Fori(2, NEXP) as e:
                    body(e)
                body(NEXP, gu=False)
                y_hi(NEXP + 1)

            experts(0)
            act.wait_ge(s_flag, 1)
            over = act.value_load(flag[0:1, 0:1], min_val=0, max_val=1)
            with act.If(over > 0):
                experts(1)
            act.end_ifs()
            norm_squares(6, x_by_ffn(2))
            norm_root(6)

        @block.gpsimd
        def _(pool):
            sub = lambda o, a, b: nc.gpsimd.tensor_tensor(o, a, b.bitcast(F32), ALU.subtract)

            def block_lo(b):
                pool.wait_ge(s_hi, b + 1)
                s = slice((b % NSPLIT) * D, (b % NSPLIT + 1) * D)
                sub(wl[:, s], raw[:, (b % NRAW) * D:(b % NRAW + 1) * D], wh[:, s]).then_inc(s_lo, 1)

            def ffn(l):
                def lo(f, fv):
                    wait(pool, s_fhi, f + (l * NF + 1))
                    s = slice((fv % 2) * FA, (fv % 2 + 1) * FA)
                    sub(wl[:, s], raw[:, s], wh[:, s]).then_inc(s_flo, 1)

                lo(0, 0)
                lo(1, 1)
                with pool.Fori(0, (NF - 2) // 4) as i:
                    f0 = pool.snap(i * 4)
                    for u in range(4):
                        lo(f0 + (2 + u), u)

            for b in range(B_F):
                block_lo(b)
            ffn(0)
            for b in range(B_F, B_Q2):
                block_lo(b)
            ffn(1)
            pool.wait_ge(s_fml, 2 * NF)
            nc.gpsimd.memset(rga[:, :, :], 0.0).then_inc(s_zero, 1)
            nc.gpsimd.memset(rgx[:, :, :], 0.0).then_inc(s_zero, 1)
            nc.gpsimd.memset(xr[:, :, 0:3], 0.0).then_inc(s_zero, 1)
            for b in range(B_Q2, NB):
                block_lo(b)

            def experts(p_):
                if p_:
                    pool.wait_ge(m["added"], MOE["added"])

                def lo(e, q):
                    moe_wait(pool, p_, "hi", e * 12 + (q - 3))
                    sub(mwl[q % MRAW], raw[:, (q % MRAW) * 2048:(q % MRAW + 1) * 2048], mwh[q % MRAW]
                        ).then_inc(m["lo_pool"], 1)

                for q in (4, 7, 10):
                    lo(0, q)
                with pool.Fori(1, NEXP) as e:
                    for q in POOL_LO:
                        lo(e, q)
                lo(NEXP, 1)

            experts(0)
            pool.wait_ge(s_flag, 1)
            over = pool.value_load(flag[0:1, 0:1], min_val=0, max_val=1)
            with pool.If(over > 0):
                experts(1)
            pool.end_ifs()

        @block.vector
        def _(dve):
            V_ = nc.vector
            TS, STT, TTn, COPY = V_.tensor_scalar, V_.scalar_tensor_tensor, V_.tensor_tensor, V_.tensor_copy
            chain = [0]

            def link(ins):
                chain[0] += 1
                ins.then_inc(s_dve, 1)
                dve.wait_ge(s_dve, chain[0])

            f32 = lambda a: a.bitcast(F32)

            def ada_step(dst, src, scalar, j):
                if j == 0:
                    return TS(dst, src, scalar, None, ALU.mult)
                return STT(dst, src, scalar, dst, ALU.mult, ALU.add)

            def ada(n):
                g, j = n // 8, n % 8
                dve.wait_ge(s_araw[n % 2], 16 * (n // 2 + 1))
                if j == 0:
                    wait(dve, s_acol, g)
                else:
                    dve.wait_ge(s_ada, n)
                if n < ADA_FIRST:
                    if j:
                        dve.wait_ge(s_adx, n)
                    ada_step(accx, araw[:, n % 2, :], csil[:, 8 + j:9 + j], j).then_inc(s_adx, 1)
                ada_step(acc[:, :], araw[:, n % 2, :], csil[:, j:j + 1] if g < 12 else V("c2", j), j).then_inc(s_ada, 1)

            def bias(g):
                return vec[:, _V["ada_b"] + 8 * g:_V["ada_b"] + 8 * g + 8]

            def mod_ready(g):
                dve.wait_ge(s_acol, g + 1)
                if g < 2:
                    TTn(modx[:, 8 * g:8 * g + 8], ps[2][:, 8:16], bias(g), ALU.add)
                TTn(mod[:, 8 * g:8 * g + 8], ps[2][:, 0:8], bias(g), ALU.add).then_inc(s_mod, 1)

            def m_col(g, j):
                return mod[:, 8 * g + j:8 * g + j + 1]

            def norm(n, gain, g_shift, hl=None, ctx_too=False):
                dve.wait_ge(s_mod, g_shift + 2)
                gcols = vec[:, gain:gain + 8]
                STT(gs[:, :], mod[:, 8 * g_shift + 8:8 * g_shift + 16], 1.0, gcols, ALU.add, ALU.mult)
                if ctx_too:
                    STT(gsx[:, :], modx[:, 8:16], 1.0, gcols, ALU.add, ALU.mult)
                w = 2 * T if ctx_too else T
                dve.wait_ge(s_rt, n + 1)
                link(V_.reciprocal(rstd[:, 0:w], rt[:, 0:w]))
                for j in range(DJ + 3):
                    if j < DJ:
                        if ctx_too:
                            TTn(work[:, j, T:2 * T], xc[:, j * TC:(j + 1) * TC], rstd[:, T:2 * T], ALU.mult)
                        TTn(work[:, j, 0:T], x[:, j, :], rstd[:, 0:T], ALU.mult).then_inc(s_nt, 1)
                    if 1 <= j <= DJ:
                        k = j - 1
                        dve.wait_ge(s_nt, DJ * n + k + 1)
                        if ctx_too:
                            TS(work[:, k, T:2 * T], work[:, k, T:2 * T], gsx[:, k:k + 1], modx[:, k:k + 1], ALU.mult, ALU.add)
                        TS(work[:, k, 0:T], work[:, k, 0:T], gs[:, k:k + 1], m_col(g_shift, k), ALU.mult, ALU.add
                           ).then_inc(s_h, 1)
                    if j >= 3 and hl is not None:
                        k = j - 3
                        dve.wait_ge(s_hh, DJ * hl + k + 1)
                        TTn(al3[:, k, 0:w], work[:, k, 0:w], f32(ah3[:, k, 0:w]), ALU.subtract).then_inc(s_hl, 1)

            def residual(b, j, g):
                dve.wait_ge(s_blk, b + 1)
                STT(x[:, j, :], ps[b % 2][:, 0:T], m_col(g, j), x[:, j, :], ALU.mult, ALU.add).then_inc(s_ev, 1)

            def evacuate(b, out, rows=slice(0, P), w=T):
                dve.wait_ge(s_blk, b + 1)
                COPY(out, ps[b % 2][rows, 0:w]).then_inc(s_ev, 1)

            dve.wait_ge(s_con, 32)
            dve.wait_ge(s_sil, 1)
            link(TTn(csil[:, :], csil[:, :], vec[:, 0:16], ALU.mult))
            for n in range(ADA_FIRST):
                ada(n)
                if n in (9, 15):
                    mod_ready(n // 10)
            norm(0, _V["n1"], 0, hl=0, ctx_too=True)

            V_.memset(czp[:, :, 0:1], 0.0).then_inc(s_zp, 1)
            V_.memset(czp[:, :, T + 1:T + 2], 0.0).then_inc(s_zp, 1)
            for b in range(B_O):
                if b < B_KV:
                    evacuate(b, cq[:, b, :])
                elif b < B_KPE:
                    evacuate(b, ckv[:, b - B_KV, :], w=2 * T)
                elif b == B_KPE:
                    evacuate(b, kpe[NOPE:QD, :], slice(NOPE, QD), 2 * T)
                elif b < B_CC:
                    evacuate(b, cbg[:, b - B_CB, :])
                elif b < B_CU:
                    evacuate(b, ccg[:, b - B_CC, :])
                else:
                    dve.wait_ge(s_blk, b + 1)
                    TTn(czp[:, b - B_CU, 1:T + 1], ps[b % 2][:, 0:T], ccg[:, b - B_CU, :], ALU.mult).then_inc(s_ev, 1)
                if b < 8:
                    ada(ADA_FIRST + b)
                if b == B_CC - 1:
                    dve.wait_ge(s_cqrt, 1)
                    link(V_.reciprocal(rstd[:, 0:T], rt[:, 0:T]))
                    for j in range(3):
                        STT(cq[:, j, :], cq[:, j, :], V("qg", j), rstd[:, 0:T], ALU.mult, ALU.mult).then_inc(s_cqn, 1)
                    dve.wait_ge(s_cqrt, 2)
                    dve.wait_ge(s_cqn, 3)
                    link(V_.reciprocal(rstd[:, :], rt[:, :]))
                    for j in range(2):
                        STT(ckv[:, j, :], ckv[:, j, :], V("kvg", j), rstd[:, :], ALU.mult, ALU.mult).then_inc(s_cqn, 1)
            dve.wait_ge(s_ev, B_O)
            dve.wait_ge(s_zp, 2)
            for c in range(CJ):
                ins = TS(ccg[:, c, :], czp[:, c, 0:T], V("conv", c), None, ALU.mult)
            link(ins)
            for i in (1, 2):
                for c in range(CJ):
                    ins = STT(ccg[:, c, :], czp[:, c, i:i + T], V("conv", 4 * i + c), ccg[:, c, :], ALU.mult, ALU.add)
                link(ins)
            for c in range(CJ):
                TTn(work[:, 4 + c, T:2 * T], ccg[:, c, :], cbg[:, c, :], ALU.mult).then_inc(s_cs, 1)
            mod_ready(2)
            for c in range(CJ):
                dve.wait_ge(s_csh, c + 1)
                TTn(al3[:, 4 + c, 0:T], work[:, 4 + c, T:2 * T], f32(ah3[:, 4 + c, 0:T]), ALU.subtract).then_inc(s_csl, 1)

            dve.wait_ge(s_cs, CJ)
            for u in range(12):
                dve.wait_ge(s_qk, u + 1)
                if u < 4:
                    COPY(qb[0:QD, 2 * u:2 * u + 2, :], ps[4 + u][0:QD, :].rearrange("p (a t) -> p a t", a=2)
                         ).then_inc(s_qkc, 1)
                else:
                    COPY(kb[NOPE:QD, u - 4, :], kpe[NOPE:QD, :])
                    COPY(kb[0:NOPE, u - 4, :], ps[4 + u % 4][0:NOPE, :]).then_inc(s_qkc, 1)
            dve.wait_ge(s_qk8r, 1)
            V_.reciprocal(rstd[0:8, 0:T], rstd[0:8, T:2 * T]).then_inc(s_qkr8, 1)
            dve.wait_ge(s_qk8r, 2)
            V_.reciprocal(rt[0:8, :], kpe[0:8, :]).then_inc(s_qkr8, 1)

            def unit(u, rows):
                return qb[rows, 2 * u:2 * u + 2, :] if u < 4 else kb[rows, u - 4, :]

            def qk_norm(u):
                dve.wait_ge(s_qkbc, u + 1)
                spread = ps[4 + u % 4][0:QD, :]
                if u < 4:
                    spread = spread.rearrange("p (a t) -> p a t", a=2)
                un = unit(u, slice(0, QD))
                STT(un, un, V("qgain" if u < 4 else "kgain", 0, QD), spread, ALU.mult, ALU.mult).then_inc(s_qkn, 1)

            cos, sin = [con[NOPE:QD, _C[n]:_C[n] + T] for n in ("cos", "sin")]

            def rope(u):
                dve.wait_ge(s_rot, u + 1)
                wait(dve, s_qrope, u - 1)
                r = slice(NOPE, QD)
                for a in range(2 if u < 4 else 1):
                    part = qb[r, 2 * u + a, :] if u < 4 else kb[r, u - 4, 0:T]
                    t = sqb[r, a, (u % 2) * T:(u % 2 + 1) * T]
                    TTn(t, ps[4 + u % 4][r, a * T:(a + 1) * T], sin, ALU.mult)
                    link(TTn(part, part, cos, ALU.mult))
                    ins = TTn(part, part, t, ALU.add)
                ins.then_inc(s_qrope, 1)

            qk_norm(0)
            for u in range(12):
                if u + 1 < 12:
                    qk_norm(u + 1)
                rope(u)

            def row_max(i):
                dve.wait_ge(s_sc, i + 1)
                link(V_.reduce_max(srow[:, i % 2, 0:1], ps[4 + i % 2][:, :], AX))
                TS(srow[:, i % 2, 1:2], srow[:, i % 2, 0:1], -QK_SCALE, None, ALU.mult).then_inc(s_nm, 1)

            def attn_lo(c):
                dve.wait_ge(s_ao, c + 1)
                TTn(al3[:, c, 0:T], ps[c % 2][:, 0:T], f32(ah3[:, c, 0:T]), ALU.subtract).then_inc(s_aol, 1)

            row_max(0)
            for i in range(2 * HEADS):
                if i + 1 < 2 * HEADS:
                    row_max(i + 1)
                dve.wait_ge(s_pe_, i + 1)
                link(V_.reciprocal(srow[:, i % 2, 3:4], srow[:, i % 2, 2:3]))
                wait(dve, s_pt, i - 1)
                TS(diag[:, i % 2, :], ident, srow[:, i % 2, 3:4], None, ALU.mult).then_inc(s_dg, 1)
                if i < 12:
                    ada(24 + 2 * i)
                    ada(25 + 2 * i)
                if i in (5, 9, 13):
                    mod_ready(3 + (i - 5) // 4)
                if i in (8, 12):
                    attn_lo((i - 8) // 4)
            attn_lo(2)
            attn_lo(3)
            for j in range(DJ):
                residual(B_O + j, j, 2)

            def ffn(l, g_gate):
                base_n, base_g = 48 + 48 * l, 6 + 6 * l

                def mul(f, slot):
                    wait(dve, s_fsig, f + (l * NF + 1))
                    TTn(sg[:, slot, :], ps[slot][:, 0:T], sg[:, slot, :], ALU.mult).then_inc(s_ft, 1)
                    wait(dve, s_ft, f + (l * NF + 1))
                    TTn(mm_[:, slot, :], ps[slot][:, T:2 * T], sg[:, slot, :], ALU.mult).then_inc(s_fm, 1)

                def los(f, slot):
                    wait(dve, s_fbhi, f + (l * NF + 1))
                    w = slice(2 * FA + slot * D, 2 * FA + (slot + 1) * D)
                    TTn(wl[:, w], raw[:, w], f32(wh[:, w]), ALU.subtract).then_inc(s_fblo, 1)
                    wait(dve, s_fmh, f + (l * NF + 1))
                    s = slice(slot * T, (slot + 1) * T)
                    TTn(ml[:, s], mm_[:, slot, :], f32(mh[:, s]), ALU.subtract).then_inc(s_fml, 1)

                for f in range(2):
                    mul(f, f)
                    los(f, f)
                    for j in range(6) if f == 0 else (6, 7):
                        ada(base_n + j)
                with dve.Fori(0, (NF - 2) // 4) as i:
                    f0 = dve.snap(i * 4)
                    n0 = dve.snap(i * 8 + (base_n + 8))
                    loaded = dve.snap(i * 64 + 16 * ((base_n + 8) // 2 + 1))
                    col = dve.snap(i * 8 + 8 * base_g)
                    cols = dve.snap(i + (base_g + 1))
                    for u in range(4):
                        mul(f0 + (2 + u), u % 2)
                        los(f0 + (2 + u), u % 2)
                        if u == 0:
                            dve.wait_ge(s_acol, cols)
                            TTn(mod[:, bass.ds(col, 8)], ps[2][:, 0:8], vec[:, bass.ds(col + _V["ada_b"], 8)], ALU.add
                                ).then_inc(s_mod, 1)
                        for j in (2 * u, 2 * u + 1):
                            dve.wait_ge(s_araw[j % 2], loaded + 16 * (j // 2))
                            if j == 0:
                                dve.wait_ge(s_acol, cols)
                            else:
                                dve.wait_ge(s_ada, n0 + j)
                            ada_step(acc[:, :], araw[:, j % 2, :], csil[:, j:j + 1] if l == 0 else V("c2", j), j
                                     ).then_inc(s_ada, 1)
                mod_ready(base_g + 5)
                dve.wait_ge(s_fdn, (l + 1) * NF)
                for j in range(DJ):
                    STT(x[:, j, :], ps[4 + j // 2][:, (j % 2) * T:(j % 2 + 1) * T], m_col(g_gate, j), x[:, j, :],
                        ALU.mult, ALU.add).then_inc(s_x, 1)

            norm(1, _V["n2"], 3, hl=1)
            ffn(0, 5)
            norm(2, _V["n1"] + 8, 6)
            for c in range(8):
                dve.wait_ge(s_f2h, c + 1)
                TTn(al3[:, c, 0:T], ps[c % 2][:, 0:T], f32(ah3[:, c, 0:T]), ALU.subtract).then_inc(s_f2l, 1)
            for j in range(DJ):
                residual(B_F + j, j, 8)
            norm(3, _V["n2"] + 8, 9, hl=2)
            ffn(1, 11)

            lam_in = vec[:, _V["lam"]:_V["lam"] + 4]
            STT(lam[:, 0, :], lam_in, -1.0, lam_in, ALU.mult, ALU.max).then_inc(s_lru, 1)
            norm(4, _V["gmix"], 12, hl=3)
            for b in range(B_Q2, B_OUT2):
                if b < B_K2:
                    evacuate(b, q2[:, b - B_Q2, :])
                elif b == B_K2:
                    evacuate(b, k2[:, :])
                elif b < B_XG:
                    evacuate(b, xr[:, b - B_XR, 3:T + 3])
                elif b < B_V2:
                    evacuate(b, xg[:, b - B_XG, :])
                else:
                    evacuate(b, v2[:, :, :].rearrange("p a n -> p (a n)"))
            dve.wait_ge(s_lru, 2)
            e_, z_, zz, q_, m8 = [lam[:, k, :] for k in (1, 2, 3, 4, 5)]
            link(TS(z_, e_, 2.0, None, ALU.add))
            link(V_.reciprocal(z_, z_))
            link(TTn(z_, e_, z_, ALU.mult))
            link(TTn(zz, z_, z_, ALU.mult))
            link(TS(q_, zz, 1.0 / 17, None, ALU.mult))
            for k in range(7, 0, -1):
                link(STT(q_, q_, 1.0 / (2 * k + 1), zz, ALU.add, ALU.mult))
            link(STT(q_, q_, 1.0, z_, ALU.add, ALU.mult))
            link(TS(m8, vec[:, _V["lam"]:_V["lam"] + 4], 0.0, 8.0, ALU.min, ALU.mult))
            link(STT(lam[:, 6, :], q_, -16.0, m8, ALU.mult, ALU.add))
            TS(lam[:, 7, :], lam[:, 6, :], -1.0, None, ALU.mult).then_inc(s_lru, 1)
            dve.wait_ge(s_zero, 3)
            dve.wait_ge(s_ev, B_OUT2)
            for i in range(4):
                for c in range(4):
                    if i == 0:
                        ins = TS(xcv[:, c, :], xr[:, c, 0:T], V("conv2", c), V("conv2b", c), ALU.mult, ALU.add)
                    else:
                        ins = STT(xcv[:, c, :], xr[:, c, i:i + T], V("conv2", 4 * i + c), xcv[:, c, :], ALU.mult, ALU.add)
                    if i == 3:
                        ins.then_inc(s_xcv, 1)
                if i < 3:
                    link(ins)
            link(TTn(gl[:, :, :], xg[:, :, :], xg[:, :, :], ALU.mult))
            link(TS(gl[:, :, :], gl[:, :, :], 0.044715, 1.0, ALU.mult, ALU.add))
            TTn(gl[:, :, :], gl[:, :, :], xg[:, :, :], ALU.mult).then_inc(s_gel, 1)

            def win_max(i):
                n = (1 + i % 2) * P
                h = i // 2
                dve.wait_ge(s_sc, 2 * HEADS + i + 1)
                wait(dve, s_ex2, 2 * (i - 1))
                STT(p2[:, i % 2, 0:n], ps[4 + i % 2][:, 0:n], Q_SCALE2, con[:, _C["mask"] + 2 * P - n:_C["mask"] + 2 * P],
                    ALU.mult, ALU.add).then_inc(s_ms2, 1)
                dve.wait_ge(s_ms2, i + 1)
                link(V_.reduce_max(srow[:, i % 2, 0:1], p2[:, i % 2, 0:n], AX))
                TS(srow[:, i % 2, 1:2], srow[:, i % 2, 0:1], V("sink", h), -1.0, ALU.max, ALU.mult).then_inc(s_nm, 1)

            def win_out(i):
                h = i // 2
                kv = slice(64 * (h // 4), 64 * (h // 4) + 64)
                dve.wait_ge(s_pv, HEADS + i + 1)
                COPY(atn[kv, h % 4, (i % 2) * P:(i % 2 + 1) * P], ps[i % 2][kv, 0:P]).then_inc(s_at2, 1)

            win_max(0)
            for i in range(16):
                if i + 1 < 16:
                    win_max(i + 1)
                dve.wait_ge(s_ex2, 2 * i + 2)
                link(TTn(srow[:, i % 2, 4:5], srow[:, i % 2, 2:3], srow[:, i % 2, 3:4], ALU.add))
                link(V_.reciprocal(srow[:, i % 2, 5:6], srow[:, i % 2, 4:5]))
                wait(dve, s_pt, 2 * HEADS + i - 1)
                TS(dg2[:, i % 2, :], ident, srow[:, i % 2, 5:6], None, ALU.mult).then_inc(s_dg, 1)
                if i >= 1:
                    win_out(i - 1)
                if i == 4:
                    dve.wait_ge(s_th, 4)
                    a_, th = work[:, 0:4, T:2 * T], work[:, 4:8, T:2 * T]
                    sq_ = xr[:, :, 0:T]
                    link(TTn(sq_, a_, a_, ALU.mult))
                    link(STT(th, sq_, 1.0, th, ALU.add, ALU.mult))
                    TS(th, th, 0.0, None, ALU.max).then_inc(s_mul2, 1)
                    dve.wait_ge(s_sgm, 8)
                    ig = work[:, 4:8, 0:T]
                    link(TTn(ig, ig, xcv[:, :, :], ALU.mult))
                    dve.wait_ge(s_gelt, 4)
                    link(STT(xg[:, :, :], work[:, 0:4, 0:T], 1.0, xg[:, :, :], ALU.add, ALU.mult))
            win_out(15)
            dve.wait_ge(s_sq2, 4)
            link(TTn(ig, th, ig, ALU.mult))
            for c in range(4):
                ins = V_.tensor_tensor_scan(gl[:, c, :], work[:, c, T:2 * T], work[:, 4 + c, 0:T], 0.0, ALU.mult, ALU.add)
            link(ins)
            for c in range(4):
                STT(xcv[:, c, :], gl[:, c, :], 0.5, xg[:, c, :], ALU.mult, ALU.mult).then_inc(s_lruo, 1)
            dve.wait_ge(s_mrt, 2)
            dve.wait_ge(s_lruo, 4)
            dve.wait_ge(s_at2, 16)
            link(V_.reciprocal(rstd[:, :], rt[:, :]))
            for c in range(10):
                if c < 8:
                    src = atn[:, c, :] if c < 4 else xcv[:, c - 4, :]
                    STT(work[:, c, 0:T], src, V("gattn", c) if c < 4 else V("glru", c - 4),
                        rstd[:, (c // 4) * T:(c // 4 + 1) * T], ALU.mult, ALU.mult).then_inc(s_mn, 1)
                if c >= 2:
                    k = c - 2
                    dve.wait_ge(s_mnh, k + 1)
                    TTn(al3[:, k, 0:T], work[:, k, 0:T], f32(ah3[:, k, 0:T]), ALU.subtract).then_inc(s_mnl, 1)
            for j in range(DJ):
                residual(B_OUT2 + j, j, 14)

            norm(5, _V["gffn"], 15)
            V_.memset(pos[:, :, :], -1.0).then_inc(s_pos, 1)
            iota32 = C("iota32", NEXP)
            for t in range(TT):
                r = lambda a, n=1: rsc[:, 32 * t + a:32 * t + a + n]
                dve.wait_ge(s_lg, t + 1)
                link(TTn(logit[:, t, :], ps[4 + t][:, 0:NEXP], vec[:, _V["brout"]:_V["brout"] + NEXP], ALU.add))
                link(V_.max(r(0, 8), logit[:, t, :]))
                TS(r(16), r(0), -1.0, None, ALU.mult).then_inc(s_tk, 1)
                link(V_.max_index(ridx[:, t, :], r(0, 8), logit[:, t, :]))
                link(COPY(r(20, TOPK), ridx[:, t, 0:TOPK]))
                for k in range(TOPK):
                    if k == 0:
                        ins = TS(mask_[:, t, :], iota32, r(20), None, ALU.is_equal)
                    else:
                        ins = STT(mask_[:, t, :], iota32, r(20 + k), mask_[:, t, :], ALU.is_equal, ALU.add)
                    if k < TOPK - 1:
                        link(ins)
                ins.then_inc(s_mask, 1)
            for i in range(4):
                dve.wait_ge(s_hth, i + 1)
                s = slice((i % 2) * 512, (i % 2 + 1) * 512)
                TTn(htl[:, i // 2, s], ps[i % 2][:, :], f32(hth[:, i // 2, s]), ALU.subtract).then_inc(s_htl, 1)
            for t in range(TT):
                r = lambda a, n=1: rsc[:, 32 * t + a:32 * t + a + n]
                dve.wait_ge(s_tke, t + 1)
                link(V_.reciprocal(r(18), r(17)))
                link(TS(r(24, TOPK), r(8, TOPK), r(18), None, ALU.mult))
                for k in range(TOPK):
                    dst = gatew[:, t, :] if k == 0 else logit[:, t, :]
                    ins = TS(dst, iota32, r(20 + k), r(24 + k), ALU.is_equal, ALU.mult)
                    if k:
                        link(ins)
                        ins = TTn(gatew[:, t, :], gatew[:, t, :], logit[:, t, :], ALU.add)
                    if k < TOPK - 1:
                        link(ins)
                ins.then_inc(s_route, 1)
            dve.wait_ge(s_cum, 1)
            dve.wait_ge(s_pos, 1)
            dve.wait_ge(s_mask, 2)
            for t in range(TT):
                link(STT(pos[:, t, 0:NEXP], ps[6][:, 32 * t:32 * t + 32], 1.0, mask_[:, t, :], ALU.add, ALU.mult))
                link(TS(pos[:, t, 0:NEXP], pos[:, t, 0:NEXP], -1.0, None, ALU.add))
            V_.reduce_max(rsc[:, 31:32], ps[6][:, 64:96], AX).then_inc(s_cumr, 1)
            dve.wait_ge(s_cumr, 1)
            TS(flag[0:1, 0:1], rsc[0:1, 31:32], CAP + 0.5, None, ALU.is_gt).then_inc(s_flag, 1)
            dve.wait_ge(s_bgh, 1)
            TTn(bgu[NEXP:2 * NEXP, :], bgr[NEXP:2 * NEXP, :], f32(bgu[NEXP:2 * NEXP, :]), ALU.subtract).then_inc(s_bgl, 1)
            dve.wait_ge(s_bgl, 1)
            dve.wait_ge(s_bd, 1)
            for i in range(4):
                COPY(oacc[:, i // 2, (i % 2) * 512:(i % 2 + 1) * 512], ps[4 + i][:, :]).then_inc(s_oi, 1)

            def experts(p_):
                if p_:
                    dve.wait_ge(m["added"], MOE["added"])
                    TS(pos[:, :, :], pos[:, :, :], -float(CAP), None, ALU.add).then_inc(s_pos, 1)
                    dve.wait_ge(s_pos, p_ + 1)
                else:
                    dve.wait_ge(s_oi, 4)

                def col(e):
                    return slice(e, e + 1) if isinstance(e, int) else bass.ds(e, 1)

                def onehot(dst, e, done):
                    for t in range(TT):
                        ins = TS(dst[:, t, :], C("iota", CAP), pos[:, t, col(e)], None, ALU.is_equal)
                    ins.then_inc(done, 1)

                def select(e):
                    TS(sel[:, :], ones[0:64, :], con[0:64, _C["eye64"]:_C["eye64"] + NEXP + 1][:, col(e)], None, ALU.mult
                       ).then_inc(m["select"], 1)

                def lo(e, q):
                    if q % CH in POOL_LO:
                        return
                    moe_wait(dve, p_, "hi", e * 12 + (q - 3))
                    TTn(mwl[q % MRAW], raw[:, (q % MRAW) * 2048:(q % MRAW + 1) * 2048], f32(mwh[q % MRAW]), ALU.subtract
                        ).then_inc(m["lo_dve"], 1)

                def xs_lo(e, half):
                    moe_wait(dve, p_, "xs_hi", 2 * e + 3 + half)
                    COPY(xsl[:, half * 512:(half + 1) * 512], ps[3][:, :]).then_inc(m["xs_lo"], 1)

                def y_lo(e):
                    for n in range(2):
                        moe_wait(dve, p_, "y_hi", 2 * (e - 2) + n + 1)
                        s = slice(n * 512, (n + 1) * 512)
                        STT(ml[:, s], ps[n][:, :], gcol[:, 0:1], f32(mh[:, s]), ALU.mult, ALU.subtract
                            ).then_inc(m["y_lo"], 1)

                def add(e, t):
                    moe_wait(dve, p_, "combined", 2 * (e - 2) + t + 1)
                    if t == 0:
                        moe_wait(dve, p_, "added", 4 * (e - 2))
                    for n in range(2):
                        o = oacc[:, t, n * 512:(n + 1) * 512]
                        TTn(o, ps[n][:, :], o, ALU.add).then_inc(m["added"], 1)

                def body(e, gu=True, dn=True, cmb=True, q0=0):
                    def lo_(q):
                        if q >= q0 and (gu or q < 4):
                            lo(e, q)

                    if gu:
                        moe_wait(dve, p_, "xs_lo", 2 * e + 2)
                        onehot(sone, e + 1, m["onehot"])
                    if dn:
                        onehot(stwo, e - 1, m["onehot2"])
                    lo_(2)
                    if cmb:
                        y_lo(e)
                    lo_(3)
                    if cmb:
                        add(e, 0)
                    for q in (5, 6):
                        lo_(q)
                    if cmb:
                        add(e, 1)
                    for q in (8, 9):
                        lo_(q)
                    if gu:
                        if not dn:
                            lo_(11)
                        moe_wait(dve, p_, "chunk", 12 * e + 4 if dn else 8)
                        xs_lo(e, 0)
                        moe_wait(dve, p_, "turned", 2 * e)
                        TS(gate_c, ps45, LIMIT, None, ALU.min).then_inc(m["gate"], 1)
                        TS(up_c, ps67, LIMIT, -LIMIT, ALU.min, ALU.max).then_inc(m["gu"], 1)
                        select(e + 1 if not isinstance(e, int) or e < NEXP - 1 else e)
                        if dn:
                            lo_(11)
                        moe_wait(dve, p_, "sig", e + 1)
                        TTn(sig_c, gate_c, sig_c, ALU.mult).then_inc(m["glu"], 1)
                        moe_wait(dve, p_, "glu", e + 1)
                        STT(act_c, up_c, 1.0, sig_c, ALU.add, ALU.mult).then_inc(m["act"], 1)
                        xs_lo(e, 1)
                        lo(e, 12)
                    if dn:
                        moe_wait(dve, p_, "stt", e)
                        COPY(gcol[:, :], ps[2][:, T:T + 1]).then_inc(m["gcol"], 1)
                    if gu:
                        for half in range(2):
                            moe_wait(dve, p_, "at_hi", 2 * e + 1 + half)
                            s = slice(half * 512, (half + 1) * 512)
                            TTn(atl[:, s], ps[2 + half][:, :], f32(ath[:, s]), ALU.subtract).then_inc(m["at_lo"], 1)

                onehot(sone, 0, m["onehot"])
                select(0)
                for q in (5, 6):
                    lo(0, q)
                xs_lo(-1, 0)
                xs_lo(-1, 1)
                body(0, dn=False, cmb=False, q0=8)
                body(1, cmb=False, q0=2)
                with dve.Fori(2, NEXP) as e:
                    body(e, q0=2)
                body(NEXP, gu=False, q0=2)
                y_lo(NEXP + 1)
                add(NEXP + 1, 0)
                add(NEXP + 1, 1)

            experts(0)
            over = dve.value_load(flag[0:1, 0:1], min_val=0, max_val=1)
            with dve.If(over > 0):
                experts(1)
            dve.end_ifs()
            for j in range(DJ):
                dve.wait_ge(s_ot, j + 1)
                STT(x[:, j, :], ps[4 + j % 4][:, 0:T], m_col(17, j), x[:, j, :], ALU.mult, ALU.add).then_inc(s_x, 1)
            dve.wait_ge(s_rt, 7)
            link(V_.reciprocal(rstd[:, 0:T], rt[:, 0:T]))
            for j in range(DJ):
                STT(work[:, j, 0:T], x[:, j, :], V("gfin", j), rstd[:, 0:T], ALU.mult, ALU.mult).then_inc(s_fy, 1)


def constants():
    c = np.zeros((P, NC_), np.float32)

    def put(name, a):
        c[:a.shape[0], _C[name]:_C[name] + a.shape[1]] = a

    r = np.arange(P)
    put("ident", np.eye(P))
    put("ones", np.ones((P, P)))
    put("triu", (r[:, None] < r[None, :]) * 1.0)
    put("iota", np.broadcast_to(np.arange(P), (P, P)))
    put("iota32", np.broadcast_to(np.arange(NEXP), (P, NEXP)))
    put("head8", np.broadcast_to(np.eye(HEADS).reshape(1, 64), (P, 64)))
    put("bcast8", np.repeat(np.eye(HEADS), QD, axis=1))
    put("eye64", np.eye(NEXP, NEXP + 1)[np.arange(2 * NEXP) % NEXP])
    put("mask", np.concatenate([np.where(r[None, :] > r[:, None], 0, NEG), np.where(r[None, :] <= r[:, None], 0, NEG)], 1))
    t = np.arange(T)
    half = ROPE // 2
    inv = (1.0 / (np.float32(10000.0) ** (np.arange(0, half, 2, dtype=np.float32) / np.float32(half)))).astype(np.float32)
    rows, cols = (t // 64).astype(np.float32), (t % 64).astype(np.float32)
    ang = np.concatenate([np.tile(rows[None] * inv[:, None], (2, 1)), np.tile(cols[None] * inv[:, None], (2, 1))])
    c[NOPE:QD, _C["cos"]:_C["cos"] + T] = np.cos(ang.astype(np.float64))
    c[NOPE:QD, _C["sin"]:_C["sin"] + T] = np.sin(ang.astype(np.float64))
    rot = np.zeros((ROPE, ROPE))
    for base in (0, half):
        for i in range(half // 2):
            rot[base + half // 2 + i, base + i] = -1.0
            rot[base + i, base + half // 2 + i] = 1.0
    c[NOPE:QD, _C["rot"]:_C["rot"] + ROPE] = rot
    phase = 2 * np.pi * ((t[:, None] * t[None, :]) % T) / T
    tab = np.stack([np.cos(phase), np.sin(phase), -np.sin(phase)], 1) / np.sqrt(float(T))
    tab = np.ascontiguousarray(tab.reshape(2, P, 3, T).transpose(1, 0, 2, 3)).astype(np.float32)
    return c, tab


def kernel(**inp):
    import concourse.bacc as bacc
    from concourse.bass_utils import run_bass_kernel_spmd

    a = {k: np.asarray(v) for k, v in inp.items()}

    def cols(v):
        return np.reshape(v, (-1, P)).T

    def feature_major(v):
        return v.T.reshape(DJ, P, -1).transpose(1, 0, 2)

    def blocks(w):
        return w.reshape(DJ, P, -1, P).transpose(2, 1, 0, 3).reshape(-1, P, D)

    perm = np.arange(512).reshape(2, 4, HD).transpose(1, 0, 2).reshape(512)
    v = np.zeros((P, NV), np.float32)

    def put(name, x):
        x = np.asarray(x)
        v[:x.shape[0], _V[name]:_V[name] + x.shape[1]] = x

    put("c", cols(a["c"][0])); put("cx", cols(a["c_ctx"])); put("c2", cols(a["c_2"][0]))
    put("ada_b", np.concatenate([cols(a["ada_b"][0]), cols(a["ada_b"][1]), cols(a["b_ada_2"][0])], 1))
    put("n1", cols(a["norm1_g"])); put("n2", cols(a["norm2_g"]))
    put("gmix", cols(a["g_mix_2"][0])); put("gffn", cols(a["g_ffn_2"][0])); put("gfin", cols(a["g_final_2"]))
    put("qg", cols(a["q_norm_g"][0])); put("kvg", cols(a["kv_norm_g"][0]))
    put("qgain", a["q_gain"][0][:, None]); put("kgain", a["k_gain"][0][:, None])
    put("conv", cols(a["conv_w"][0])); put("conv2", cols(a["conv_w_2"][0])); put("conv2b", cols(a["conv_b_2"][0]))
    put("ba", cols(a["b_rg_a_2"][0])); put("bx", cols(a["b_rg_x_2"][0])); put("lam", cols(a["lru_lambda_2"][0]))
    put("gattn", cols(a["g_attn_out_2"][0][perm])); put("glru", cols(a["g_lru_out_2"][0]))
    put("sink", np.broadcast_to(a["sinks_2"][0], (P, 8)))
    put("eps", np.full((P, 1), EPS, np.float32))
    put("brout", np.broadcast_to(a["b_router_2"][0], (P, NEXP)))

    w = a["w_in"][0]
    kp = np.zeros((D, P), np.float32)
    kp[:, NOPE:QD] = w[:, QR + KVR:QR + KVR + ROPE]
    w2 = a["w_in_2"][0]
    wo2 = a["w_out_2"][0]
    blk = np.concatenate([
        blocks(w[:, 0:QR + KVR]), blocks(kp), blocks(w[:, QR + KVR + ROPE:]), blocks(a["w_o"][0]),
        blocks(a["w_fourier"][0]), blocks(w2[:, 0:512][:, perm]), blocks(w2[:, 512:640]), blocks(w2[:, 768:1280]),
        blocks(w2[:, 1280:1792]), blocks(w2[:, 640:768]), blocks(np.concatenate([wo2[0:512][perm], wo2[512:]]))])
    uq = a["w_uq"][0].reshape(3, P, HEADS * QD).transpose(1, 0, 2)
    uk = a["w_ukv"][0].reshape(2, P, HEADS, 2, NOPE).transpose(1, 0, 3, 2, 4).reshape(P, 2, 2 * HEADS * NOPE)
    ffa = np.stack([np.stack([a[n][l].reshape(DJ, P, NF, P).transpose(2, 1, 0, 3).reshape(NF, P, D)
                              for n in ("ffn_w1", "ffn_w3")], 2).reshape(NF, P, FA) for l in range(2)])
    con, tab = constants()
    arrays = {
        "xT": feature_major(a["x"][0]), "xc": feature_major(a["ctx"][0]).reshape(P, -1), "vec": v, "con": con, "tab": tab,
        "ada": np.concatenate([a["ada_w"], a["w_ada_2"]]), "blk": blk, "uq": uq, "uk": uk, "ffa": ffa,
        "ffb": a["ffn_w2"].reshape(2, NF, P, D), "rga": a["w_rg_a_2"][0], "rgx": a["w_rg_x_2"][0],
        "rout": a["w_router_2"][0].reshape(DJ, P, NEXP).transpose(1, 0, 2), "gu": a["w_gu_2"][0], "bgu": a["b_gu_2"][0],
        "dn": a["w_down_2"][0], "bdn": a["b_down_2"][0],
    }
    arrays = {k + "_dram": np.ascontiguousarray(x) for k, x in arrays.items()}
    nc = bacc.Bacc("TRN2", target_bir_lowering=False, num_devices=1)
    args = [nc.dram_tensor(k, x.shape, mybir.dt.from_np(x.dtype), kind="ExternalInput").ap() for k, x in arrays.items()]
    args.append(nc.dram_tensor("out_dram", (P, DJ, T), mybir.dt.float32, kind="ExternalOutput").ap())
    build(nc, *args)
    r = run_bass_kernel_spmd(nc, [arrays], core_ids=[0])
    out = r.results[0]["out_dram"]
    return np.ascontiguousarray(np.asarray(out).transpose(2, 1, 0).reshape(1, T, D))
```

```python
import numpy as np
import concourse.bass as bass
from concourse import mybir
from concourse.alu_op_type import AluOpType as ALU
from contextlib import ExitStack

P = 128
D = 1024
DJ = D // P
T = 256
TT = T // P
TC = 256
EPS = 1e-6
QR, KVR, ROPE, NOPE, VD, HEADS = 384, 256, 32, 64, 64, 8
QD = NOPE + ROPE
QK_SCALE = QD ** -0.5
CONV = 512
CJ = CONV // P
FF = 2816
NF = FF // P
FA = 2 * D
HD = 64
Q_SCALE2 = HD ** -0.5
NEXP, TOPK = 32, 4
CAP = 128
PASSES = T // CAP
LIMIT, ALPHA = 7.0, 1.702
NEG = -3.0e38
B_Q, B_KV, B_KPE, B_CB, B_CC, B_CU = 0, 3, 5, 6, 10, 14
B_O, B_F = 18, 26
B_XR, B_Q2, B_K2, B_V2, B_XG = 34, 38, 42, 43, 44
B_2 = B_XR
B_OUT2 = 48
NB = 56
NRAW, NSPLIT = 3, 6
WIN = [(0, (0, 1, 2, 3)), (0, (4, 5, 6, 7)), (1, (0, 1)), (1, (2, 3)), (1, (4, 5)), (1, (6, 7))]
AG = 1024
NGRP = 18
GU_CH, DN_CH = D // P, D // (2 * P)
CH = GU_CH + DN_CH
MRAW = 4
TOKEN_BANK = (0, 1, 6, 7)
POOL_LO = (1, 4, 7, 10)

_V = {}
_n = 0
for _name, _m in [("c", 8), ("cx", 8), ("c2", 8), ("ada_b", 18 * 8), ("n1", 16), ("n2", 16), ("gmix", 8), ("gffn", 8),
                  ("gfin", 8), ("qg", 3), ("kvg", 2), ("qgain", 1), ("kgain", 1), ("conv", 12), ("conv2", 16),
                  ("conv2b", 4), ("ba", 4), ("bx", 4), ("lam", 4), ("gattn", 4), ("glru", 4), ("sink", 8),
                  ("eps", 1), ("brout", 32)]:
    _V[_name] = _n
    _n += _m
NV = _n
_C = {}
_n = 0
for _name, _m in [("ident", 128), ("ones", 128), ("triu", 128), ("iota", 128), ("iota32", 32), ("head8", 64),
                  ("bcast8", 8 * QD), ("cos", T), ("sin", T), ("rot", ROPE), ("mask", 2 * P), ("eye64", NEXP + 1)]:
    _C[_name] = _n
    _n += _m
NC_ = _n


def build(nc, xT_d, xc_d, vec_d, con_d, tab_d, ada_d, blk_d, uq_d, uk_d, ffna_d, ffnb_d, rga_d, rgx_d, rout_d,
          gu_d, bgu_d, dn_d, bdn_d, out_d):
    F32, F32R, I32 = mybir.dt.float32, mybir.dt.float32r, mybir.dt.int32
    ACT = mybir.ActivationFunctionType
    AX = mybir.AxisListType.X
    ctx = ExitStack()
    with ctx:
        def sb(name, shape, dt=F32, stack=ctx):
            return stack.enter_context(nc.sbuf_tensor(name, shape, dt))

        def sem(name):
            return ctx.enter_context(nc.semaphore(name))

        x = sb("x", [P, DJ, T])
        work = sb("work", [P, DJ, 2 * T])
        ah = sb("ah", [P, DJ * 2 * T], F32R)
        al = sb("al", [P, DJ * 2 * T], F32R)
        ah3 = ah[:, :].rearrange("p (j t) -> p j t", j=DJ)
        al3 = al[:, :].rearrange("p (j t) -> p j t", j=DJ)
        raw = sb("raw", [P, 8192])
        wh = sb("wh", [P, 6144], F32R)
        wl = sb("wl", [P, 6144], F32R)
        mh = sb("mh", [P, 1024], F32R)
        ml = sb("ml", [P, 1024], F32R)
        con = sb("con", [P, NC_])
        vec = sb("vec", [P, NV])
        mod = sb("mod", [P, NGRP * 8])
        gs = sb("gs", [P, 8])
        gsx = sb("gsx", [P, 8])
        rt = sb("rt", [P, 2 * T])
        rstd = sb("rstd", [P, 2 * T])
        csil = sb("csil", [P, 16])
        modx = sb("modx", [P, 16])
        srow = sb("srow", [P, 2, 8])
        flag = sb("flag", [1, 1], I32)

        def C(name, w, rows=P):
            return con[0:rows, _C[name]:_C[name] + w]

        def V(name, i=0, rows=P):
            return vec[0:rows, _V[name] + i:_V[name] + i + 1]

        ident, ones = C("ident", P), C("ones", P)

        ph = ExitStack()
        acc = sb("acc", [P, AG], F32, ph)
        araw = sb("araw", [P, 2, AG], F32, ph)
        base = ExitStack()
        xc = sb("xc", [P, DJ * TC], F32, base)
        kbuf = sb("kbuf", [P, HEADS * 2 * T], F32, base)
        pbuf = sb("pbuf", [P, 2, 2 * T], F32, base)
        sqb = sb("sqb", [P, 2, 2 * T], F32, base)
        kpe = sb("kpe", [P, 2 * T], F32, base)
        base.close()
        base = ExitStack()
        sg = sb("sg", [P, 2, T], F32, base)
        mm_ = sb("mm_", [P, 2, T], F32, base)
        tabs = sb("tabs", [P, 2, 3, T], F32, base)
        vdft = sb("vdft", [P, TT, 4, 2 * T], F32, base)
        base.close()
        base = ExitStack()
        q2 = sb("q2", [P, 4, T], F32, base)
        k2 = sb("k2", [P, T], F32, base)
        v2 = sb("v2", [P, TT, P], F32, base)
        xr = sb("xr", [P, 4, T + 3], F32, base)
        xg = sb("xg", [P, 4, T], F32, base)
        xcv = sb("xcv", [P, 4, T], F32, base)
        rga = sb("rga", [P, 4, P], F32, base)
        rgx = sb("rgx", [P, 4, P], F32, base)
        atn = sb("atn", [P, 4, T], F32, base)
        p2 = sb("p2", [P, 2, 2 * T], F32, base)
        pt2 = sb("pt2", [P, 2, 2 * T], F32, base)
        wcol = sb("wcol", [P, 6, 5, 4], F32, base)
        nsink = sb("nsink", [P, 8], F32, base)
        lam = sb("lam", [P, 8, 4], F32, base)
        base.close()
        ph.close()
        mo = ExitStack()
        oacc = sb("oacc", [P, TT, D], F32, mo)
        wh4 = sb("wh4", [P, 2048], F32R, mo)
        wl4 = sb("wl4", [P, 2048], F32R, mo)
        sone = sb("sone", [P, TT, CAP], F32R, mo)
        stwo = sb("stwo", [P, TT, CAP], F32, mo)
        stt = sb("stt", [P, T], F32R, mo)
        sel = sb("sel", [64, P], F32R, mo)
        bgu = sb("bgu", [64, 2 * D], F32R, mo)
        gcol = sb("gcol", [P, 1], F32, mo)
        rout = sb("rout", [P, DJ, NEXP], F32, mo)
        logit = sb("logit", [P, TT, NEXP], F32, mo)
        gatew = sb("gatew", [P, TT, NEXP], F32, mo)
        pos = sb("pos", [P, TT, NEXP + 1], F32, mo)
        mask_ = sb("mask_", [P, TT, NEXP], F32, mo)
        rsc = sb("rsc", [P, 64], F32, mo)
        ridx = sb("ridx", [P, TT, 8], mybir.dt.uint32, mo)
        gT = sb("gT", [NEXP, T], F32, mo)
        bdn = sb("bdn", [NEXP, D], F32, mo)
        mo.close()

        psum = ctx.enter_context(nc.psum_tensor("psum", [P, 8, 512], F32))
        ps = [psum[:, i, :] for i in range(8)]
        ps45, ps67 = [psum[:, i:i + 2, :].rearrange("p a n -> p (a n)") for i in (4, 6)]

        uq = raw[:, 3072:3072 + 3 * HEADS * QD].rearrange("p (k n) -> p k n", k=3)
        uk = raw[:, 5376:5376 + 2 * D].rearrange("p (k n) -> p k n", k=2)
        ukn = uk.rearrange("p k (a h d) -> p k a h d", a=2, h=HEADS)
        qb = work[:, 0:4, :].rearrange("p a (b t) -> p (a b) t", b=2)
        vb = work[:, 4:8, :]
        cq = xc[:, 0:768].rearrange("p (j t) -> p j t", j=3)
        ckv = xc[:, 768:1792].rearrange("p (j t) -> p j t", j=2)
        pt = xc[:, :].rearrange("p (s k t) -> p s k t", s=2, k=4)
        kb = kbuf[:, :].rearrange("p (h t) -> p h t", h=HEADS)
        cbg = kbuf[:, 0:1024].rearrange("p (j t) -> p j t", j=4)
        ccg = kbuf[:, 1024:2048].rearrange("p (j t) -> p j t", j=4)
        czp = kbuf[:, 2048:2048 + 4 * (T + 2)].rearrange("p (j t) -> p j t", j=4)
        sqf = sqb[:, :, :].rearrange("p a t -> p (a t)")
        hth = ah[:, 0:2048].rearrange("p (a n) -> p a n", a=TT)
        htl = al[:, 0:2048].rearrange("p (a n) -> p a n", a=TT)
        xsh, xsl = ah[:, 2048:3072], al[:, 2048:3072]
        ath, atl = ah[:, 3072:4096], al[:, 3072:4096]
        atsq = q2
        wflat = work[:, :, :].rearrange("p j t -> p (j t)")
        gate_c, up_c, sig_c, act_c = [wflat[:, i * D:(i + 1) * D] for i in range(4)]
        mwh = [wh[:, i * 2048:(i + 1) * 2048] for i in range(3)] + [wh4[:, :]]
        mwl = [wl[:, i * 2048:(i + 1) * 2048] for i in range(3)] + [wl4[:, :]]
        afirst = [araw[:, 0, :], araw[:, 1, :], kbuf[:, 0:AG], kbuf[:, AG:2 * AG]]
        arow = kbuf[0:2, 2 * AG:4 * AG]
        bgr = oacc[0:64, :, :].rearrange("p a n -> p (a n)")
        gl = acc[:, :].rearrange("p (j t) -> p j t", j=4)

        s_con, s_vec, s_xin, s_xcin, s_out = [sem(n) for n in (
            "consts_loaded", "vectors_loaded", "x_loaded", "ctx_loaded", "out_stored")]
        s_par = sem("parameters_loaded")
        MLA_IN, DFT_IN, LRU_IN, EXP_IN = 32, 48, 48 + 256, 48 + 256 + 64
        s_raw = [sem(f"block_loaded{i}") for i in range(NRAW)]
        s_hi, s_lo, s_blk, s_ev = [sem(n) for n in ("block_hi", "block_lo", "block_product", "block_evacuated")]
        s_araw = [sem(f"ada_loaded{i}") for i in range(4)]
        s_ada, s_adp, s_arow, s_acol, s_mod = [sem(n) for n in (
            "ada_acc", "ada_product", "ada_rows", "ada_columns", "mod_ready")]
        s_sil = sem("c_sigmoid")
        s_x = sem("x_chunk")
        s_nt, s_zp, s_pos = sem("norm_scaled"), sem("conv_pads"), sem("places_cleared")
        s_sq, s_sum, s_rt, s_h, s_hh, s_hl = [sem(n) for n in (
            "norm_squares", "norm_sums", "norm_root", "h_chunk", "h_hi", "h_lo")]
        s_sqx = sem("squares_summed")
        s_ntx, s_hx, s_hhx, s_hlx = [sem("ctx_" + n) for n in ("norm_scaled", "h_chunk", "h_hi", "h_lo")]
        s_dve, s_act = sem("dve_chain"), sem("act_chain")
        s_cqs, s_cqsum, s_cqrt, s_cqn = [sem(n) for n in ("lora_squares", "lora_sums", "lora_root", "lora_normed")]
        s_qk, s_qkc, s_qksq, s_qks8, s_qk8r, s_qkr8, s_qkbc, s_qkn, s_rot, s_qrope = [sem(n) for n in (
            "qk_product", "qk_copied", "qk_squares", "qk_sums", "qk_root", "qk_rstd", "qk_rstd_spread", "qk_normed",
            "rope_turned", "rope_done")]
        s_v, s_vc = sem("v_product"), sem("v_copied")
        s_sc, s_nm, s_pe_, s_dg, s_pt, s_ptc, s_pv, s_ao = [sem(n) for n in (
            "scores", "row_max", "probs", "probs_scaled", "probs_turned", "probs_copied", "pv_product", "attn_hi")]
        s_aol, s_cs, s_csh, s_csl = [sem(n) for n in ("attn_lo", "conv_out", "conv_hi", "conv_lo")]
        s_fraw = [sem(f"ffn_loaded{i}") for i in range(2)]
        s_fbraw = [sem(f"ffn_down_loaded{i}") for i in range(2)]
        s_fbhi, s_fblo, s_fhi, s_flo, s_fgu, s_fsig, s_ft, s_fm, s_fmh, s_fml, s_fdn = [sem(f"ffn_{n}") for n in (
            "down_hi", "down_lo", "hi", "lo", "gate_up", "sigmoid", "gate", "mul", "mul_hi", "mul_lo", "down")]
        s_v1, s_v1c, s_f2, s_f2h, s_f2l = [sem(n) for n in (
            "dft_features", "dft_features_copied", "dft_tokens", "dft_hi", "dft_lo")]
        s_th, s_lruo = sem("lru_tanh"), sem("lru_out")
        s_zero = sem("pads_cleared")
        s_xcv, s_rg1, s_sgm, s_lru, s_ex, s_mul2, s_sq2, s_gel, s_gelt = [sem(n) for n in (
            "lru_conv", "lru_gates", "lru_sigmoids", "lru_log", "lru_exp", "lru_mult", "lru_root", "gelu_arg", "gelu_tanh")]
        s_ms2, s_ex2, s_at2 = [sem(n) for n in ("win_masked", "win_probs", "win_out")]
        s_msq, s_msum, s_mrt, s_mn, s_mnh, s_mnl = [sem(n) for n in (
            "merge_squares", "merge_sums", "merge_root", "merged", "merged_hi", "merged_lo")]
        s_lg, s_tk, s_tke, s_mask, s_cum, s_route, s_ht, s_hth, s_htl, s_flag = [sem(n) for n in (
            "logits", "top_values", "top_exp", "chosen", "slot_counts", "routed", "h_turned", "h_tok_hi", "h_tok_lo",
            "overflow_known")]
        s_cumr = sem("slot_counts_read")
        s_gtt, s_gtc, s_bd, s_oi, s_bgh, s_bgl = [sem(n) for n in (
            "gates_turned", "gates_copied", "down_bias_sum", "out_started", "gu_bias_hi", "gu_bias_lo")]
        MOE = {"hi": 12 * NEXP, "lo_dve": 8 * NEXP, "lo_pool": 4 * NEXP, "chunk": 12 * NEXP, "onehot": NEXP + 1,
               "onehot2": NEXP, "select": NEXP + 1, "gathered": 2 * NEXP + 2, "xs_hi": 2 * NEXP + 2, "xs_lo": 2 * NEXP + 2,
               "gu": NEXP, "gate": NEXP, "sig": NEXP, "glu": NEXP, "act": NEXP, "turned": 2 * NEXP, "at_hi": 2 * NEXP,
               "at_lo": 2 * NEXP, "slots": NEXP, "stt": NEXP, "gcol": NEXP, "y_hi": 2 * NEXP, "y_lo": 2 * NEXP,
               "combined": 2 * NEXP, "added": 4 * NEXP}
        m = {n: sem("moe_" + n) for n in MOE}
        s_mraw = [sem(f"moe_loaded{i}") for i in range(MRAW)]
        MOE_RAW = 16 * CH * NEXP // MRAW
        s_ot, s_fy = sem("out_turned"), sem("final_chunk")

        block = ctx.enter_context(nc.Block())

        def lo_before(q):
            n = q + 24
            pool = sum(1 for k in range(4, n) if k % CH in POOL_LO)
            return (n - 4 - pool) - 16, pool - 8

        def wait(eng, s, value):
            if not isinstance(value, int) or value > 0:
                eng.wait_ge(s, value)

        def moe_wait(eng, p_, name, value):
            if p_ or not isinstance(value, int) or value > 0:
                eng.wait_ge(m[name], value + p_ * MOE[name])

        def ada_chunk_ap(g, j):
            return ada_d[g // 6, j * P:(j + 1) * P, (g % 6) * AG:(g % 6 + 1) * AG]

        ADA_FIRST = 2 * 8

        @block.sync
        def _(sp):
            def ada(n):
                if n < ADA_FIRST:
                    if n >= 4:
                        sp.wait_ge(s_adp, n - 3)
                    sp.dma_start(afirst[n % 4], ada_chunk_ap(n // 8, n % 8)).then_inc(s_araw[n % 4], 16)
                else:
                    if n < ADA_FIRST + 2:
                        sp.wait_ge(s_adp, n - 3)
                    else:
                        sp.wait_ge(s_ada, n - 1 - ADA_FIRST)
                    sp.dma_start(araw[:, n % 2, :], ada_chunk_ap(n // 8, n % 8)).then_inc(s_araw[n % 2], 16)

            def blk(b):
                if b >= NRAW:
                    sp.wait_ge(s_hi, b - NRAW + 1)
                    sp.wait_ge(s_lo, b - NRAW + 1)
                sp.dma_start(raw[:, (b % NRAW) * D:(b % NRAW + 1) * D], blk_d[b]).then_inc(s_raw[b % NRAW], 16)

            sp.dma_start(vec[:, :], vec_d).then_inc(s_vec, 16)
            ada(0)
            sp.dma_start(x[:, :, :], xT_d).then_inc(s_xin, 16)
            ada(1)
            sp.dma_start(xc[:, :], xc_d).then_inc(s_xcin, 16)
            ada(2)
            sp.dma_start(con[:, :], con_d).then_inc(s_con, 16)
            for n in range(3, 12):
                ada(n)
            for b in range(NRAW):
                blk(b)
            for n in range(12, ADA_FIRST):
                ada(n)
            ada(ADA_FIRST)
            ada(ADA_FIRST + 1)
            for b in range(NRAW, 6):
                blk(b)
            sp.dma_start(uq, uq_d).then_inc(s_par, 16)
            sp.dma_start(uk, uk_d).then_inc(s_par, 16)
            blk(6)
            blk(7)
            for n in range(2, 8):
                ada(ADA_FIRST + n)
                blk(6 + n)
            for b in range(14, B_O + 3):
                blk(b)
            for n in range(24, 42):
                ada(n)
            for b in range(B_O + 3, B_F):
                blk(b)
                ada(b - B_O + 39)
            ada(47)

            def ffn_a(l, slot, src):
                sp.dma_start(raw[:, slot * FA:(slot + 1) * FA], src).then_inc(s_fraw[slot], 16)

            def ffn_b(l, slot, src):
                sp.dma_start(raw[:, 2 * FA + slot * D:2 * FA + (slot + 1) * D], src).then_inc(s_fbraw[slot], 16)

            def ffn(l):
                sp.wait_ge(s_lo, B_F if l == 0 else B_2)
                if l == 0:
                    sp.wait_ge(s_v, 4)
                for f in range(2):
                    ffn_a(l, f, ffna_d[l, f])
                    ffn_b(l, f, ffnb_d[l, f])
                base_n = 48 + 48 * l
                with sp.Fori(0, (NF - 2) // 4) as i:
                    f0 = sp.snap(i * 4)
                    g0 = sp.snap(i * AG)
                    ada_done = sp.snap(i * 8 + (base_n - 1 - ADA_FIRST))
                    for u in range(4):
                        f, split = sp.snap(f0 + (2 + u)), sp.snap(f0 + (l * NF + 1 + u))
                        sp.wait_ge(s_flo, split)
                        ffn_a(l, u % 2, ffna_d[l, bass.ds(f, 1), :, :].rearrange("a p n -> p (a n)"))
                        for j in (2 * u, 2 * u + 1):
                            summed = sp.snap(ada_done + j)
                            sp.wait_ge(s_ada, summed)
                            sp.dma_start(araw[:, j % 2, :], ada_d[l + 1, j * P:(j + 1) * P, bass.ds(g0, AG)]
                                         ).then_inc(s_araw[j % 2], 16)
                        sp.wait_ge(s_fblo, split)
                        ffn_b(l, u % 2, ffnb_d[l, bass.ds(f, 1), :, :].rearrange("a p n -> p (a n)"))
                for j in range(8):
                    ada(base_n + 40 + j)

            ffn(0)
            sp.wait_ge(s_flo, NF)
            sp.wait_ge(s_pv, HEADS)
            sp.dma_start(tabs[:, :, :, :], tab_d).then_inc(s_par, 16)
            for b in range(B_F, B_2):
                blk(b)
            ffn(1)
            sp.wait_ge(s_flo, 2 * NF)
            for b in range(B_2, B_2 + NRAW):
                blk(b)
            sp.wait_ge(s_f2, 8)
            sp.wait_ge(s_fml, 2 * NF)
            sp.wait_ge(s_zero, 3)
            for c_ in range(4):
                for hb in range(2):
                    sl = slice(64 * hb, 64 * hb + 64)
                    sp.dma_start(rga[sl, c_, 64 * hb:64 * hb + 64], rga_d[2 * c_ + hb]).then_inc(s_par, 16)
                    sp.dma_start(rgx[sl, c_, 64 * hb:64 * hb + 64], rgx_d[2 * c_ + hb]).then_inc(s_par, 16)
            for b in range(B_2 + NRAW, NB):
                blk(b)
            sp.wait_ge(s_mnl, 8)
            sp.dma_start(rout[:, :, :], rout_d).then_inc(s_par, 16)
            sp.dma_start(bgr[0:NEXP, :], bgu_d).then_inc(s_par, 16)
            sp.dma_start(bgr[NEXP:2 * NEXP, :], bgu_d).then_inc(s_par, 16)
            sp.dma_start(bdn[:, :], bdn_d).then_inc(s_par, 16)
            sp.wait_ge(s_lo, NB)

            def experts(p_):

                def load(q, e, static):
                    slot = raw[:, (q % MRAW) * 2048:(q % MRAW + 1) * 2048]
                    if q < GU_CH:
                        src = gu_d[e, q * P:(q + 1) * P, :] if static else \
                            gu_d[bass.ds(e, 1), q * P:(q + 1) * P, :].rearrange("a p n -> p (a n)")
                    else:
                        c_ = q - GU_CH
                        src = dn_d[e - 1] if static else dn_d[bass.ds(e - 1, 1), :, :].rearrange("a k n -> (a k) n")
                        src = src[c_ * 256:(c_ + 1) * 256, :].rearrange("(i p) n -> p i n", p=P)
                        slot = slot.rearrange("p (i n) -> p i n", i=2)
                    sp.dma_start(slot, src).then_inc(s_mraw[q % MRAW], 16)

                def chunk(e, q, e8, e4, static, kind=None):
                    d_, l_ = lo_before(q - MRAW + 1)
                    name, value = ("lo_pool", e4 + l_) if (q - MRAW) % CH in POOL_LO else ("lo_dve", e8 + d_)
                    if not static or 12 * e - 4 + q >= MRAW:
                        if not static:
                            value = sp.snap(value + p_ * MOE[name])
                            sp.wait_ge(m[name], value)
                        else:
                            moe_wait(sp, p_, name, value)
                    load(q if kind is None else kind, e, static)

                for q in range(4, 12):
                    chunk(0, q, 0, 0, True, q - 4)
                with sp.Fori(1, NEXP) as e:
                    e8, e4, ev = sp.snap(e * 8), sp.snap(e * 4), sp.snap(e + 0)
                    for q in range(CH):
                        chunk(ev, q, e8, e4, False)
                for q in range(DN_CH):
                    chunk(NEXP, q, 8 * NEXP, 4 * NEXP, True, GU_CH + q)

            experts(0)
            sp.wait_ge(s_flag, 1)
            over = sp.value_load(flag[0:1, 0:1], min_val=0, max_val=1)
            with sp.If(over > 0):
                sp.wait_ge(m["added"], MOE["added"])
                experts(1)
            sp.end_ifs()
            for j in range(DJ):
                sp.wait_ge(s_fy, j + 1)
                sp.dma_start(out_d[:, j, :], work[:, j, 0:T]).then_inc(s_out, 16)
            sp.wait_ge(s_out, 16 * DJ)

        @block.tensor
        def _(pe):
            mm = nc.tensor.matmul

            def ada_columns(g):
                pe.wait_ge(s_ada, 8 * (g - 1))
                pe.wait_ge(s_mod, g)
                for i in range(8):
                    last = mm(ps[2][:, i:i + 1], acc[:, i * P:(i + 1) * P], ones[:, 0:1], start=True, stop=True)
                last.then_inc(s_acol, 1)

            def ada_rows(g):
                both = csil[:, :].rearrange("p (a j) -> p a j", a=2)
                for j in range(8):
                    n = 8 * g + j
                    pe.wait_ge(s_araw[n % 4], 16 * (n // 4 + 1))
                    for half in range(2):
                        last = mm(ps[4 + 2 * g + half][0:2, :], both[:, :, j], afirst[n % 4][:, half * 512:(half + 1) * 512],
                                  start=(j == 0), stop=(j == 7))
                    last.then_inc(s_adp, 1)

            def row_columns(g):
                pe.wait_ge(s_arow, g + 1)
                wait(pe, s_mod, g)
                for i in range(8):
                    c0 = g * AG + i * P
                    last = mm(ps[2][:, 2 * i:2 * i + 2], arow[:, c0:c0 + P], ident[0:2, 0:2], start=True, stop=True)
                last.then_inc(s_acol, 1)

            def norm_sums(n):
                for j in range(DJ):
                    pe.wait_ge(s_sq, DJ * n + j + 1)
                    last = mm(ps[3][:, 0:T], ones, work[:, j, 0:T], start=(j == 0), stop=(j == DJ - 1))
                    if n == 1 and j == 0:
                        last.then_inc(s_fdn, 1)
                last.then_inc(s_sum, 1)

            def block_product(b, width=T, fresh=None):
                pe.wait_ge(s_lo, b + 1)
                wait(pe, s_ev, b - 1)
                w0 = (b % NSPLIT) * D
                for j in range(DJ):
                    if fresh is not None:
                        pe.wait_ge(fresh[0], fresh[1] + j + 1)
                    w = slice(w0 + j * P, w0 + (j + 1) * P)
                    o = ps[b % 2][:, 0:width]
                    mm(o, wh[:, w], ah3[:, j, 0:width], start=(j == 0), stop=False)
                    mm(o, wh[:, w], al3[:, j, 0:width], start=False, stop=False)
                    last = mm(o, wl[:, w], ah3[:, j, 0:width], start=False, stop=(j == DJ - 1))
                last.then_inc(s_blk, 1)

            pe.wait_ge(s_dve, 1)
            ada_rows(0)
            pe.wait_ge(s_con, 16)
            pe.wait_ge(s_sqx, 1)
            mm(ps[3][:, :], ones, kpe[:, :], start=True, stop=True).then_inc(s_sum, 1)
            row_columns(0)
            ada_rows(1)
            row_columns(1)
            for b in range(B_CB):
                block_product(b, T if b < B_KV else 2 * T, fresh={0: (s_hl, 0), B_KV: (s_hlx, 0)}.get(b))
            for b in range(B_CB, B_CC):
                block_product(b)
            for j in range(3):
                pe.wait_ge(s_cqs, j + 1)
                last = mm(ps[3][:, 0:T], ones, sqf[:, j * T:(j + 1) * T], start=(j == 0), stop=(j == 2))
            last.then_inc(s_cqsum, 1)
            for j in range(2):
                pe.wait_ge(s_cqs, 4 + j)
                last = mm(ps[4][:, :], ones, pbuf[:, j, :], start=(j == 0), stop=(j == 1))
            last.then_inc(s_cqsum, 1)
            for b in range(B_CC, B_O):
                block_product(b)
            ada_columns(2)

            pe.wait_ge(s_par, MLA_IN)
            pe.wait_ge(s_cqn, 5)

            def qk_product(u):
                wait(pe, s_qkc, u - 3)
                if u < 4:
                    for h in (2 * u, 2 * u + 1):
                        for k in range(3):
                            last = mm(ps[4 + u % 4][0:QD, (h % 2) * T:(h % 2 + 1) * T], uq[:, k, h * QD:(h + 1) * QD],
                                      cq[:, k, :], start=(k == 0), stop=(k == 2))
                else:
                    for k in range(2):
                        last = mm(ps[4 + u % 4][0:NOPE, :], ukn[:, k, 0, u - 4, :], ckv[:, k, :], start=(k == 0),
                                  stop=(k == 1))
                last.then_inc(s_qk, 1)

            def qk_sums(u):
                pe.wait_ge(s_qksq, u + 1)
                if u < 4:
                    for h in (2 * u, 2 * u + 1):
                        last = mm(ps[3][0:8, 0:T], C("head8", 64, QD)[:, 8 * h:8 * h + 8],
                                  sqb[0:QD, u % 2, (h % 2) * T:(h % 2 + 1) * T], start=(h == 0), stop=(h == HEADS - 1))
                else:
                    h = u - 4
                    if h == 0:
                        pe.wait_ge(s_ev, B_O)
                    last = mm(ps[1][0:8, :], C("head8", 64, QD)[:, 8 * h:8 * h + 8], sqb[0:QD, u % 2, :],
                              start=(h == 0), stop=(h == HEADS - 1))
                last.then_inc(s_qks8, 1)

            qk_product(0)
            qk_product(1)
            for u in range(12):
                if u + 2 < 12:
                    qk_product(u + 2)
                qk_sums(u)
            pe.wait_ge(s_qkc, 12)
            for t in range(4):
                for k in range(2):
                    last = mm(ps[4 + t][:, :], ckv[:, k, t * P:(t + 1) * P], uk[:, k, 512:1024], start=(k == 0), stop=(k == 1))
                last.then_inc(s_v, 1)
            def spread(u):
                pe.wait_ge(s_qkr8, 1 if u < 4 else 2)
                if u < 4:
                    pe.wait_ge(s_vc, u + 1)
                else:
                    pe.wait_ge(s_qrope, u - 3)
                for h in (2 * u, 2 * u + 1) if u < 4 else (u - 4,):
                    o = ps[4 + u % 4][0:QD, (h % 2) * T:(h % 2 + 1) * T] if u < 4 else ps[4 + u % 4][0:QD, :]
                    last = mm(o, C("bcast8", 768, 8)[:, h * QD:(h + 1) * QD], rstd[0:8, 0:T] if u < 4 else rt[0:8, :],
                              start=True, stop=True)
                last.then_inc(s_qkbc, 1)

            def rope_turn(u):
                pe.wait_ge(s_qkn, u + 1)
                if u < 4:
                    moving = qb[NOPE:QD, 2 * u:2 * u + 2, :].rearrange("p a t -> p (a t)")
                else:
                    moving = kb[NOPE:QD, u - 4, 0:T]
                mm(ps[4 + u % 4][NOPE:QD, 0:2 * T if u < 4 else T], con[NOPE:QD, _C["rot"]:_C["rot"] + ROPE], moving,
                   start=True, stop=True).then_inc(s_rot, 1)

            spread(0)
            for u in range(12):
                if u + 1 < 12:
                    spread(u + 1)
                rope_turn(u)

            pe.wait_ge(s_qrope, 12)

            def scores(i):
                wait(pe, s_pe_, i - 1)
                mm(ps[4 + i % 2][:, :], qb[0:QD, i // 2, (i % 2) * P:(i % 2 + 1) * P], kb[0:QD, i // 2, :],
                   start=True, stop=True).then_inc(s_sc, 1)

            def turn(i):
                pe.wait_ge(s_dg, i + 1)
                wait(pe, s_ptc, i - 1)
                for k in range(4):
                    last = nc.tensor.transpose(ps[6 + i % 2][:, k * P:(k + 1) * P], pbuf[:, i % 2, k * P:(k + 1) * P], ident)
                last.then_inc(s_pt, 1)

            def times_v(h):
                pe.wait_ge(s_ptc, 2 * h + 2)
                pe.wait_ge(s_qkr8, 2)
                c = h // 2
                if h % 2 == 0:
                    wait(pe, s_aol, c - 1)
                for k in range(4):
                    last = mm(ps[c % 2][64 * (h % 2):64 * (h % 2) + 64, 0:T], vb[:, k, h * VD:(h + 1) * VD],
                              pt[:, h % 2, k, :], start=(k == 0), stop=(k == 3))
                last.then_inc(s_pv, 1)

            scores(0)
            scores(1)
            for i in range(2 * HEADS):
                if i + 2 < 2 * HEADS:
                    scores(i + 2)
                turn(i)
                if i % 2:
                    if i // 2 >= 1:
                        times_v(i // 2 - 1)
                if i == 8:
                    ada_columns(3)
            times_v(HEADS - 1)

            pe.wait_ge(s_aol, 4)
            pe.wait_ge(s_csl, 4)
            for b in range(B_O, B_F):
                block_product(b)
                if b == B_O:
                    ada_columns(4)

            def ffn(l):
                def gate_up(f, fv, fresh=None):
                    wait(pe, s_flo, f + (l * NF + 1))
                    wait(pe, s_fm, f + (l * NF - 1))
                    for half in range(2):
                        for j in range(DJ):
                            if fresh is not None:
                                pe.wait_ge(s_hl, DJ * fresh + j + 1)
                            w0 = (fv % 2) * FA + half * D + j * P
                            o = ps[fv % 2][:, half * T:(half + 1) * T]
                            mm(o, wh[:, w0:w0 + P], ah3[:, j, 0:T], start=(j == 0), stop=False)
                            mm(o, wh[:, w0:w0 + P], al3[:, j, 0:T], start=False, stop=False)
                            last = mm(o, wl[:, w0:w0 + P], ah3[:, j, 0:T], start=False, stop=(j == DJ - 1))
                    last.then_inc(s_fgu, 1)

                def down(f, fv, first=False, end=False):
                    wait(pe, s_fblo, f + (l * NF + 1))
                    wait(pe, s_fml, f + (l * NF + 1))
                    for j in range(DJ):
                        w0 = 2 * FA + (fv % 2) * D + j * P
                        o = ps[4 + j // 2][:, (j % 2) * T:(j % 2 + 1) * T]
                        a, b_ = mh[:, (fv % 2) * T:(fv % 2 + 1) * T], ml[:, (fv % 2) * T:(fv % 2 + 1) * T]
                        mm(o, wh[:, w0:w0 + P], a, start=first and j % 2 == 0, stop=False, skip_group_check=True)
                        mm(o, wh[:, w0:w0 + P], b_, start=False, stop=False, skip_group_check=True)
                        last = mm(o, wl[:, w0:w0 + P], a, start=False, stop=end, skip_group_check=True)
                    last.then_inc(s_fdn, 1)

                gate_up(0, 0, fresh=1 + l)
                gate_up(1, 1)
                down(0, 0, first=True)
                with pe.Fori(0, (NF - 2) // 4) as i:
                    f0 = pe.snap(i * 4)
                    for u in range(4):
                        gate_up(f0 + (2 + u), u)
                        if u == 2:
                            pe.wait_ge(s_ada, i * 8 + (8 * (5 + 6 * l)))
                            pe.wait_ge(s_mod, i + (6 + 6 * l))
                            for k in range(8):
                                last = mm(ps[2][:, k:k + 1], acc[:, k * P:(k + 1) * P], ones[:, 0:1], start=True, stop=True)
                            last.then_inc(s_acol, 1)
                        down(f0 + (1 + u), u + 1)
                down(NF - 1, NF - 1, end=True)
                ada_columns(11 + 6 * l)

            norm_sums(1)
            ada_columns(5)
            ffn(0)

            norm_sums(2)
            pe.wait_ge(s_par, DFT_IN)
            pe.wait_ge(s_h, DJ * 3)
            for i in range(8):
                t, g = i // 4, i % 4
                wait(pe, s_v1c, i - 3)
                for k in range(2):
                    last = mm(ps[4 + i % 4][:, :], work[:, 2 * g + k, t * P:(t + 1) * P],
                              tabs[:, k, 0:2, :].rearrange("p a n -> p (a n)"), start=(k == 0), stop=(k == 1))
                last.then_inc(s_v1, 1)
            for c in range(8):
                g, half = c // 2, c % 2
                if c == 0:
                    pe.wait_ge(s_v1c, 8)
                wait(pe, s_f2l, c - 1)
                for t in range(TT):
                    for part in range(2):
                        last = mm(ps[c % 2][:, 0:T], vdft[:, t, g, part * T + half * P:part * T + (half + 1) * P],
                                  tabs[:, t, 2 * part, :], start=(t + part == 0), stop=(t + part == 2))
                last.then_inc(s_f2, 1)
            pe.wait_ge(s_f2l, 8)
            for b in range(B_F, B_2):
                block_product(b)
            norm_sums(3)
            ffn(1)

            norm_sums(4)
            for b in range(B_2, B_V2):
                block_product(b, fresh=(s_hl, 3 * DJ) if b == B_2 else None)
            pe.wait_ge(s_par, LRU_IN)
            for c in range(4):
                pe.wait_ge(s_xcv, c + 1)
                wait(pe, s_sgm, 2 * (c - 1))
                mm(ps[2 + c % 2][:, 0:T], rga[:, c, :], xcv[:, c, :], start=True, stop=True)
                mm(ps[2 + c % 2][:, T:2 * T], rgx[:, c, :], xcv[:, c, :], start=True, stop=True).then_inc(s_rg1, 1)
            pe.wait_ge(s_lo, B_V2 + 1)
            pe.wait_ge(s_ev, B_V2 - 1)
            for t in range(TT):
                for j in range(DJ):
                    w = slice((B_V2 % NSPLIT) * D + j * P, (B_V2 % NSPLIT) * D + (j + 1) * P)
                    tok = slice(t * P, (t + 1) * P)
                    o = ps[B_V2 % 2][:, tok]
                    mm(o, ah3[:, j, tok], wh[:, w], start=(j == 0), stop=False)
                    mm(o, al3[:, j, tok], wh[:, w], start=False, stop=False)
                    last = mm(o, ah3[:, j, tok], wl[:, w], start=False, stop=(j == DJ - 1))
            last.then_inc(s_blk, 1)

            def win_scores(i):
                block_, heads = WIN[i]
                n = (1 + block_) * P
                kv = slice(64 * (heads[0] // 4), 64 * (heads[0] // 4) + 64)
                pe.wait_ge(s_ev, B_V2)
                wait(pe, s_ms2, i if i >= 2 else 0)
                for a, h in enumerate(heads):
                    last = mm(ps[4 + i % 2][:, a * n:(a + 1) * n], q2[kv, h % 4, block_ * P:(block_ + 1) * P], k2[kv, 0:n],
                              start=True, stop=True)
                last.then_inc(s_sc, 1)

            def win_turn(i):
                pe.wait_ge(s_dg, 2 * HEADS + i + 1)
                wait(pe, s_ptc, 2 * HEADS + i - 1)
                for k in range(4):
                    last = nc.tensor.transpose(ps[6 + i % 2][:, k * P:(k + 1) * P], p2[:, i % 2, k * P:(k + 1) * P], ident)
                last.then_inc(s_pt, 1)

            def win_pv(i):
                block_, heads = WIN[i]
                kv = slice(64 * (heads[0] // 4), 64 * (heads[0] // 4) + 64)
                pe.wait_ge(s_ptc, 2 * HEADS + i + 1)
                pe.wait_ge(s_ev, B_V2 + 1)
                pe.wait_ge(s_sgm, 8)
                wait(pe, s_at2, i - 1)
                for k in range(1 + block_):
                    src = pt2[:, i % 2, :] if block_ == 0 else \
                        pt2[:, i % 2, :].rearrange("p (h k q) -> p h k q", h=2, k=2)[:, :, k, :]
                    last = mm(ps[2 + i % 2][kv, 0:len(heads) * P], v2[:, k, kv], src, start=(k == 0), stop=(k == block_))
                last.then_inc(s_pv, 1)

            win_scores(0)
            win_scores(1)
            for i in range(len(WIN)):
                if i < 4:
                    block_product(B_XG + i)
                if i + 2 < len(WIN):
                    win_scores(i + 2)
                win_turn(i)
                if i >= 1:
                    win_pv(i - 1)
            win_pv(len(WIN) - 1)
            for half in range(2):
                for c in range(4):
                    pe.wait_ge(s_msq, 4 * half + c + 1)
                    last = mm(ps[2 + half][:, 0:T], ones, atsq[:, c, :] if half == 0 else work[:, 4 + c, T:2 * T],
                              start=(c == 0), stop=(c == 3))
                last.then_inc(s_msum, 1)
            pe.wait_ge(s_mnl, 8)
            for b in range(B_OUT2, NB):
                block_product(b)

            norm_sums(5)
            pe.wait_ge(s_ev, NB)
            pe.wait_ge(s_mod, NGRP)

            def h_turn(i):
                for k in range(4):
                    j = (i // 2) * 4 + k
                    pe.wait_ge(s_h, DJ * 5 + j + 1)
                    last = nc.tensor.transpose(ps[TOKEN_BANK[i]][:, k * P:(k + 1) * P], work[:, j, (i % 2) * P:(i % 2 + 1) * P], ident)
                last.then_inc(s_ht, 1)

            h_turn(0)
            h_turn(1)
            pe.wait_ge(s_par, EXP_IN)
            for t in range(TT):
                for j in range(DJ):
                    pe.wait_ge(s_h, DJ * 5 + j + 1)
                    last = mm(ps[4 + t][:, 0:NEXP], work[:, j, t * P:(t + 1) * P], rout[:, j, :], start=(j == 0),
                              stop=(j == DJ - 1))
                last.then_inc(s_lg, 1)
            h_turn(2)
            h_turn(3)
            pe.wait_ge(s_mask, 2)
            mm(ps[3][:, 0:NEXP], C("triu", P), mask_[:, 0, :], start=True, stop=True)
            mm(ps[3][:, 32:64], ones, mask_[:, 0, :], start=True, stop=False)
            mm(ps[3][:, 32:64], C("triu", P), mask_[:, 1, :], start=False, stop=True)
            mm(ps[3][:, 64:96], ones, mask_[:, 0, :], start=True, stop=False)
            mm(ps[3][:, 64:96], ones, mask_[:, 1, :], start=False, stop=True).then_inc(s_cum, 1)
            pe.wait_ge(s_bgl, 1)
            pe.wait_ge(s_flag, 1)

            def sum_start(k):
                if k == 2:
                    pe.wait_ge(s_route, 2)
                    for t in range(TT):
                        last = nc.tensor.transpose(ps[0][0:NEXP, t * P:(t + 1) * P], gatew[:, t, :], ident)
                    last.then_inc(s_gtt, 1)
                if k in (4, 6):
                    pe.wait_ge(s_gtc, 1)
                    if k == 6:
                        pe.wait_ge(s_oi, 2)
                    t = (k - 4) // 2
                    for n in range(2):
                        last = mm(ps[n][:, :], gT[:, t * P:(t + 1) * P], bdn[:, n * 512:(n + 1) * 512], start=True, stop=True)
                    last.then_inc(s_bd, 1)

            def experts(p_):
                if p_:
                    pe.wait_ge(m["added"], MOE["added"])

                def gather(e, half):
                    moe_wait(pe, p_, "onehot", e + 2)
                    if half == 0:
                        moe_wait(pe, p_, "at_lo", 2 * e)
                    else:
                        moe_wait(pe, p_, "xs_lo", 2 * e + 3)
                    for src, bank in ((hth, 2), (htl, 3)):
                        for k in range(4):
                            f = slice((4 * half + k) * P, (4 * half + k + 1) * P)
                            for t in range(TT):
                                last = mm(ps[bank][:, k * P:(k + 1) * P], src[:, t, f], sone[:, t, :], start=(t == 0),
                                          stop=(t == TT - 1))
                    last.then_inc(m["gathered"], 1)

                def chunk_ready(e, q):
                    d_, l_ = lo_before(q + 1)
                    if q % CH in POOL_LO:
                        moe_wait(pe, p_, "lo_pool", e * 4 + l_)
                    else:
                        moe_wait(pe, p_, "lo_dve", e * 8 + d_)

                def first_product(e, q, k):
                    chunk_ready(e, q)
                    w_h, w_l = mwh[q % MRAW], mwl[q % MRAW]
                    s = slice(k * P, (k + 1) * P)
                    for stat, mov, end in ((xsh, w_h, False), (xsh, w_l, False), (xsl, w_h, k == GU_CH - 1)):
                        for n in range(4):
                            last = mm(ps[4 + n][:, :], stat[:, s], mov[:, n * 512:(n + 1) * 512], start=False, stop=end)
                    last.then_inc(m["chunk"], 1)

                def second_product(e, q, c):
                    chunk_ready(e, q)
                    w_h, w_l = mwh[q % MRAW], mwl[q % MRAW]
                    for i in range(2):
                        k = 2 * c + i
                        s = slice(k * P, (k + 1) * P)
                        for step, (stat, mov) in enumerate(((ath, w_h), (ath, w_l), (atl, w_h))):
                            for n in range(2):
                                last = mm(ps[n][:, :], stat[:, s], mov[:, i * D + n * 512:i * D + (n + 1) * 512],
                                          start=(k == 0 and step == 0), stop=(k == 7 and step == 2))
                    last.then_inc(m["chunk"], 1)

                def combine(e, t):
                    if t == 0:
                        moe_wait(pe, p_, "stt", e - 1)
                        moe_wait(pe, p_, "y_lo", 2 * (e - 1))
                    else:
                        moe_wait(pe, p_, "added", 4 * (e - 1) - 2)
                    for n in range(2):
                        mm(ps[n][:, :], stt[:, t * P:(t + 1) * P], mh[:, n * 512:(n + 1) * 512], start=True, stop=False)
                        last = mm(ps[n][:, :], stt[:, t * P:(t + 1) * P], ml[:, n * 512:(n + 1) * 512], start=False,
                                  stop=True)
                    last.then_inc(m["combined"], 1)

                def slots(e, col):
                    moe_wait(pe, p_, "xs_lo", 2 * e + 4)
                    moe_wait(pe, p_, "onehot2", e)
                    for t in range(TT):
                        nc.tensor.transpose(ps[2][:, t * P:(t + 1) * P], stwo[:, t, :], ident)
                    for t in range(TT):
                        last = mm(ps[2][:, T:T + 1], stwo[:, t, :], gatew[:, t, col], start=(t == 0), stop=(t == TT - 1))
                    last.then_inc(m["slots"], 1)

                def body(e, gu=True, dn=True, cmb=True, first=False):
                    if gu:
                        moe_wait(pe, p_, "select", e + 1)
                        moe_wait(pe, p_, "xs_lo", 2 * e + 2)
                        moe_wait(pe, p_, "gu", e)
                        for n in range(4):
                            mm(ps[4 + n][:, :], sel[:, :], bgu[:, n * 512:(n + 1) * 512], start=True, stop=False)
                    for k in range(GU_CH):
                        if first and p_ == 0:
                            sum_start(k)
                        if gu:
                            first_product(e, k + 4 if first else k, k)
                        if cmb and k in (1, 4):
                            combine(e, 0 if k == 1 else 1)
                    if gu:
                        gather(e, 0)
                    if dn:
                        moe_wait(pe, p_, "at_lo", 2 * e)
                        if cmb:
                            moe_wait(pe, p_, "added", 4 * (e - 1))
                        shift = 0 if gu else GU_CH
                        second_product(e, 8 - shift, 0)
                        second_product(e, 9 - shift, 1)
                    if gu:
                        gather(e, 1)
                    if dn:
                        second_product(e, 10 - shift, 2)
                        if isinstance(e, int):
                            col = slice(e - 1, e)
                        else:
                            col = bass.ds(e - 1, 1)
                        if not gu:
                            moe_wait(pe, p_, "at_lo", 2 * e)
                        slots(e, col) if gu else slots_last(e, col)
                        second_product(e, 11 - shift, 3)
                    if gu:
                        moe_wait(pe, p_, "act", e + 1)
                        if dn:
                            moe_wait(pe, p_, "gcol", e)
                        else:
                            moe_wait(pe, p_, "xs_lo", 2 * e + 4)
                        for half in range(2):
                            for k in range(4):
                                f = (4 * half + k) * P
                                last = nc.tensor.transpose(ps[2 + half][:, k * P:(k + 1) * P], act_c[:, f:f + P], ident)
                            last.then_inc(m["turned"], 1)

                def slots_last(e, col):
                    moe_wait(pe, p_, "onehot2", e)
                    for t in range(TT):
                        nc.tensor.transpose(ps[2][:, t * P:(t + 1) * P], stwo[:, t, :], ident)
                    for t in range(TT):
                        last = mm(ps[2][:, T:T + 1], stwo[:, t, :], gatew[:, t, col], start=(t == 0), stop=(t == TT - 1))
                    last.then_inc(m["slots"], 1)

                if p_ == 0:
                    pe.wait_ge(s_htl, 2)
                gather(-1, 0)
                if p_ == 0:
                    pe.wait_ge(s_htl, 4)
                gather(-1, 1)
                body(0, dn=False, cmb=False, first=True)
                body(1, cmb=False)
                with pe.Fori(2, NEXP) as e:
                    body(e)
                body(NEXP, gu=False)
                combine(NEXP + 1, 0)
                combine(NEXP + 1, 1)
                pe.wait_ge(m["added"], (p_ + 1) * MOE["added"])

            experts(0)
            pe.wait_ge(s_flag, 1)
            over = pe.value_load(flag[0:1, 0:1], min_val=0, max_val=1)
            with pe.If(over > 0):
                experts(1)
            pe.end_ifs()
            for j in range(DJ):
                if j >= 4:
                    pe.wait_ge(s_x, 2 * DJ + j - 3)
                for t in range(TT):
                    last = nc.tensor.transpose(ps[4 + j % 4][:, t * P:(t + 1) * P], oacc[:, t, j * P:(j + 1) * P], ident)
                last.then_inc(s_ot, 1)
            norm_sums(6)

        @block.scalar
        def _(act):
            A = nc.scalar.activation
            chain = [0]

            def link(ins):
                chain[0] += 1
                ins.then_inc(s_act, 1)
                act.wait_ge(s_act, chain[0])

            def block_hi(b):
                act.wait_ge(s_raw[b % NRAW], 16 * (b // NRAW + 1))
                wait(act, s_blk, b - NSPLIT + 1)
                A(wh[:, (b % NSPLIT) * D:(b % NSPLIT + 1) * D], raw[:, (b % NRAW) * D:(b % NRAW + 1) * D], ACT.Copy
                  ).then_inc(s_hi, 1)

            def norm_squares(n, ready):
                for j in range(DJ):
                    ready(j)
                    A(work[:, j, 0:T], x[:, j, :], ACT.Square).then_inc(s_sq, 1)

            def norm_root(n, width=T):
                act.wait_ge(s_sum, n + 1)
                A(rt[:, 0:width], ps[3][:, 0:width], ACT.Sqrt, bias=V("eps"), scale=1.0 / D).then_inc(s_rt, 1)

            def h_hi(n, width=T):
                for j in range(DJ):
                    act.wait_ge(s_h, DJ * n + j + 1)
                    A(ah3[:, j, 0:width], work[:, j, 0:width], ACT.Copy).then_inc(s_hh, 1)

            act.wait_ge(s_vec, 16)
            A(csil[:, :], vec[:, 0:16], ACT.Sigmoid).then_inc(s_sil, 1)
            act.wait_ge(s_xin, 16)
            act.wait_ge(s_xcin, 16)
            for j in range(DJ):
                A(work[:, j, 0:T], x[:, j, :], ACT.Square)
                A(work[:, j, T:2 * T], xc[:, j * TC:(j + 1) * TC], ACT.Square).then_inc(s_sq, 1)
            norm_root(0, 2 * T)

            def ada_row(g):
                act.wait_ge(s_adp, 8 * (g + 1))
                A(arow[:, g * AG:(g + 1) * AG], psum[0:2, 4 + 2 * g:6 + 2 * g, :].rearrange("p a n -> p (a n)"), ACT.Copy
                  ).then_inc(s_arow, 1)

            ada_row(0)
            for b in range(3):
                block_hi(b)
            ada_row(1)
            h_hi(0)
            for b in range(3, 5):
                block_hi(b)
            for j in range(DJ):
                act.wait_ge(s_hx, j + 1)
                A(ah3[:, j, T:2 * T], work[:, j, T:2 * T], ACT.Copy).then_inc(s_hhx, 1)
            for b in range(5, 10):
                block_hi(b)
            for j in range(5):
                act.wait_ge(s_ev, j + 1)
                if j < 3:
                    A(sqf[:, j * T:(j + 1) * T], cq[:, j, :], ACT.Square).then_inc(s_cqs, 1)
                else:
                    A(pbuf[:, j - 3, :], ckv[:, j - 3, :], ACT.Square).then_inc(s_cqs, 1)
            for b in range(10, 13):
                block_hi(b)
            act.wait_ge(s_cqsum, 1)
            A(rt[:, 0:T], ps[3][:, 0:T], ACT.Sqrt, bias=V("eps"), scale=1.0 / QR).then_inc(s_cqrt, 1)
            act.wait_ge(s_cqsum, 2)
            act.wait_ge(s_cqn, 3)
            A(rt[:, :], ps[4][:, :], ACT.Sqrt, bias=V("eps"), scale=1.0 / KVR).then_inc(s_cqrt, 1)
            for b in range(13, B_O):
                block_hi(b)
            for c in range(CJ):
                act.wait_ge(s_cs, c + 1)
                act.wait_ge(s_blk, B_O)
                A(ah3[:, 4 + c, 0:T], work[:, 4 + c, T:2 * T], ACT.Copy).then_inc(s_csh, 1)
            for b in range(B_O, B_O + 3):
                block_hi(b)
            for u in range(12):
                act.wait_ge(s_qkc, u + 1)
                wait(act, s_qks8, u - 1)
                src = qb[0:QD, 2 * u:2 * u + 2, :].rearrange("p a t -> p (a t)") if u < 4 else kb[0:QD, u - 4, :]
                A(sqb[0:QD, u % 2, :], src, ACT.Square).then_inc(s_qksq, 1)
                if u == 5:
                    act.wait_ge(s_qks8, 4)
                    A(rstd[0:8, T:2 * T], ps[3][0:8, 0:T], ACT.Sqrt, bias=V("eps", 0, 8), scale=1.0 / QD
                      ).then_inc(s_qk8r, 1)
            act.wait_ge(s_qks8, 12)
            A(kpe[0:8, :], ps[1][0:8, :], ACT.Sqrt, bias=V("eps", 0, 8), scale=1.0 / QD).then_inc(s_qk8r, 1)
            for t in range(4):
                act.wait_ge(s_v, t + 1)
                A(vb[:, t, :], ps[4 + t][:, :], ACT.Copy).then_inc(s_vc, 1)

            def probs(i):
                act.wait_ge(s_nm, i + 1)
                wait(act, s_pt, i - 1)
                A(pbuf[:, i % 2, :], ps[4 + i % 2][:, :], ACT.Exp, bias=srow[:, i % 2, 1:2], scale=QK_SCALE,
                  accum_out=srow[:, i % 2, 2:3]).then_inc(s_pe_, 1)

            def probs_copy(i):
                act.wait_ge(s_pt, i + 1)
                h = i // 2
                wait(act, s_pv, h - 1)
                A(pt[:, h % 2, :, (i % 2) * P:(i % 2 + 1) * P], ps[6 + i % 2][:, :].rearrange("p (k t) -> p k t", k=4),
                  ACT.Copy).then_inc(s_ptc, 1)

            probs(0)
            for i in range(2 * HEADS):
                if i + 1 < 2 * HEADS:
                    probs(i + 1)
                probs_copy(i)
                if i % 4 == 3 and i >= 7:
                    attn_hi = (i - 7) // 4
                    act.wait_ge(s_pv, 2 * attn_hi + 2)
                    A(ah3[:, attn_hi, 0:T], ps[attn_hi % 2][:, 0:T], ACT.Copy).then_inc(s_ao, 1)
            act.wait_ge(s_pv, HEADS)
            A(ah3[:, 3, 0:T], ps[1][:, 0:T], ACT.Copy).then_inc(s_ao, 1)
            for b in range(B_O + 3, B_F):
                block_hi(b)

            def x_by_blocks(b):
                return lambda j: act.wait_ge(s_ev, b + j + 1)

            def x_by_ffn(k):
                return lambda j: act.wait_ge(s_x, DJ * k + j + 1)

            def ffn_hi(l, slot, loaded):
                act.wait_ge(s_fraw[slot], loaded + l * NF * 8)
                w = slice(slot * FA, (slot + 1) * FA)
                A(wh[:, w], raw[:, w], ACT.Copy).then_inc(s_fhi, 1)

            def ffn(l):
                def sigmoid(f, slot):
                    wait(act, s_fgu, f + (l * NF + 1))
                    A(sg[:, slot, :], ps[slot][:, 0:T], ACT.Sigmoid).then_inc(s_fsig, 1)

                def mul_hi(f, slot):
                    wait(act, s_fm, f + (l * NF + 1))
                    A(mh[:, slot * T:(slot + 1) * T], mm_[:, slot, :], ACT.Copy).then_inc(s_fmh, 1)

                def down_hi(f, slot, loaded):
                    act.wait_ge(s_fbraw[slot], loaded + l * NF * 8)
                    wait(act, s_fdn, f + l * NF)
                    w = slice(2 * FA + slot * D, 2 * FA + (slot + 1) * D)
                    A(wh[:, w], raw[:, w], ACT.Copy).then_inc(s_fbhi, 1)

                down_hi(0, 0, 16)
                with act.Fori(0, (NF - 2) // 4) as i:
                    f0 = act.snap(i * 4)
                    r0 = act.snap(i * 32)
                    for u in range(4):
                        sigmoid(f0 + u, u % 2)
                        ffn_hi(l, u % 2, r0 + 16 * (u // 2 + 2))
                        mul_hi(f0 + u, u % 2)
                        down_hi(f0 + (u + 1), (u + 1) % 2, r0 + 16 * ((u + 1) // 2 + 1))
                for f in (NF - 2, NF - 1):
                    sigmoid(f, f % 2)
                    mul_hi(f, f % 2)
                    if f == NF - 2:
                        down_hi(NF - 1, (NF - 1) % 2, 16 * ((NF - 1) // 2 + 1))

            norm_squares(1, x_by_blocks(B_O))
            norm_root(1)
            act.wait_ge(s_blk, B_F)
            ffn_hi(0, 0, 16)
            h_hi(1)
            ffn_hi(0, 1, 16)
            ffn(0)

            norm_squares(2, x_by_ffn(0))
            norm_root(2)
            act.wait_ge(s_fdn, 1 + NF)
            for b in range(B_F, B_F + NRAW):
                block_hi(b)
            for i in range(8):
                act.wait_ge(s_v1, i + 1)
                A(vdft[:, i // 4, i % 4, :], ps[4 + i % 4][:, :], ACT.Copy).then_inc(s_v1c, 1)
            for c in range(8):
                act.wait_ge(s_f2, c + 1)
                A(ah3[:, c, 0:T], ps[c % 2][:, 0:T], ACT.Copy).then_inc(s_f2h, 1)
                if c in (2, 4, 6):
                    block_hi(B_F + NRAW + c // 2 - 1)
            for b in range(B_F + NSPLIT, B_2):
                block_hi(b)
            norm_squares(3, x_by_blocks(B_F))
            norm_root(3)
            act.wait_ge(s_blk, B_2)
            ffn_hi(1, 0, 16)
            h_hi(3)
            ffn_hi(1, 1, 16)
            ffn(1)

            norm_squares(4, x_by_ffn(1))
            norm_root(4)
            act.wait_ge(s_fdn, 1 + 2 * NF)
            for b in range(B_2, B_2 + NRAW):
                block_hi(b)
            h_hi(4)
            for b in range(B_2 + NRAW, B_2 + NSPLIT):
                block_hi(b)
            act.wait_ge(s_lru, 1)
            A(lam[:, 1, :], lam[:, 0, :], ACT.Exp, scale=-1.0).then_inc(s_lru, 1)
            for b in range(B_2 + NSPLIT, B_OUT2):
                block_hi(b)
            for c in range(4):
                act.wait_ge(s_rg1, c + 1)
                A(work[:, c, 0:T], ps[2 + c % 2][:, 0:T], ACT.Sigmoid, bias=V("ba", c)).then_inc(s_sgm, 1)
                A(work[:, 4 + c, 0:T], ps[2 + c % 2][:, T:2 * T], ACT.Sigmoid, bias=V("bx", c)).then_inc(s_sgm, 1)
            act.wait_ge(s_lru, 3)
            for c in range(4):
                act.wait_ge(s_sgm, 8)
                A(work[:, c, T:2 * T], work[:, c, 0:T], ACT.Exp, scale=lam[:, 6, c:c + 1]).then_inc(s_ex, 1)
            for c in range(4):
                act.wait_ge(s_ex, 4)
                A(work[:, 4 + c, T:2 * T], work[:, c, 0:T], ACT.Tanh, scale=lam[:, 7, c:c + 1]).then_inc(s_th, 1)

            def win_probs(i):
                block_, heads = WIN[i]
                n = (1 + block_) * P
                act.wait_ge(s_nm, 2 * HEADS + i + 1)
                for a in range(len(heads)):
                    A(p2[:, i % 2, a * n:(a + 1) * n], p2[:, i % 2, a * n:(a + 1) * n], ACT.Exp, bias=wcol[:, i, 1, a:a + 1],
                      accum_out=wcol[:, i, 2, a:a + 1])
                A(wcol[:, i, 3, 0:len(heads)], wcol[:, i, 3, 0:len(heads)], ACT.Exp).then_inc(s_ex2, 1)

            def win_copy(i):
                act.wait_ge(s_pt, 2 * HEADS + i + 1)
                wait(act, s_pv, HEADS + i - 1)
                A(pt2[:, i % 2, :], ps[6 + i % 2][:, :], ACT.Copy).then_inc(s_ptc, 1)

            win_probs(0)
            win_probs(1)
            for i in range(len(WIN)):
                if i == 4:
                    act.wait_ge(s_th, 4)
                    for c in range(4):
                        act.wait_ge(s_gel, 1)
                        A(work[:, c, 0:T], gl[:, c, :], ACT.Tanh, scale=0.7978845608028654).then_inc(s_gelt, 1)
                if i == 5:
                    for c in range(4):
                        act.wait_ge(s_mul2, 1)
                        A(work[:, 4 + c, T:2 * T], work[:, 4 + c, T:2 * T], ACT.Sqrt).then_inc(s_sq2, 1)
                win_copy(i)
                if i + 2 < len(WIN):
                    win_probs(i + 2)
                block_hi(B_OUT2 + i)
            for half in range(2):
                for c in range(4):
                    if half == 0:
                        act.wait_ge(s_at2, len(WIN))
                        A(atsq[:, c, :], atn[:, c, :], ACT.Square).then_inc(s_msq, 1)
                    else:
                        act.wait_ge(s_lruo, c + 1)
                        A(work[:, 4 + c, T:2 * T], xcv[:, c, :], ACT.Square).then_inc(s_msq, 1)
                act.wait_ge(s_msum, half + 1)
                A(rt[:, half * T:(half + 1) * T], ps[2 + half][:, 0:T], ACT.Sqrt, bias=V("eps"), scale=1.0 / 512
                  ).then_inc(s_mrt, 1)
            for c in range(8):
                act.wait_ge(s_mn, c + 1)
                act.wait_ge(s_blk, B_OUT2)
                A(ah3[:, c, 0:T], work[:, c, 0:T], ACT.Copy).then_inc(s_mnh, 1)
            for b in range(B_OUT2 + len(WIN), NB):
                block_hi(b)

            act.wait_ge(s_par, EXP_IN)
            A(bgu[:, :], bgr[:, :], ACT.Copy).then_inc(s_bgh, 1)
            norm_squares(5, x_by_blocks(B_OUT2))
            norm_root(5)

            def token_hi(i):
                act.wait_ge(s_ht, i + 1)
                A(hth[:, i % 2, (i // 2) * 512:(i // 2 + 1) * 512], ps[TOKEN_BANK[i]][:, :], ACT.Copy).then_inc(s_hth, 1)

            def top_exp(t):
                act.wait_ge(s_tk, t + 1)
                A(rsc[:, t * 32 + 8:t * 32 + 12], rsc[:, t * 32:t * 32 + 4], ACT.Exp, bias=rsc[:, t * 32 + 16:t * 32 + 17],
                  accum_out=rsc[:, t * 32 + 17:t * 32 + 18]).then_inc(s_tke, 1)

            def experts(p_):
                if p_:
                    act.wait_ge(m["added"], MOE["added"])
                else:
                    act.wait_ge(s_blk, NB)

                def hi(e, q):
                    n_ = e * 12 + (q - 4)
                    wait(act, s_mraw[q % MRAW], e * 48 + 16 * (q // 4) + p_ * MOE_RAW)
                    moe_wait(act, p_, "chunk", n_ - 3)
                    A(mwh[q % MRAW], raw[:, (q % MRAW) * 2048:(q % MRAW + 1) * 2048], ACT.Copy).then_inc(m["hi"], 1)

                def xs_hi(e, half):
                    moe_wait(act, p_, "gathered", 2 * e + 3 + half)
                    A(xsh[:, half * 512:(half + 1) * 512], ps[2][:, :], ACT.Copy).then_inc(m["xs_hi"], 1)

                def y_hi(e):
                    moe_wait(act, p_, "chunk", MOE["chunk"] if isinstance(e, int) and e > NEXP else 12 * (e - 1) + 8)
                    moe_wait(act, p_, "gcol", e - 1)
                    for n in range(2):
                        A(mh[:, n * 512:(n + 1) * 512], ps[n][:, :], ACT.Copy, scale=gcol[:, 0:1]).then_inc(m["y_hi"], 1)

                def body(e, gu=True, dn=True, cmb=True, q0=2):
                    if cmb:
                        y_hi(e)
                    for q in range(q0, 12 if gu else 4):
                        if q == 10 and dn and gu:
                            xs_hi(e, 0)
                        if q == 10 and not dn and p_ == 0:
                            act.wait_ge(s_gtt, 1)
                            A(gT[:, :], ps[0][0:NEXP, 0:T], ACT.Copy).then_inc(s_gtc, 1)
                        hi(e, q)
                    if gu:
                        if not dn:
                            xs_hi(e, 0)
                        moe_wait(act, p_, "gate", e + 1)
                        moe_wait(act, p_, "act", e)
                        A(sig_c, gate_c, ACT.Sigmoid, scale=ALPHA).then_inc(m["sig"], 1)
                        xs_hi(e, 1)
                        hi(e, 12)
                    if dn:
                        moe_wait(act, p_, "slots", e)
                        A(stt[:, :], ps[2][:, 0:T], ACT.Copy).then_inc(m["stt"], 1)
                    if gu:
                        hi(e, 13)
                        for half in range(2):
                            moe_wait(act, p_, "turned", 2 * e + 1 + half)
                            A(ath[:, half * 512:(half + 1) * 512], ps[2 + half][:, :], ACT.Copy).then_inc(m["at_hi"], 1)

                for q in range(4, 8):
                    if p_ == 0 and q == 6:
                        token_hi(0)
                        token_hi(1)
                    hi(0, q)
                if p_ == 0:
                    token_hi(2)
                    token_hi(3)
                xs_hi(-1, 0)
                xs_hi(-1, 1)
                if p_ == 0:
                    top_exp(0)
                    top_exp(1)
                body(0, dn=False, cmb=False, q0=8)
                body(1, cmb=False)
                with act.Fori(2, NEXP) as e:
                    body(e)
                body(NEXP, gu=False)
                y_hi(NEXP + 1)

            experts(0)
            act.wait_ge(s_flag, 1)
            over = act.value_load(flag[0:1, 0:1], min_val=0, max_val=1)
            with act.If(over > 0):
                experts(1)
            act.end_ifs()
            norm_squares(6, x_by_ffn(2))
            norm_root(6)

        @block.gpsimd
        def _(pool):
            sub = lambda o, a, b: nc.gpsimd.tensor_tensor(o, a, b.bitcast(F32), ALU.subtract)

            def block_lo(b):
                pool.wait_ge(s_hi, b + 1)
                s = slice((b % NSPLIT) * D, (b % NSPLIT + 1) * D)
                sub(wl[:, s], raw[:, (b % NRAW) * D:(b % NRAW + 1) * D], wh[:, s]).then_inc(s_lo, 1)

            def ffn(l):
                def lo(f, fv):
                    wait(pool, s_fhi, f + (l * NF + 1))
                    s = slice((fv % 2) * FA, (fv % 2 + 1) * FA)
                    sub(wl[:, s], raw[:, s], wh[:, s]).then_inc(s_flo, 1)

                lo(0, 0)
                lo(1, 1)
                with pool.Fori(0, (NF - 2) // 4) as i:
                    f0 = pool.snap(i * 4)
                    for u in range(4):
                        lo(f0 + (2 + u), u)

            for b in range(B_F):
                block_lo(b)
            ffn(0)
            for b in range(B_F, B_2):
                block_lo(b)
            ffn(1)
            pool.wait_ge(s_fml, 2 * NF)
            nc.gpsimd.memset(rga[:, :, :], 0.0).then_inc(s_zero, 1)
            nc.gpsimd.memset(rgx[:, :, :], 0.0).then_inc(s_zero, 1)
            nc.gpsimd.memset(xr[:, :, 0:3], 0.0).then_inc(s_zero, 1)
            for b in range(B_2, NB):
                block_lo(b)

            def experts(p_):
                if p_:
                    pool.wait_ge(m["added"], MOE["added"])

                def lo(e, q):
                    moe_wait(pool, p_, "hi", e * 12 + (q - 3))
                    sub(mwl[q % MRAW], raw[:, (q % MRAW) * 2048:(q % MRAW + 1) * 2048], mwh[q % MRAW]
                        ).then_inc(m["lo_pool"], 1)

                for q in (4, 7, 10):
                    lo(0, q)
                with pool.Fori(1, NEXP) as e:
                    for q in POOL_LO:
                        lo(e, q)
                lo(NEXP, 1)

            experts(0)
            pool.wait_ge(s_flag, 1)
            over = pool.value_load(flag[0:1, 0:1], min_val=0, max_val=1)
            with pool.If(over > 0):
                experts(1)
            pool.end_ifs()

        @block.vector
        def _(dve):
            V_ = nc.vector
            TS, STT, TTn, COPY = V_.tensor_scalar, V_.scalar_tensor_tensor, V_.tensor_tensor, V_.tensor_copy
            chain = [0]

            def link(ins):
                chain[0] += 1
                ins.then_inc(s_dve, 1)
                dve.wait_ge(s_dve, chain[0])

            f32 = lambda a: a.bitcast(F32)

            def ada_step(dst, src, scalar, j):
                if j == 0:
                    return TS(dst, src, scalar, None, ALU.mult)
                return STT(dst, src, scalar, dst, ALU.mult, ALU.add)

            def ada(n):
                g, j = n // 8, n % 8
                dve.wait_ge(s_araw[n % 2], 16 * (n // 2 - 3))
                if j == 0:
                    dve.wait_ge(s_acol, g)
                else:
                    dve.wait_ge(s_ada, n - ADA_FIRST)
                ada_step(acc[:, :], araw[:, n % 2, :], csil[:, j:j + 1] if g < 12 else V("c2", j), j).then_inc(s_ada, 1)

            def bias(g):
                return vec[:, _V["ada_b"] + 8 * g:_V["ada_b"] + 8 * g + 8]

            def mod_ready(g):
                dve.wait_ge(s_acol, g + 1)
                cols = ps[2][:, 0:8]
                if g < 2:
                    both = ps[2][:, 0:16].rearrange("p (i a) -> p i a", a=2)
                    TTn(modx[:, 8 * g:8 * g + 8], both[:, :, 1], bias(g), ALU.add)
                    cols = both[:, :, 0]
                TTn(mod[:, 8 * g:8 * g + 8], cols, bias(g), ALU.add).then_inc(s_mod, 1)

            def m_col(g, j):
                return mod[:, 8 * g + j:8 * g + j + 1]

            def norm(n, gain, g_shift, hl=None):
                ahead = DJ if n == 0 else 1
                dve.wait_ge(s_rt, n + 1)
                link(V_.reciprocal(rstd[:, 0:T], rt[:, 0:T]))
                for j in range(ahead + DJ + 2):
                    if j < DJ:
                        TTn(work[:, j, 0:T], x[:, j, :], rstd[:, 0:T], ALU.mult).then_inc(s_nt, 1)
                    if j == ahead:
                        if n == 0:
                            link(V_.reciprocal(rstd[:, T:2 * T], rt[:, T:2 * T]))
                            for i in range(DJ):
                                TTn(work[:, i, T:2 * T], xc[:, i * TC:(i + 1) * TC], rstd[:, T:2 * T], ALU.mult
                                    ).then_inc(s_ntx, 1)
                            mod_ready(0)
                            mod_ready(1)
                        dve.wait_ge(s_mod, g_shift + 2)
                        gcols = vec[:, gain:gain + 8]
                        if n == 0:
                            STT(gsx[:, :], modx[:, 8:16], 1.0, gcols, ALU.add, ALU.mult)
                        link(STT(gs[:, :], mod[:, 8 * g_shift + 8:8 * g_shift + 16], 1.0, gcols, ALU.add, ALU.mult))
                    k = j - ahead
                    if 0 <= k < DJ:
                        dve.wait_ge(s_nt, DJ * n + k + 1)
                        TS(work[:, k, 0:T], work[:, k, 0:T], gs[:, k:k + 1], m_col(g_shift, k), ALU.mult, ALU.add
                           ).then_inc(s_h, 1)
                    if k >= 2 and hl is not None:
                        k = k - 2
                        dve.wait_ge(s_hh, DJ * hl + k + 1)
                        TTn(al3[:, k, 0:T], work[:, k, 0:T], f32(ah3[:, k, 0:T]), ALU.subtract).then_inc(s_hl, 1)

            def ctx_norm():
                for j in range(DJ + 2):
                    if j < DJ:
                        dve.wait_ge(s_ntx, j + 1)
                        TS(work[:, j, T:2 * T], work[:, j, T:2 * T], gsx[:, j:j + 1], modx[:, j:j + 1], ALU.mult, ALU.add
                           ).then_inc(s_hx, 1)
                    if j >= 2:
                        k = j - 2
                        dve.wait_ge(s_hhx, k + 1)
                        TTn(al3[:, k, T:2 * T], work[:, k, T:2 * T], f32(ah3[:, k, T:2 * T]), ALU.subtract).then_inc(s_hlx, 1)

            def residual(b, j, g):
                dve.wait_ge(s_blk, b + 1)
                STT(x[:, j, :], ps[b % 2][:, 0:T], m_col(g, j), x[:, j, :], ALU.mult, ALU.add).then_inc(s_ev, 1)

            def evacuate(b, out, rows=slice(0, P), w=T):
                dve.wait_ge(s_blk, b + 1)
                COPY(out, ps[b % 2][rows, 0:w]).then_inc(s_ev, 1)

            dve.wait_ge(s_vec, 16)
            dve.wait_ge(s_sil, 1)
            link(TTn(csil[:, :], csil[:, :], vec[:, 0:16], ALU.mult))
            dve.wait_ge(s_sq, DJ)
            V_.reduce_sum(kpe[:, :], work[:, :, :].rearrange("p j t -> p t j"), AX).then_inc(s_sqx, 1)
            norm(0, _V["n1"], 0, hl=0)
            ctx_norm()

            V_.memset(czp[:, :, 0:1], 0.0).then_inc(s_zp, 1)
            V_.memset(czp[:, :, T + 1:T + 2], 0.0).then_inc(s_zp, 1)
            for b in range(B_O):
                if b < B_KV:
                    evacuate(b, cq[:, b, :])
                elif b < B_KPE:
                    evacuate(b, ckv[:, b - B_KV, :], w=2 * T)
                elif b == B_KPE:
                    evacuate(b, kpe[NOPE:QD, :], slice(NOPE, QD), 2 * T)
                elif b < B_CC:
                    evacuate(b, cbg[:, b - B_CB, :])
                elif b < B_CU:
                    evacuate(b, ccg[:, b - B_CC, :])
                else:
                    dve.wait_ge(s_blk, b + 1)
                    TTn(czp[:, b - B_CU, 1:T + 1], ps[b % 2][:, 0:T], ccg[:, b - B_CU, :], ALU.mult).then_inc(s_ev, 1)
                if b < 8:
                    ada(ADA_FIRST + b)
                if b == B_CC - 1:
                    dve.wait_ge(s_cqrt, 1)
                    link(V_.reciprocal(rstd[:, 0:T], rt[:, 0:T]))
                    for j in range(3):
                        STT(cq[:, j, :], cq[:, j, :], V("qg", j), rstd[:, 0:T], ALU.mult, ALU.mult).then_inc(s_cqn, 1)
                    dve.wait_ge(s_cqrt, 2)
                    dve.wait_ge(s_cqn, 3)
                    link(V_.reciprocal(rstd[:, :], rt[:, :]))
                    for j in range(2):
                        STT(ckv[:, j, :], ckv[:, j, :], V("kvg", j), rstd[:, :], ALU.mult, ALU.mult).then_inc(s_cqn, 1)
            dve.wait_ge(s_ev, B_O)
            dve.wait_ge(s_zp, 2)
            for c in range(CJ):
                ins = TS(ccg[:, c, :], czp[:, c, 0:T], V("conv", c), None, ALU.mult)
            link(ins)
            for i in (1, 2):
                for c in range(CJ):
                    ins = STT(ccg[:, c, :], czp[:, c, i:i + T], V("conv", 4 * i + c), ccg[:, c, :], ALU.mult, ALU.add)
                link(ins)
            for c in range(CJ):
                TTn(work[:, 4 + c, T:2 * T], ccg[:, c, :], cbg[:, c, :], ALU.mult).then_inc(s_cs, 1)
            mod_ready(2)
            for c in range(CJ):
                dve.wait_ge(s_csh, c + 1)
                TTn(al3[:, 4 + c, 0:T], work[:, 4 + c, T:2 * T], f32(ah3[:, 4 + c, 0:T]), ALU.subtract).then_inc(s_csl, 1)

            dve.wait_ge(s_cs, CJ)
            for u in range(12):
                dve.wait_ge(s_qk, u + 1)
                if u < 4:
                    COPY(qb[0:QD, 2 * u:2 * u + 2, :], ps[4 + u][0:QD, :].rearrange("p (a t) -> p a t", a=2)
                         ).then_inc(s_qkc, 1)
                else:
                    COPY(kb[NOPE:QD, u - 4, :], kpe[NOPE:QD, :])
                    COPY(kb[0:NOPE, u - 4, :], ps[4 + u % 4][0:NOPE, :]).then_inc(s_qkc, 1)
            dve.wait_ge(s_qk8r, 1)
            V_.reciprocal(rstd[0:8, 0:T], rstd[0:8, T:2 * T]).then_inc(s_qkr8, 1)
            dve.wait_ge(s_qk8r, 2)
            V_.reciprocal(rt[0:8, :], kpe[0:8, :]).then_inc(s_qkr8, 1)

            def unit(u, rows):
                return qb[rows, 2 * u:2 * u + 2, :] if u < 4 else kb[rows, u - 4, :]

            def qk_norm(u):
                dve.wait_ge(s_qkbc, u + 1)
                spread = ps[4 + u % 4][0:QD, :]
                if u < 4:
                    spread = spread.rearrange("p (a t) -> p a t", a=2)
                un = unit(u, slice(0, QD))
                STT(un, un, V("qgain" if u < 4 else "kgain", 0, QD), spread, ALU.mult, ALU.mult).then_inc(s_qkn, 1)

            cos, sin = [con[NOPE:QD, _C[n]:_C[n] + T] for n in ("cos", "sin")]

            def rope(u):
                dve.wait_ge(s_rot, u + 1)
                wait(dve, s_qrope, u - 1)
                r = slice(NOPE, QD)
                for a in range(2 if u < 4 else 1):
                    part = qb[r, 2 * u + a, :] if u < 4 else kb[r, u - 4, 0:T]
                    t = sqb[r, a, (u % 2) * T:(u % 2 + 1) * T]
                    TTn(t, ps[4 + u % 4][r, a * T:(a + 1) * T], sin, ALU.mult)
                    link(TTn(part, part, cos, ALU.mult))
                    ins = TTn(part, part, t, ALU.add)
                ins.then_inc(s_qrope, 1)

            qk_norm(0)
            for u in range(12):
                if u + 1 < 12:
                    qk_norm(u + 1)
                rope(u)

            def row_max(i):
                dve.wait_ge(s_sc, i + 1)
                link(V_.reduce_max(srow[:, i % 2, 0:1], ps[4 + i % 2][:, :], AX))
                TS(srow[:, i % 2, 1:2], srow[:, i % 2, 0:1], -QK_SCALE, None, ALU.mult).then_inc(s_nm, 1)

            def attn_lo(c):
                dve.wait_ge(s_ao, c + 1)
                TTn(al3[:, c, 0:T], ps[c % 2][:, 0:T], f32(ah3[:, c, 0:T]), ALU.subtract).then_inc(s_aol, 1)

            row_max(0)
            for i in range(2 * HEADS):
                if i + 1 < 2 * HEADS:
                    row_max(i + 1)
                dve.wait_ge(s_pe_, i + 1)
                link(V_.reciprocal(srow[:, i % 2, 3:4], srow[:, i % 2, 2:3]))
                TS(pbuf[:, i % 2, :], pbuf[:, i % 2, :], srow[:, i % 2, 3:4], None, ALU.mult).then_inc(s_dg, 1)
                ada(24 + i)
                if i == 10:
                    mod_ready(3)
                if i in (8, 12):
                    attn_lo((i - 8) // 4)
            attn_lo(2)
            attn_lo(3)
            for j in range(DJ):
                residual(B_O + j, j, 2)
                if j == 0:
                    mod_ready(4)
                    ada(40)
                if j < DJ - 1:
                    ada(41 + j)

            def ffn(l, g_gate):
                base_n, base_g = 48 + 48 * l, 6 + 6 * l

                def mul(f, slot):
                    wait(dve, s_fsig, f + (l * NF + 1))
                    TTn(sg[:, slot, :], ps[slot][:, 0:T], sg[:, slot, :], ALU.mult).then_inc(s_ft, 1)
                    wait(dve, s_ft, f + (l * NF + 1))
                    TTn(mm_[:, slot, :], ps[slot][:, T:2 * T], sg[:, slot, :], ALU.mult).then_inc(s_fm, 1)

                def mul_lo(f, slot):
                    wait(dve, s_fmh, f + (l * NF + 1))
                    s = slice(slot * T, (slot + 1) * T)
                    TTn(ml[:, s], mm_[:, slot, :], f32(mh[:, s]), ALU.subtract).then_inc(s_fml, 1)

                def down_lo(f, slot):
                    wait(dve, s_fbhi, f + (l * NF + 1))
                    w = slice(2 * FA + slot * D, 2 * FA + (slot + 1) * D)
                    TTn(wl[:, w], raw[:, w], f32(wh[:, w]), ALU.subtract).then_inc(s_fblo, 1)

                down_lo(0, 0)
                with dve.Fori(0, (NF - 2) // 4) as i:
                    f0 = dve.snap(i * 4)
                    n0 = dve.snap(i * 8 + (base_n - ADA_FIRST))
                    loaded = dve.snap(i * 64 + 16 * (base_n // 2 - 3))
                    col = dve.snap(i * 8 + 8 * (base_g - 1))
                    cols = dve.snap(i + base_g)
                    for u in range(4):
                        mul(f0 + u, u % 2)
                        if u == 0:
                            dve.wait_ge(s_acol, cols)
                            TTn(mod[:, bass.ds(col, 8)], ps[2][:, 0:8], vec[:, bass.ds(col + _V["ada_b"], 8)], ALU.add
                                ).then_inc(s_mod, 1)
                        for j in (2 * u, 2 * u + 1):
                            dve.wait_ge(s_araw[j % 2], loaded + 16 * (j // 2))
                            if j == 0:
                                dve.wait_ge(s_acol, cols)
                            else:
                                dve.wait_ge(s_ada, n0 + j)
                            ada_step(acc[:, :], araw[:, j % 2, :], csil[:, j:j + 1] if l == 0 else V("c2", j), j
                                     ).then_inc(s_ada, 1)
                            if j % 2 == 0:
                                mul_lo(f0 + u, u % 2)
                        down_lo(f0 + (u + 1), (u + 1) % 2)
                mul(NF - 2, 0)
                mod_ready(base_g + 4)
                mul_lo(NF - 2, 0)
                down_lo(NF - 1, 1)
                for j in range(4):
                    ada(base_n + 40 + j)
                mul(NF - 1, 1)
                mul_lo(NF - 1, 1)
                for j in range(4, 8):
                    ada(base_n + 40 + j)
                if l == 1:
                    mod_ready(base_g + 5)
                dve.wait_ge(s_fdn, 1 + (l + 1) * NF)
                for j in range(DJ):
                    STT(x[:, j, :], ps[4 + j // 2][:, (j % 2) * T:(j % 2 + 1) * T], m_col(g_gate, j), x[:, j, :],
                        ALU.mult, ALU.add).then_inc(s_x, 1)

            norm(1, _V["n2"], 3, hl=1)
            ffn(0, 5)
            norm(2, _V["n1"] + 8, 6)
            for c in range(8):
                dve.wait_ge(s_f2h, c + 1)
                TTn(al3[:, c, 0:T], ps[c % 2][:, 0:T], f32(ah3[:, c, 0:T]), ALU.subtract).then_inc(s_f2l, 1)
            for j in range(DJ):
                residual(B_F + j, j, 8)
            norm(3, _V["n2"] + 8, 9, hl=2)
            ffn(1, 11)

            lam_in = vec[:, _V["lam"]:_V["lam"] + 4]
            STT(lam[:, 0, :], lam_in, -1.0, lam_in, ALU.mult, ALU.max).then_inc(s_lru, 1)
            norm(4, _V["gmix"], 12, hl=3)
            TS(nsink[:, :], vec[:, _V["sink"]:_V["sink"] + 8], -1.0, None, ALU.mult).then_inc(s_ms2, 1)
            dve.wait_ge(s_zero, 3)
            for b in range(B_2, B_XG):
                if b < B_Q2:
                    evacuate(b, xr[:, b - B_XR, 3:T + 3])
                elif b < B_K2:
                    evacuate(b, q2[:, b - B_Q2, :])
                elif b == B_K2:
                    evacuate(b, k2[:, :])
                else:
                    evacuate(b, v2[:, :, :].rearrange("p a n -> p (a n)"))
                if B_Q2 <= b < B_K2:
                    i = b - B_Q2
                    dve.wait_ge(s_ev, B_Q2)
                    for c in range(4):
                        if i == 0:
                            ins = TS(xcv[:, c, :], xr[:, c, 0:T], V("conv2", c), V("conv2b", c), ALU.mult, ALU.add)
                        else:
                            ins = STT(xcv[:, c, :], xr[:, c, i:i + T], V("conv2", 4 * i + c), xcv[:, c, :], ALU.mult, ALU.add)
                        if i == 3:
                            ins.then_inc(s_xcv, 1)
                    if i < 3:
                        link(ins)
                if b == B_K2:
                    dve.wait_ge(s_lru, 2)
                    e_, z_, zz, q_, m8 = [lam[:, k, :] for k in (1, 2, 3, 4, 5)]
                    link(TS(z_, e_, 2.0, None, ALU.add))
                    link(V_.reciprocal(z_, z_))
                    link(TTn(z_, e_, z_, ALU.mult))
                    link(TTn(zz, z_, z_, ALU.mult))
                    link(TS(q_, zz, 1.0 / 17, None, ALU.mult))
                    for k in range(7, 0, -1):
                        link(STT(q_, q_, 1.0 / (2 * k + 1), zz, ALU.add, ALU.mult))
                    link(STT(q_, q_, 1.0, z_, ALU.add, ALU.mult))
                    link(TS(m8, vec[:, _V["lam"]:_V["lam"] + 4], 0.0, 8.0, ALU.min, ALU.mult))
                    link(STT(lam[:, 6, :], q_, -16.0, m8, ALU.mult, ALU.add))
                    TS(lam[:, 7, :], lam[:, 6, :], -1.0, None, ALU.mult).then_inc(s_lru, 1)

            def win_max(i):
                block_, heads = WIN[i]
                nh, n = len(heads), (1 + block_) * P
                sl = slice(heads[0], heads[0] + nh)
                dve.wait_ge(s_sc, 2 * HEADS + i + 1)
                wait(dve, s_pt, 2 * HEADS + i - 1 if i >= 2 else 0)
                mask = con[:, _C["mask"] + 2 * P - n:_C["mask"] + 2 * P].unsqueeze(1).to_broadcast([P, nh, n])
                p_ = p2[:, i % 2, :].rearrange("p (h n) -> p h n", h=nh)
                STT(p_, ps[4 + i % 2][:, :].rearrange("p (h n) -> p h n", h=nh), Q_SCALE2, mask, ALU.mult, ALU.add
                    ).then_inc(s_ms2, 1)
                dve.wait_ge(s_ms2, i + 2)
                link(V_.reduce_max(wcol[:, i, 0, 0:nh], p_, AX))
                link(STT(wcol[:, i, 1, 0:nh], wcol[:, i, 0, 0:nh], -1.0, nsink[:, sl], ALU.mult, ALU.min))
                TTn(wcol[:, i, 3, 0:nh], wcol[:, i, 1, 0:nh], vec[:, _V["sink"] + heads[0]:_V["sink"] + heads[0] + nh], ALU.add
                    ).then_inc(s_nm, 1)

            def win_scale(i):
                block_, heads = WIN[i]
                nh, n = len(heads), (1 + block_) * P
                dve.wait_ge(s_ex2, i + 1)
                link(TTn(wcol[:, i, 2, 0:nh], wcol[:, i, 2, 0:nh], wcol[:, i, 3, 0:nh], ALU.add))
                link(V_.reciprocal(wcol[:, i, 4, 0:nh], wcol[:, i, 2, 0:nh]))
                for a in range(nh):
                    ins = TS(p2[:, i % 2, a * n:(a + 1) * n], p2[:, i % 2, a * n:(a + 1) * n], wcol[:, i, 4, a:a + 1], None, ALU.mult)
                ins.then_inc(s_dg, 1)

            def win_out(i):
                block_, heads = WIN[i]
                nh = len(heads)
                kv = slice(64 * (heads[0] // 4), 64 * (heads[0] // 4) + 64)
                dve.wait_ge(s_pv, HEADS + i + 1)
                COPY(atn[kv, heads[0] % 4:heads[0] % 4 + nh, block_ * P:(block_ + 1) * P],
                     ps[2 + i % 2][kv, 0:nh * P].rearrange("p (h q) -> p h q", h=nh)).then_inc(s_at2, 1)

            a_, th, ig = work[:, 0:4, T:2 * T], work[:, 4:8, T:2 * T], work[:, 4:8, 0:T]
            sq_ = xr[:, :, 0:T]
            win_max(0)
            win_max(1)
            for i in range(len(WIN)):
                if i < 4:
                    evacuate(B_XG + i, xg[:, i, :])
                win_scale(i)
                if i + 2 < len(WIN):
                    win_max(i + 2)
                if i == 1:
                    dve.wait_ge(s_th, 4)
                    link(TTn(sq_, a_, a_, ALU.mult))
                    link(STT(th, sq_, 1.0, th, ALU.add, ALU.mult))
                    TS(th, th, 0.0, None, ALU.max).then_inc(s_mul2, 1)
                    link(TTn(ig, ig, xcv[:, :, :], ALU.mult))
                if i == 3:
                    dve.wait_ge(s_ev, B_OUT2)
                    link(TTn(gl[:, :, :], xg[:, :, :], xg[:, :, :], ALU.mult))
                    link(TS(gl[:, :, :], gl[:, :, :], 0.044715, 1.0, ALU.mult, ALU.add))
                    TTn(gl[:, :, :], gl[:, :, :], xg[:, :, :], ALU.mult).then_inc(s_gel, 1)
                if i >= 1:
                    win_out(i - 1)
            win_out(len(WIN) - 1)
            dve.wait_ge(s_at2, len(WIN))
            dve.wait_ge(s_gelt, 4)
            link(STT(xg[:, :, :], work[:, 0:4, 0:T], 1.0, xg[:, :, :], ALU.add, ALU.mult))
            dve.wait_ge(s_sq2, 4)
            link(TTn(ig, th, ig, ALU.mult))
            for c in range(4):
                ins = V_.tensor_tensor_scan(gl[:, c, :], work[:, c, T:2 * T], work[:, 4 + c, 0:T], 0.0, ALU.mult, ALU.add)
            link(ins)
            for c in range(4):
                STT(xcv[:, c, :], gl[:, c, :], 0.5, xg[:, c, :], ALU.mult, ALU.mult).then_inc(s_lruo, 1)
            for c in range(10):
                if c in (0, 4):
                    dve.wait_ge(s_mrt, c // 4 + 1)
                    half = slice((c // 4) * T, (c // 4 + 1) * T)
                    link(V_.reciprocal(rstd[:, half], rt[:, half]))
                if c < 8:
                    src = atn[:, c, :] if c < 4 else xcv[:, c - 4, :]
                    STT(work[:, c, 0:T], src, V("gattn", c) if c < 4 else V("glru", c - 4), rstd[:, half], ALU.mult, ALU.mult
                        ).then_inc(s_mn, 1)
                if c >= 2:
                    k = c - 2
                    dve.wait_ge(s_mnh, k + 1)
                    TTn(al3[:, k, 0:T], work[:, k, 0:T], f32(ah3[:, k, 0:T]), ALU.subtract).then_inc(s_mnl, 1)
            for j in range(DJ):
                residual(B_OUT2 + j, j, 14)
                if j == 3:
                    dve.wait_ge(s_bgh, 1)
                    TTn(bgu[NEXP:2 * NEXP, :], bgr[NEXP:2 * NEXP, :], f32(bgu[NEXP:2 * NEXP, :]), ALU.subtract
                        ).then_inc(s_bgl, 1)

            norm(5, _V["gffn"], 15)
            V_.memset(pos[:, :, :], -1.0).then_inc(s_pos, 1)
            iota32 = C("iota32", NEXP)
            for t in range(TT):
                r = lambda a, n=1: rsc[:, 32 * t + a:32 * t + a + n]
                dve.wait_ge(s_lg, t + 1)
                link(TTn(logit[:, t, :], ps[4 + t][:, 0:NEXP], vec[:, _V["brout"]:_V["brout"] + NEXP], ALU.add))
                link(V_.max(r(0, 8), logit[:, t, :]))
                TS(r(16), r(0), -1.0, None, ALU.mult).then_inc(s_tk, 1)
                link(V_.max_index(ridx[:, t, :], r(0, 8), logit[:, t, :]))
                link(COPY(r(20, TOPK), ridx[:, t, 0:TOPK]))
                for k in range(TOPK):
                    if k == 0:
                        ins = TS(mask_[:, t, :], iota32, r(20), None, ALU.is_equal)
                    else:
                        ins = STT(mask_[:, t, :], iota32, r(20 + k), mask_[:, t, :], ALU.is_equal, ALU.add)
                    if k < TOPK - 1:
                        link(ins)
                ins.then_inc(s_mask, 1)

            def token_lo(i):
                dve.wait_ge(s_hth, i + 1)
                f = slice((i // 2) * 512, (i // 2 + 1) * 512)
                TTn(htl[:, i % 2, f], ps[TOKEN_BANK[i]][:, :], f32(hth[:, i % 2, f]), ALU.subtract).then_inc(s_htl, 1)

            token_lo(0)
            token_lo(1)
            dve.wait_ge(s_cum, 1)
            dve.wait_ge(s_pos, 1)
            dve.wait_ge(s_mask, 2)
            for t in range(TT):
                link(STT(pos[:, t, 0:NEXP], ps[3][:, 32 * t:32 * t + 32], 1.0, mask_[:, t, :], ALU.add, ALU.mult))
                link(TS(pos[:, t, 0:NEXP], pos[:, t, 0:NEXP], -1.0, None, ALU.add))
            V_.reduce_max(rsc[:, 31:32], ps[3][:, 64:96], AX).then_inc(s_cumr, 1)
            dve.wait_ge(s_cumr, 1)
            TS(flag[0:1, 0:1], rsc[0:1, 31:32], CAP + 0.5, None, ALU.is_gt).then_inc(s_flag, 1)

            def gates():
                for t in range(TT):
                    r = lambda a, n=1: rsc[:, 32 * t + a:32 * t + a + n]
                    dve.wait_ge(s_tke, t + 1)
                    link(V_.reciprocal(r(18), r(17)))
                    link(TS(r(24, TOPK), r(8, TOPK), r(18), None, ALU.mult))
                    for k in range(TOPK):
                        dst = gatew[:, t, :] if k == 0 else logit[:, t, :]
                        ins = TS(dst, iota32, r(20 + k), r(24 + k), ALU.is_equal, ALU.mult)
                        if k:
                            link(ins)
                            ins = TTn(gatew[:, t, :], gatew[:, t, :], logit[:, t, :], ALU.add)
                        if k < TOPK - 1:
                            link(ins)
                    ins.then_inc(s_route, 1)

            def sum_start(t):
                dve.wait_ge(s_bd, t + 1)
                for n in range(2):
                    COPY(oacc[:, t, n * 512:(n + 1) * 512], ps[n][:, :]).then_inc(s_oi, 1)

            def experts(p_):
                if p_:
                    dve.wait_ge(m["added"], MOE["added"])
                    TS(pos[:, :, :], pos[:, :, :], -float(CAP), None, ALU.add).then_inc(s_pos, 1)
                    dve.wait_ge(s_pos, p_ + 1)

                def col(e):
                    return slice(e, e + 1) if isinstance(e, int) else bass.ds(e, 1)

                def onehot(dst, e, done):
                    for t in range(TT):
                        ins = TS(dst[:, t, :], C("iota", CAP), pos[:, t, col(e)], None, ALU.is_equal)
                    ins.then_inc(done, 1)

                def select(e):
                    TS(sel[:, :], ones[0:64, :], con[0:64, _C["eye64"]:_C["eye64"] + NEXP + 1][:, col(e)], None, ALU.mult
                       ).then_inc(m["select"], 1)

                def lo(e, q):
                    if q % CH in POOL_LO:
                        return
                    moe_wait(dve, p_, "hi", e * 12 + (q - 3))
                    TTn(mwl[q % MRAW], raw[:, (q % MRAW) * 2048:(q % MRAW + 1) * 2048], f32(mwh[q % MRAW]), ALU.subtract
                        ).then_inc(m["lo_dve"], 1)

                def xs_lo(e, half):
                    moe_wait(dve, p_, "xs_hi", 2 * e + 3 + half)
                    COPY(xsl[:, half * 512:(half + 1) * 512], ps[3][:, :]).then_inc(m["xs_lo"], 1)

                def y_lo(e):
                    for n in range(2):
                        moe_wait(dve, p_, "y_hi", 2 * (e - 2) + n + 1)
                        s = slice(n * 512, (n + 1) * 512)
                        STT(ml[:, s], ps[n][:, :], gcol[:, 0:1], f32(mh[:, s]), ALU.mult, ALU.subtract
                            ).then_inc(m["y_lo"], 1)

                def add(e, t):
                    moe_wait(dve, p_, "combined", 2 * (e - 2) + t + 1)
                    for n in range(2):
                        o = oacc[:, t, n * 512:(n + 1) * 512]
                        TTn(o, ps[n][:, :], o, ALU.add).then_inc(m["added"], 1)

                def body(e, gu=True, dn=True, cmb=True, q0=0):
                    def lo_(q):
                        if q >= q0 and (gu or q < 4):
                            lo(e, q)

                    if gu:
                        moe_wait(dve, p_, "xs_lo", 2 * e + 2)
                        onehot(sone, e + 1, m["onehot"])
                    if dn:
                        onehot(stwo, e - 1, m["onehot2"])
                    if cmb:
                        y_lo(e)
                    lo_(2)
                    lo_(3)
                    if cmb:
                        add(e, 0)
                    for q in (5, 6):
                        lo_(q)
                    if cmb:
                        add(e, 1)
                    for q in (8, 9):
                        lo_(q)
                        if not dn and p_ == 0:
                            sum_start(q - 8)
                    if gu:
                        if not dn:
                            if p_ == 0:
                                dve.wait_ge(s_oi, 4)
                            lo_(11)
                        moe_wait(dve, p_, "chunk", 12 * e + 4 if dn else 8)
                        xs_lo(e, 0)
                        moe_wait(dve, p_, "turned", 2 * e)
                        TS(gate_c, ps45, LIMIT, None, ALU.min).then_inc(m["gate"], 1)
                        TS(up_c, ps67, LIMIT, -LIMIT, ALU.min, ALU.max).then_inc(m["gu"], 1)
                        select(e + 1 if not isinstance(e, int) or e < NEXP - 1 else e)
                        if dn:
                            lo_(11)
                        moe_wait(dve, p_, "sig", e + 1)
                        TTn(sig_c, gate_c, sig_c, ALU.mult).then_inc(m["glu"], 1)
                        moe_wait(dve, p_, "glu", e + 1)
                        STT(act_c, up_c, 1.0, sig_c, ALU.add, ALU.mult).then_inc(m["act"], 1)
                        xs_lo(e, 1)
                        lo(e, 12)
                    if dn:
                        moe_wait(dve, p_, "stt", e)
                        COPY(gcol[:, :], ps[2][:, T:T + 1]).then_inc(m["gcol"], 1)
                    if gu:
                        for half in range(2):
                            moe_wait(dve, p_, "at_hi", 2 * e + 1 + half)
                            s = slice(half * 512, (half + 1) * 512)
                            TTn(atl[:, s], ps[2 + half][:, :], f32(ath[:, s]), ALU.subtract).then_inc(m["at_lo"], 1)

                onehot(sone, 0, m["onehot"])
                select(0)
                if p_ == 0:
                    token_lo(2)
                    token_lo(3)
                for q in (5, 6):
                    lo(0, q)
                xs_lo(-1, 0)
                xs_lo(-1, 1)
                if p_ == 0:
                    gates()
                body(0, dn=False, cmb=False, q0=8)
                body(1, cmb=False, q0=2)
                with dve.Fori(2, NEXP) as e:
                    body(e, q0=2)
                body(NEXP, gu=False, q0=2)
                y_lo(NEXP + 1)
                add(NEXP + 1, 0)
                add(NEXP + 1, 1)

            experts(0)
            over = dve.value_load(flag[0:1, 0:1], min_val=0, max_val=1)
            with dve.If(over > 0):
                experts(1)
            dve.end_ifs()
            for j in range(DJ):
                dve.wait_ge(s_ot, j + 1)
                STT(x[:, j, :], ps[4 + j % 4][:, 0:T], m_col(17, j), x[:, j, :], ALU.mult, ALU.add).then_inc(s_x, 1)
            dve.wait_ge(s_rt, 7)
            link(V_.reciprocal(rstd[:, 0:T], rt[:, 0:T]))
            for j in range(DJ):
                STT(work[:, j, 0:T], x[:, j, :], V("gfin", j), rstd[:, 0:T], ALU.mult, ALU.mult).then_inc(s_fy, 1)


def constants():
    c = np.zeros((P, NC_), np.float32)

    def put(name, a):
        c[:a.shape[0], _C[name]:_C[name] + a.shape[1]] = a

    r = np.arange(P)
    put("ident", np.eye(P))
    put("ones", np.ones((P, P)))
    put("triu", (r[:, None] < r[None, :]) * 1.0)
    put("iota", np.broadcast_to(np.arange(P), (P, P)))
    put("iota32", np.broadcast_to(np.arange(NEXP), (P, NEXP)))
    put("head8", np.broadcast_to(np.eye(HEADS).reshape(1, 64), (P, 64)))
    put("bcast8", np.repeat(np.eye(HEADS), QD, axis=1))
    put("eye64", np.eye(NEXP, NEXP + 1)[np.arange(2 * NEXP) % NEXP])
    put("mask", np.concatenate([np.where(r[None, :] > r[:, None], 0, NEG), np.where(r[None, :] <= r[:, None], 0, NEG)], 1))
    t = np.arange(T)
    half = ROPE // 2
    inv = (1.0 / (np.float32(10000.0) ** (np.arange(0, half, 2, dtype=np.float32) / np.float32(half)))).astype(np.float32)
    rows, cols = (t // 64).astype(np.float32), (t % 64).astype(np.float32)
    ang = np.concatenate([np.tile(rows[None] * inv[:, None], (2, 1)), np.tile(cols[None] * inv[:, None], (2, 1))])
    c[NOPE:QD, _C["cos"]:_C["cos"] + T] = np.cos(ang.astype(np.float64))
    c[NOPE:QD, _C["sin"]:_C["sin"] + T] = np.sin(ang.astype(np.float64))
    rot = np.zeros((ROPE, ROPE))
    for base in (0, half):
        for i in range(half // 2):
            rot[base + half // 2 + i, base + i] = -1.0
            rot[base + i, base + half // 2 + i] = 1.0
    c[NOPE:QD, _C["rot"]:_C["rot"] + ROPE] = rot
    phase = 2 * np.pi * ((t[:, None] * t[None, :]) % T) / T
    tab = np.stack([np.cos(phase), np.sin(phase), -np.sin(phase)], 1) / np.sqrt(float(T))
    tab = np.ascontiguousarray(tab.reshape(2, P, 3, T).transpose(1, 0, 2, 3)).astype(np.float32)
    return c, tab


def kernel(**inp):
    import concourse.bacc as bacc
    from concourse.bass_utils import run_bass_kernel_spmd

    a = {k: np.asarray(v) for k, v in inp.items()}

    def cols(v):
        return np.reshape(v, (-1, P)).T

    def feature_major(v):
        return v.T.reshape(DJ, P, -1).transpose(1, 0, 2)

    def blocks(w):
        return w.reshape(DJ, P, -1, P).transpose(2, 1, 0, 3).reshape(-1, P, D)

    perm = np.arange(512).reshape(2, 4, HD).transpose(1, 0, 2).reshape(512)
    v = np.zeros((P, NV), np.float32)

    def put(name, x):
        x = np.asarray(x)
        v[:x.shape[0], _V[name]:_V[name] + x.shape[1]] = x

    put("c", cols(a["c"][0])); put("cx", cols(a["c_ctx"])); put("c2", cols(a["c_2"][0]))
    put("ada_b", np.concatenate([cols(a["ada_b"][0]), cols(a["ada_b"][1]), cols(a["b_ada_2"][0])], 1))
    put("n1", cols(a["norm1_g"])); put("n2", cols(a["norm2_g"]))
    put("gmix", cols(a["g_mix_2"][0])); put("gffn", cols(a["g_ffn_2"][0])); put("gfin", cols(a["g_final_2"]))
    put("qg", cols(a["q_norm_g"][0])); put("kvg", cols(a["kv_norm_g"][0]))
    put("qgain", a["q_gain"][0][:, None]); put("kgain", a["k_gain"][0][:, None])
    put("conv", cols(a["conv_w"][0])); put("conv2", cols(a["conv_w_2"][0])); put("conv2b", cols(a["conv_b_2"][0]))
    put("ba", cols(a["b_rg_a_2"][0])); put("bx", cols(a["b_rg_x_2"][0])); put("lam", cols(a["lru_lambda_2"][0]))
    put("gattn", cols(a["g_attn_out_2"][0][perm])); put("glru", cols(a["g_lru_out_2"][0]))
    put("sink", np.broadcast_to(a["sinks_2"][0], (P, 8)))
    put("eps", np.full((P, 1), EPS, np.float32))
    put("brout", np.broadcast_to(a["b_router_2"][0], (P, NEXP)))

    w = a["w_in"][0]
    kp = np.zeros((D, P), np.float32)
    kp[:, NOPE:QD] = w[:, QR + KVR:QR + KVR + ROPE]
    w2 = a["w_in_2"][0]
    wo2 = a["w_out_2"][0]
    blk = np.concatenate([
        blocks(w[:, 0:QR + KVR]), blocks(kp), blocks(w[:, QR + KVR + ROPE:]), blocks(a["w_o"][0]),
        blocks(a["w_fourier"][0]), blocks(w2[:, 768:1280]), blocks(w2[:, 0:512][:, perm]), blocks(w2[:, 512:640]),
        blocks(w2[:, 640:768]), blocks(w2[:, 1280:1792]), blocks(np.concatenate([wo2[0:512][perm], wo2[512:]]))])
    uq = a["w_uq"][0].reshape(3, P, HEADS * QD).transpose(1, 0, 2)
    uk = a["w_ukv"][0].reshape(2, P, HEADS, 2, NOPE).transpose(1, 0, 3, 2, 4).reshape(P, 2, 2 * HEADS * NOPE)
    ffa = np.stack([np.stack([a[n][l].reshape(DJ, P, NF, P).transpose(2, 1, 0, 3).reshape(NF, P, D)
                              for n in ("ffn_w1", "ffn_w3")], 2).reshape(NF, P, FA) for l in range(2)])
    con, tab = constants()
    arrays = {
        "xT": feature_major(a["x"][0]), "xc": feature_major(a["ctx"][0]).reshape(P, -1), "vec": v, "con": con, "tab": tab,
        "ada": np.concatenate([a["ada_w"], a["w_ada_2"]]), "blk": blk, "uq": uq, "uk": uk, "ffa": ffa,
        "ffb": a["ffn_w2"].reshape(2, NF, P, D), "rga": a["w_rg_a_2"][0], "rgx": a["w_rg_x_2"][0],
        "rout": a["w_router_2"][0].reshape(DJ, P, NEXP).transpose(1, 0, 2), "gu": a["w_gu_2"][0], "bgu": a["b_gu_2"][0],
        "dn": a["w_down_2"][0], "bdn": a["b_down_2"][0],
    }
    arrays = {k + "_dram": np.ascontiguousarray(x) for k, x in arrays.items()}
    nc = bacc.Bacc("TRN2", target_bir_lowering=False, num_devices=1)
    args = [nc.dram_tensor(k, x.shape, mybir.dt.from_np(x.dtype), kind="ExternalInput").ap() for k, x in arrays.items()]
    args.append(nc.dram_tensor("out_dram", (P, DJ, T), mybir.dt.float32, kind="ExternalOutput").ap())
    build(nc, *args)
    r = run_bass_kernel_spmd(nc, [arrays], core_ids=[0])
    out = r.results[0]["out_dram"]
    return np.ascontiguousarray(np.asarray(out).transpose(2, 1, 0).reshape(1, T, D))
```

```python
import numpy as np
import concourse.bass as bass
from concourse import mybir
from concourse.alu_op_type import AluOpType as ALU
from contextlib import ExitStack

P = 128
D = 1024
DJ = D // P
T = 256
TT = T // P
TC = 256
EPS = 1e-6
QR, KVR, ROPE, NOPE, VD, HEADS = 384, 256, 32, 64, 64, 8
QD = NOPE + ROPE
QK_SCALE = QD ** -0.5
PAIRS = HEADS // 2
PAIR_BANK = (5, 6, 7, 4)
CONV = 512
CJ = CONV // P
FF = 2816
NF = FF // P
FA = 2 * D
HD = 64
Q_SCALE2 = HD ** -0.5
NEXP, TOPK = 32, 4
CAP = 128
PASSES = T // CAP
LIMIT, ALPHA = 7.0, 1.702
NEG = -3.0e38
B_Q, B_KV, B_KPE, B_CB, B_CC, B_CU = 0, 3, 5, 6, 10, 14
B_O, B_F = 18, 26
B_XR, B_Q2, B_K2, B_V2, B_XG = 34, 38, 42, 43, 44
B_2 = B_XR
B_OUT2 = 48
NB = 56
NRAW, NSPLIT = 3, 6
WIN = [(0, (0, 1, 2, 3)), (0, (4, 5, 6, 7)), (1, (0, 1)), (1, (2, 3)), (1, (4, 5)), (1, (6, 7))]
AG = 1024
NGRP = 18
GU_CH, DN_CH = D // P, D // (2 * P)
CH = GU_CH + DN_CH
MRAW = 4
TOKEN_BANK = (0, 1, 6, 7)
POOL_LO = (1, 4, 7, 10)

_V = {}
_n = 0
for _name, _m in [("c", 8), ("cx", 8), ("c2", 8), ("ada_b", 18 * 8), ("n1", 16), ("n2", 16), ("gmix", 8), ("gffn", 8),
                  ("gfin", 8), ("qg", 3), ("kvg", 2), ("qgain", 1), ("kgain", 1), ("conv", 12), ("conv2", 16),
                  ("conv2b", 4), ("ba", 4), ("bx", 4), ("lam", 4), ("gattn", 4), ("glru", 4), ("sink", 8),
                  ("eps", 1), ("brout", 32)]:
    _V[_name] = _n
    _n += _m
NV = _n
_C = {}
_n = 0
for _name, _m in [("ident", 128), ("ones", 128), ("triu", 128), ("iota", 128), ("iota32", 32), ("pair8", 32), ("head8", 64),
                  ("bcast8", 8 * QD), ("cos", T), ("sin", T), ("rot", ROPE), ("mask", 2 * P), ("eye64", NEXP + 1)]:
    _C[_name] = _n
    _n += _m
NC_ = _n


def build(nc, xT_d, xc_d, vec_d, con_d, tab_d, ada_d, blk_d, uq_d, uk_d, ffna_d, ffnb_d, rga_d, rgx_d, rout_d,
          gu_d, bgu_d, dn_d, bdn_d, out_d):
    F32, F32R, I32 = mybir.dt.float32, mybir.dt.float32r, mybir.dt.int32
    ACT = mybir.ActivationFunctionType
    AX = mybir.AxisListType.X
    ctx = ExitStack()
    with ctx:
        def sb(name, shape, dt=F32, stack=ctx):
            return stack.enter_context(nc.sbuf_tensor(name, shape, dt))

        def sem(name):
            return ctx.enter_context(nc.semaphore(name))

        x = sb("x", [P, DJ, T])
        work = sb("work", [P, DJ, 2 * T])
        ah = sb("ah", [P, DJ * 2 * T], F32R)
        al = sb("al", [P, DJ * 2 * T], F32R)
        ah3 = ah[:, :].rearrange("p (j t) -> p j t", j=DJ)
        al3 = al[:, :].rearrange("p (j t) -> p j t", j=DJ)
        raw = sb("raw", [P, 8192])
        wh = sb("wh", [P, 6144], F32R)
        wl = sb("wl", [P, 6144], F32R)
        mh = sb("mh", [P, 1024], F32R)
        ml = sb("ml", [P, 1024], F32R)
        con = sb("con", [P, NC_])
        vec = sb("vec", [P, NV])
        mod = sb("mod", [P, NGRP * 8])
        gs = sb("gs", [P, 8])
        gsx = sb("gsx", [P, 8])
        rt = sb("rt", [P, 2 * T])
        rstd = sb("rstd", [P, 2 * T])
        csil = sb("csil", [P, 16])
        modx = sb("modx", [P, 16])
        srow = sb("srow", [P, 2, 8])
        kgone = sb("kgone", [P, 1])
        qrs = sb("qrs", [P, TT * HEADS])
        warm = sb("warm", [1, 1])
        flag = sb("flag", [1, 1], I32)

        def C(name, w, rows=P):
            return con[0:rows, _C[name]:_C[name] + w]

        def V(name, i=0, rows=P):
            return vec[0:rows, _V[name] + i:_V[name] + i + 1]

        ident, ones = C("ident", P), C("ones", P)

        def q_scale(i):
            return qrs[:, (i % 2) * HEADS + i // 2:(i % 2) * HEADS + i // 2 + 1]

        ph = ExitStack()
        acc = sb("acc", [P, AG], F32, ph)
        araw = sb("araw", [P, 2, AG], F32, ph)
        base = ExitStack()
        xc = sb("xc", [P, DJ * TC], F32, base)
        kbuf = sb("kbuf", [P, HEADS * 2 * T], F32, base)
        pbuf = sb("pbuf", [P, 2, 2 * T], F32, base)
        sqb = sb("sqb", [P, 2, 2 * T], F32, base)
        kpe = sb("kpe", [P, 2 * T], F32, base)
        base.close()
        base = ExitStack()
        sg = sb("sg", [P, 2, T], F32, base)
        mm_ = sb("mm_", [P, 2, T], F32, base)
        tabs = sb("tabs", [P, 2, 3, T], F32, base)
        vdft = sb("vdft", [P, TT, 4, 2 * T], F32, base)
        base.close()
        base = ExitStack()
        q2 = sb("q2", [P, 4, T], F32, base)
        k2 = sb("k2", [P, T], F32, base)
        v2 = sb("v2", [P, TT, P], F32, base)
        xr = sb("xr", [P, 4, T + 3], F32, base)
        xg = sb("xg", [P, 4, T], F32, base)
        xcv = sb("xcv", [P, 4, T], F32, base)
        rga = sb("rga", [P, 4, P], F32, base)
        rgx = sb("rgx", [P, 4, P], F32, base)
        atn = sb("atn", [P, 4, T], F32, base)
        p2 = sb("p2", [P, 2, 2 * T], F32, base)
        pt2 = sb("pt2", [P, 2, 2 * T], F32, base)
        wcol = sb("wcol", [P, 6, 5, 4], F32, base)
        nsink = sb("nsink", [P, 8], F32, base)
        lam = sb("lam", [P, 8, 4], F32, base)
        base.close()
        ph.close()
        mo = ExitStack()
        oacc = sb("oacc", [P, TT, D], F32, mo)
        wh4 = sb("wh4", [P, 2048], F32R, mo)
        wl4 = sb("wl4", [P, 2048], F32R, mo)
        sone = sb("sone", [P, TT, CAP], F32R, mo)
        stwo = sb("stwo", [P, TT, CAP], F32, mo)
        stt = sb("stt", [P, T], F32R, mo)
        sel = sb("sel", [64, P], F32R, mo)
        bgu = sb("bgu", [64, 2 * D], F32R, mo)
        gcol = sb("gcol", [P, 1], F32, mo)
        rout = sb("rout", [P, DJ, NEXP], F32, mo)
        logit = sb("logit", [P, TT, NEXP], F32, mo)
        gatew = sb("gatew", [P, TT, NEXP], F32, mo)
        pos = sb("pos", [P, TT, NEXP + 1], F32, mo)
        mask_ = sb("mask_", [P, TT, NEXP], F32, mo)
        rsc = sb("rsc", [P, 64], F32, mo)
        ridx = sb("ridx", [P, TT, 8], mybir.dt.uint32, mo)
        gT = sb("gT", [NEXP, T], F32, mo)
        bdn = sb("bdn", [NEXP, D], F32, mo)
        mo.close()

        psum = ctx.enter_context(nc.psum_tensor("psum", [P, 8, 512], F32))
        ps = [psum[:, i, :] for i in range(8)]
        ps45, ps67 = [psum[:, i:i + 2, :].rearrange("p a n -> p (a n)") for i in (4, 6)]

        uq = raw[:, 3072:3072 + 3 * HEADS * QD].rearrange("p (k n) -> p k n", k=3)
        uk = raw[:, 5376:5376 + 2 * D].rearrange("p (k n) -> p k n", k=2)
        ukn = uk.rearrange("p k (a h d) -> p k a h d", a=2, h=HEADS)
        qb = work[:, 0:4, :].rearrange("p a (b t) -> p (a b) t", b=2)
        vb = work[:, 4:8, :]
        cq = xc[:, 0:768].rearrange("p (j t) -> p j t", j=3)
        ckv = xc[:, 768:1792].rearrange("p (j t) -> p j t", j=2)
        pt = xc[:, :].rearrange("p (s k t) -> p s k t", s=2, k=4)
        kb = kbuf[:, :].rearrange("p (h t) -> p h t", h=HEADS)
        cbg = kbuf[:, 0:1024].rearrange("p (j t) -> p j t", j=4)
        ccg = kbuf[:, 1024:2048].rearrange("p (j t) -> p j t", j=4)
        czp = kbuf[:, 2048:2048 + 4 * (T + 2)].rearrange("p (j t) -> p j t", j=4)
        sqf = sqb[:, :, :].rearrange("p a t -> p (a t)")
        hth = ah[:, 0:2048].rearrange("p (a n) -> p a n", a=TT)
        htl = al[:, 0:2048].rearrange("p (a n) -> p a n", a=TT)
        xsh, xsl = ah[:, 2048:3072], al[:, 2048:3072]
        ath, atl = ah[:, 3072:4096], al[:, 3072:4096]
        atsq = q2
        wflat = work[:, :, :].rearrange("p j t -> p (j t)")
        gate_c, up_c, sig_c, act_c = [wflat[:, i * D:(i + 1) * D] for i in range(4)]
        mwh = [wh[:, i * 2048:(i + 1) * 2048] for i in range(3)] + [wh4[:, :]]
        mwl = [wl[:, i * 2048:(i + 1) * 2048] for i in range(3)] + [wl4[:, :]]
        afirst = [araw[:, 0, :], araw[:, 1, :], kbuf[:, 0:AG], kbuf[:, AG:2 * AG]]
        arow = kbuf[0:2, 2 * AG:4 * AG]
        bgr = oacc[0:64, :, :].rearrange("p a n -> p (a n)")
        gl = acc[:, :].rearrange("p (j t) -> p j t", j=4)

        s_con, s_vec, s_xin, s_xcin, s_out = [sem(n) for n in (
            "consts_loaded", "vectors_loaded", "x_loaded", "ctx_loaded", "out_stored")]
        s_par = sem("parameters_loaded")
        MLA_IN, DFT_IN, LRU_IN, EXP_IN = 32, 48, 48 + 256, 48 + 256 + 64
        s_raw = [sem(f"block_loaded{i}") for i in range(NRAW)]
        s_hi, s_lo, s_blk, s_ev = [sem(n) for n in ("block_hi", "block_lo", "block_product", "block_evacuated")]
        s_araw = [sem(f"ada_loaded{i}") for i in range(4)]
        s_ada, s_adp, s_arow, s_acol, s_mod = [sem(n) for n in (
            "ada_acc", "ada_product", "ada_rows", "ada_columns", "mod_ready")]
        s_sil = sem("c_sigmoid")
        s_x = sem("x_chunk")
        s_nt, s_pos = sem("norm_scaled"), sem("places_cleared")
        s_sq, s_sum, s_rt, s_h, s_hh, s_hl = [sem(n) for n in (
            "norm_squares", "norm_sums", "norm_root", "h_chunk", "h_hi", "h_lo")]
        s_sqx = sem("squares_summed")
        s_ntx, s_hx, s_hhx, s_hlx = [sem("ctx_" + n) for n in ("norm_scaled", "h_chunk", "h_hi", "h_lo")]
        s_dve, s_act = sem("dve_chain"), sem("act_chain")
        s_cqs, s_cqsum, s_cqrt, s_cqn = [sem(n) for n in ("lora_squares", "lora_sums", "lora_root", "lora_normed")]
        s_qk, s_qkc, s_qksq, s_qks8, s_qk8r, s_qkr8, s_qkbc, s_qkn, s_rot, s_qrope = [sem(n) for n in (
            "qk_product", "qk_copied", "qk_squares", "qk_sums", "qk_root", "qk_rstd", "qk_rstd_spread", "qk_normed",
            "turned", "rope_done")]
        s_psc = sem("probs_divided")
        s_v, s_vc = sem("v_product"), sem("v_copied")
        s_sc, s_nm, s_pe_, s_dg, s_pt, s_ptc, s_pv, s_ao = [sem(n) for n in (
            "scores", "row_max", "probs", "probs_scaled", "probs_turned", "probs_copied", "pv_product", "attn_hi")]
        s_aol, s_cs, s_csh, s_csl = [sem(n) for n in ("attn_lo", "conv_out", "conv_hi", "conv_lo")]
        s_fraw = [sem(f"ffn_loaded{i}") for i in range(2)]
        s_fbraw = [sem(f"ffn_down_loaded{i}") for i in range(2)]
        s_fbhi, s_fblo, s_fhi, s_flo, s_fgu, s_fsig, s_ft, s_fm, s_fmh, s_fml, s_fdn = [sem(f"ffn_{n}") for n in (
            "down_hi", "down_lo", "hi", "lo", "gate_up", "sigmoid", "gate", "mul", "mul_hi", "mul_lo", "down")]
        s_v1, s_v1c, s_f2, s_f2h, s_f2l = [sem(n) for n in (
            "dft_features", "dft_features_copied", "dft_tokens", "dft_hi", "dft_lo")]
        s_th, s_lruo = sem("lru_tanh"), sem("lru_out")
        s_zero = sem("pads_cleared")
        s_xcv, s_rg1, s_sgm, s_lru, s_ex, s_mul2, s_sq2, s_gel, s_gelt = [sem(n) for n in (
            "lru_conv", "lru_gates", "lru_sigmoids", "lru_log", "lru_exp", "lru_mult", "lru_root", "gelu_arg", "gelu_tanh")]
        s_ms2, s_ex2, s_at2 = [sem(n) for n in ("win_masked", "win_probs", "win_out")]
        s_msq, s_msum, s_mrt, s_mn, s_mnh, s_mnl = [sem(n) for n in (
            "merge_squares", "merge_sums", "merge_root", "merged", "merged_hi", "merged_lo")]
        s_lg, s_tk, s_tke, s_mask, s_cum, s_route, s_ht, s_hth, s_htl, s_flag = [sem(n) for n in (
            "logits", "top_values", "top_exp", "chosen", "slot_counts", "routed", "h_turned", "h_tok_hi", "h_tok_lo",
            "overflow_known")]
        s_cumr = sem("slot_counts_read")
        s_gtt, s_gtc, s_bd, s_oi, s_bgh, s_bgl = [sem(n) for n in (
            "gates_turned", "gates_copied", "down_bias_sum", "out_started", "gu_bias_hi", "gu_bias_lo")]
        MOE = {"hi": 12 * NEXP, "lo_dve": 8 * NEXP, "lo_pool": 4 * NEXP, "chunk": 12 * NEXP, "onehot": NEXP + 1,
               "onehot2": NEXP, "select": NEXP + 1, "gathered": 2 * NEXP + 2, "xs_hi": 2 * NEXP + 2, "xs_lo": 2 * NEXP + 2,
               "gu": NEXP, "gate": NEXP, "sig": NEXP, "glu": NEXP, "act": NEXP, "turned": 2 * NEXP, "at_hi": 2 * NEXP,
               "at_lo": 2 * NEXP, "slots": NEXP, "stt": NEXP, "gcol": NEXP, "y_hi": 2 * NEXP, "y_lo": 2 * NEXP,
               "combined": 2 * NEXP, "added": 4 * NEXP}
        m = {n: sem("moe_" + n) for n in MOE}
        s_mraw = [sem(f"moe_loaded{i}") for i in range(MRAW)]
        MOE_RAW = 16 * CH * NEXP // MRAW
        s_ot, s_fy = sem("out_turned"), sem("final_chunk")

        block = ctx.enter_context(nc.Block())

        def lo_before(q):
            n = q + 24
            pool = sum(1 for k in range(4, n) if k % CH in POOL_LO)
            return (n - 4 - pool) - 16, pool - 8

        def wait(eng, s, value):
            if not isinstance(value, int) or value > 0:
                eng.wait_ge(s, value)

        def moe_wait(eng, p_, name, value):
            if p_ or not isinstance(value, int) or value > 0:
                eng.wait_ge(m[name], value + p_ * MOE[name])

        def ada_chunk_ap(g, j):
            return ada_d[g // 6, j * P:(j + 1) * P, (g % 6) * AG:(g % 6 + 1) * AG]

        ADA_FIRST = 2 * 8

        @block.sync
        def _(sp):
            def ada(n):
                if n < ADA_FIRST:
                    if n >= 4:
                        sp.wait_ge(s_adp, n - 3)
                    sp.dma_start(afirst[n % 4], ada_chunk_ap(n // 8, n % 8)).then_inc(s_araw[n % 4], 16)
                else:
                    if n < ADA_FIRST + 2:
                        sp.wait_ge(s_adp, n - 3)
                    else:
                        sp.wait_ge(s_ada, n - 1 - ADA_FIRST)
                    sp.dma_start(araw[:, n % 2, :], ada_chunk_ap(n // 8, n % 8)).then_inc(s_araw[n % 2], 16)

            def blk(b):
                if b >= NRAW:
                    sp.wait_ge(s_hi, b - NRAW + 1)
                    sp.wait_ge(s_lo, b - NRAW + 1)
                sp.dma_start(raw[:, (b % NRAW) * D:(b % NRAW + 1) * D], blk_d[b]).then_inc(s_raw[b % NRAW], 16)

            sp.dma_start(vec[:, :], vec_d).then_inc(s_vec, 16)
            ada(0)
            sp.dma_start(x[:, :, :], xT_d).then_inc(s_xin, 16)
            ada(1)
            sp.dma_start(xc[:, :], xc_d).then_inc(s_xcin, 16)
            ada(2)
            sp.dma_start(con[:, :], con_d).then_inc(s_con, 16)
            for n in range(3, 12):
                ada(n)
            for b in range(NRAW):
                blk(b)
            for n in range(12, ADA_FIRST):
                ada(n)
            ada(ADA_FIRST)
            ada(ADA_FIRST + 1)
            for b in range(NRAW, 6):
                blk(b)
            sp.dma_start(uq, uq_d).then_inc(s_par, 16)
            sp.dma_start(uk, uk_d).then_inc(s_par, 16)
            blk(6)
            blk(7)
            for n in range(2, 8):
                ada(ADA_FIRST + n)
                blk(6 + n)
            for b in range(14, B_O + 3):
                blk(b)
            ada(24)
            ada(25)
            for b in range(B_O + NRAW, B_O + NSPLIT):
                blk(b)
            ada(26)
            ada(27)
            for b in range(B_O + NSPLIT, B_F):
                blk(b)
            for n in range(28, 48):
                ada(n)

            def ffn_a(l, slot, src):
                sp.dma_start(raw[:, slot * FA:(slot + 1) * FA], src).then_inc(s_fraw[slot], 16)

            def ffn_b(l, slot, src):
                sp.dma_start(raw[:, 2 * FA + slot * D:2 * FA + (slot + 1) * D], src).then_inc(s_fbraw[slot], 16)

            def ffn(l):
                sp.wait_ge(s_lo, B_F if l == 0 else B_2)
                if l == 0:
                    sp.wait_ge(s_v, 4)
                for f in range(2):
                    ffn_a(l, f, ffna_d[l, f])
                    ffn_b(l, f, ffnb_d[l, f])
                base_n = 48 + 48 * l
                with sp.Fori(0, (NF - 2) // 4) as i:
                    f0 = sp.snap(i * 4)
                    g0 = sp.snap(i * AG)
                    ada_done = sp.snap(i * 8 + (base_n - 1 - ADA_FIRST))
                    for u in range(4):
                        f, split = sp.snap(f0 + (2 + u)), sp.snap(f0 + (l * NF + 1 + u))
                        sp.wait_ge(s_flo, split)
                        ffn_a(l, u % 2, ffna_d[l, bass.ds(f, 1), :, :].rearrange("a p n -> p (a n)"))
                        for j in (2 * u, 2 * u + 1):
                            summed = sp.snap(ada_done + j)
                            sp.wait_ge(s_ada, summed)
                            sp.dma_start(araw[:, j % 2, :], ada_d[l + 1, j * P:(j + 1) * P, bass.ds(g0, AG)]
                                         ).then_inc(s_araw[j % 2], 16)
                        sp.wait_ge(s_fblo, split)
                        ffn_b(l, u % 2, ffnb_d[l, bass.ds(f, 1), :, :].rearrange("a p n -> p (a n)"))
                for j in range(6):
                    ada(base_n + 40 + j)
                if l == 0:
                    sp.wait_ge(s_flo, NF)
                    sp.wait_ge(s_pv, HEADS)
                    sp.dma_start(tabs[:, :, :, :], tab_d).then_inc(s_par, 16)
                else:
                    sp.wait_ge(s_flo, 2 * NF)
                    sp.wait_ge(s_fblo, 2 * NF)
                    for b in range(B_2, B_2 + NRAW):
                        blk(b)
                for j in range(6, 8):
                    ada(base_n + 40 + j)

            ffn(0)
            for b in range(B_F, B_2):
                blk(b)
            ffn(1)
            for b in range(B_2 + NRAW, B_V2):
                blk(b)
            sp.wait_ge(s_f2, 8)
            sp.wait_ge(s_fml, 2 * NF)
            sp.wait_ge(s_zero, 3)
            for c_ in range(4):
                for hb in range(2):
                    sl = slice(64 * hb, 64 * hb + 64)
                    sp.dma_start(rga[sl, c_, 64 * hb:64 * hb + 64], rga_d[2 * c_ + hb]).then_inc(s_par, 16)
                    sp.dma_start(rgx[sl, c_, 64 * hb:64 * hb + 64], rgx_d[2 * c_ + hb]).then_inc(s_par, 16)
            for b in range(B_V2, NB):
                blk(b)
            sp.wait_ge(s_mnl, 8)
            sp.dma_start(rout[:, :, :], rout_d).then_inc(s_par, 16)
            sp.dma_start(bgr[0:NEXP, :], bgu_d).then_inc(s_par, 16)
            sp.dma_start(bgr[NEXP:2 * NEXP, :], bgu_d).then_inc(s_par, 16)
            sp.dma_start(bdn[:, :], bdn_d).then_inc(s_par, 16)
            sp.wait_ge(s_lo, NB)

            def experts(p_):

                def load(q, e, static):
                    slot = raw[:, (q % MRAW) * 2048:(q % MRAW + 1) * 2048]
                    if q < GU_CH:
                        src = gu_d[e, q * P:(q + 1) * P, :] if static else \
                            gu_d[bass.ds(e, 1), q * P:(q + 1) * P, :].rearrange("a p n -> p (a n)")
                    else:
                        c_ = q - GU_CH
                        src = dn_d[e - 1] if static else dn_d[bass.ds(e - 1, 1), :, :].rearrange("a k n -> (a k) n")
                        src = src[c_ * 256:(c_ + 1) * 256, :].rearrange("(i p) n -> p i n", p=P)
                        slot = slot.rearrange("p (i n) -> p i n", i=2)
                    sp.dma_start(slot, src).then_inc(s_mraw[q % MRAW], 16)

                def chunk(e, q, e8, e4, static, kind=None):
                    d_, l_ = lo_before(q - MRAW + 1)
                    name, value = ("lo_pool", e4 + l_) if (q - MRAW) % CH in POOL_LO else ("lo_dve", e8 + d_)
                    if not static or 12 * e - 4 + q >= MRAW:
                        if not static:
                            value = sp.snap(value + p_ * MOE[name])
                            sp.wait_ge(m[name], value)
                        else:
                            moe_wait(sp, p_, name, value)
                    load(q if kind is None else kind, e, static)

                for q in range(4, 12):
                    chunk(0, q, 0, 0, True, q - 4)
                with sp.Fori(1, NEXP) as e:
                    e8, e4, ev = sp.snap(e * 8), sp.snap(e * 4), sp.snap(e + 0)
                    for q in range(CH):
                        chunk(ev, q, e8, e4, False)
                for q in range(DN_CH):
                    chunk(NEXP, q, 8 * NEXP, 4 * NEXP, True, GU_CH + q)

            experts(0)
            sp.wait_ge(s_flag, 1)
            over = sp.value_load(flag[0:1, 0:1], min_val=0, max_val=1)
            with sp.If(over > 0):
                sp.wait_ge(m["added"], MOE["added"])
                experts(1)
            sp.end_ifs()
            for j in range(DJ):
                sp.wait_ge(s_fy, j + 1)
                sp.dma_start(out_d[:, j, :], work[:, j, 0:T]).then_inc(s_out, 16)
            sp.wait_ge(s_out, 16 * DJ)

        @block.tensor
        def _(pe):
            mm = nc.tensor.matmul

            def ada_columns(g):
                pe.wait_ge(s_ada, 8 * (g - 1))
                pe.wait_ge(s_mod, g)
                for i in range(8):
                    last = mm(ps[2][:, i:i + 1], acc[:, i * P:(i + 1) * P], ones[:, 0:1], start=True, stop=True)
                last.then_inc(s_acol, 1)

            def ada_rows(g):
                both = csil[:, :].rearrange("p (a j) -> p a j", a=2)
                for j in range(8):
                    n = 8 * g + j
                    pe.wait_ge(s_araw[n % 4], 16 * (n // 4 + 1))
                    for half in range(2):
                        last = mm(ps[4 + 2 * g + half][0:2, :], both[:, :, j], afirst[n % 4][:, half * 512:(half + 1) * 512],
                                  start=(j == 0), stop=(j == 7))
                    last.then_inc(s_adp, 1)

            def row_columns(g):
                pe.wait_ge(s_arow, g + 1)
                wait(pe, s_mod, g)
                for i in range(8):
                    c0 = g * AG + i * P
                    last = mm(ps[2][:, 2 * i:2 * i + 2], arow[:, c0:c0 + P], ident[0:2, 0:2], start=True, stop=True)
                last.then_inc(s_acol, 1)

            def norm_sums(n):
                for j in range(DJ):
                    pe.wait_ge(s_sq, DJ * n + j + 1)
                    last = mm(ps[3][:, 0:T], ones, work[:, j, 0:T], start=(j == 0), stop=(j == DJ - 1))
                    if n == 1 and j == 0:
                        last.then_inc(s_fdn, 1)
                last.then_inc(s_sum, 1)

            def block_product(b, width=T, fresh=None):
                pe.wait_ge(s_lo, b + 1)
                wait(pe, s_ev, b - 1)
                w0 = (b % NSPLIT) * D
                for j in range(DJ):
                    if fresh is not None:
                        pe.wait_ge(fresh[0], fresh[1] + j + 1)
                    w = slice(w0 + j * P, w0 + (j + 1) * P)
                    o = ps[b % 2][:, 0:width]
                    mm(o, wh[:, w], ah3[:, j, 0:width], start=(j == 0), stop=False)
                    mm(o, wh[:, w], al3[:, j, 0:width], start=False, stop=False)
                    last = mm(o, wl[:, w], ah3[:, j, 0:width], start=False, stop=(j == DJ - 1))
                last.then_inc(s_blk, 1)

            pe.wait_ge(s_dve, 1)
            ada_rows(0)
            pe.wait_ge(s_con, 16)
            pe.wait_ge(s_sqx, 1)
            mm(ps[3][:, :], ones, kpe[:, :], start=True, stop=True).then_inc(s_sum, 1)
            row_columns(0)
            ada_rows(1)
            row_columns(1)
            for b in range(B_CB):
                block_product(b, T if b < B_KV else 2 * T, fresh={0: (s_hl, 0), B_KV: (s_hlx, 0)}.get(b))
            for b in range(B_CB, B_CC):
                block_product(b)
            for j in range(3):
                pe.wait_ge(s_cqs, j + 1)
                last = mm(ps[3][:, 0:T], ones, sqf[:, j * T:(j + 1) * T], start=(j == 0), stop=(j == 2))
            last.then_inc(s_cqsum, 1)
            for j in range(2):
                pe.wait_ge(s_cqs, 4 + j)
                last = mm(ps[4][:, :], ones, pbuf[:, j, :], start=(j == 0), stop=(j == 1))
            last.then_inc(s_cqsum, 1)
            rot = con[NOPE:QD, _C["rot"]:_C["rot"] + ROPE]
            for b in range(B_CC, B_O):
                block_product(b)
                if b == B_CU:
                    pe.wait_ge(s_cqn, 5)
                    pe.wait_ge(s_qkc, 1)
                    mm(ps[4][NOPE:QD, 0:T], rot, pbuf[NOPE:QD, 0, 0:T], start=True, stop=True).then_inc(s_rot, 1)
            ada_columns(2)

            pe.wait_ge(s_par, MLA_IN)

            def k_product(j):
                if PAIR_BANK[j] == 4:
                    pe.wait_ge(s_qrope, 1)
                for k in range(2):
                    last = mm(ps[PAIR_BANK[j]][:, :], uk[:, k, j * P:(j + 1) * P], ckv[:, k, :], start=(k == 0), stop=(k == 1))
                last.then_inc(s_qk, 1)

            def q_product(j):
                pe.wait_ge(s_qkc, 2 + j)
                for h in (2 * j, 2 * j + 1):
                    for k in range(3):
                        last = mm(ps[PAIR_BANK[j]][0:QD, (h % 2) * T:(h % 2 + 1) * T], uq[:, k, h * QD:(h + 1) * QD],
                                  cq[:, k, :], start=(k == 0), stop=(k == 2))
                last.then_inc(s_qk, 1)

            def qk_sums(u):
                pe.wait_ge(s_qksq, u + 1)
                if u == 0:
                    pe.wait_ge(s_ev, B_O)
                    last = mm(ps[1][0:8, :], con[NOPE:QD, _C["ones"]:_C["ones"] + 8], sqb[NOPE:QD, 0, :], start=True, stop=False)
                elif u <= PAIRS:
                    last = mm(ps[1][0:8, :], C("pair8", 32)[:, 8 * (u - 1):8 * u], sqb[:, u % 2, :], start=False,
                              stop=(u == PAIRS))
                else:
                    for h in (2 * (u - 5), 2 * (u - 5) + 1):
                        last = mm(ps[3][0:8, 0:T], C("head8", 64, QD)[:, 8 * h:8 * h + 8],
                                  sqb[0:QD, u % 2, (h % 2) * T:(h % 2 + 1) * T], start=(h == 0), stop=(h == HEADS - 1))
                last.then_inc(s_qks8, 1)

            def q_turn(j):
                pe.wait_ge(s_qkc, 6 + j)
                mm(ps[PAIR_BANK[j]][NOPE:QD, :], rot, qb[NOPE:QD, 2 * j:2 * j + 2, :].rearrange("p a t -> p (a t)"),
                   start=True, stop=True).then_inc(s_rot, 1)

            def v_product(t):
                pe.wait_ge(s_qk8r, 1)
                pe.wait_ge(s_csl, CJ)
                wait(pe, s_vc, t - 1)
                for k in range(2):
                    last = mm(ps[t % 2][:, :], ckv[:, k, t * P:(t + 1) * P], uk[:, k, 512:1024], start=(k == 0), stop=(k == 1))
                last.then_inc(s_v, 1)

            def spread(h):
                pe.wait_ge(s_qkr8, 1)
                if h < PAIRS:
                    pe.wait_ge(s_qrope, 2 + h)
                else:
                    pe.wait_ge(s_qkn, h - PAIRS + 1)
                mm(ps[PAIR_BANK[h % PAIRS]][0:QD, :], C("bcast8", 768, 8)[:, h * QD:(h + 1) * QD], rt[0:8, :],
                   start=True, stop=True).then_inc(s_qkbc, 1)

            k_product(0)
            qk_sums(0)
            k_product(1)
            k_product(2)
            qk_sums(1)
            k_product(3)
            qk_sums(2)
            q_product(0)
            qk_sums(3)
            q_product(1)
            qk_sums(4)
            for j in range(PAIRS):
                qk_sums(1 + PAIRS + j)
                q_turn(j)
                if j + 2 < PAIRS:
                    q_product(j + 2)
                else:
                    v_product(j - 2)
            v_product(2)
            spread(0)
            v_product(3)
            for h in range(1, PAIRS):
                spread(h)
            pe.wait_ge(s_qk8r, 2)
            for t in range(TT):
                last = nc.tensor.transpose(ps[3][:, T + t * HEADS:T + (t + 1) * HEADS], rstd[0:8, t * P:(t + 1) * P],
                                           con[0:8, _C["ident"]:_C["ident"] + 8])
            last.then_inc(s_rot, 1)
            for h in range(PAIRS, HEADS):
                spread(h)

            pe.wait_ge(s_qrope, 5)
            pe.wait_ge(s_qkn, HEADS)

            def scores(i):
                wait(pe, s_pe_, i - 1)
                mm(ps[4 + i % 2][:, :], qb[0:QD, i // 2, (i % 2) * P:(i % 2 + 1) * P], kb[0:QD, i // 2, :],
                   start=True, stop=True).then_inc(s_sc, 1)

            def turn(i):
                pe.wait_ge(s_psc, i + 1)
                wait(pe, s_ptc, i - 1)
                for k in range(4):
                    last = nc.tensor.transpose(ps[6 + i % 2][:, k * P:(k + 1) * P], pbuf[:, i % 2, k * P:(k + 1) * P], ident)
                last.then_inc(s_pt, 1)

            def times_v(h):
                pe.wait_ge(s_ptc, 2 * h + 2)
                pe.wait_ge(s_vc, 4)
                c = h // 2
                if h % 2 == 0:
                    wait(pe, s_aol, c - 1)
                for k in range(4):
                    last = mm(ps[c % 2][64 * (h % 2):64 * (h % 2) + 64, 0:T], vb[:, k, h * VD:(h + 1) * VD],
                              pt[:, h % 2, k, :], start=(k == 0), stop=(k == 3))
                last.then_inc(s_pv, 1)

            scores(0)
            scores(1)
            for i in range(2 * HEADS):
                if i + 2 < 2 * HEADS:
                    scores(i + 2)
                turn(i)
                if i % 2:
                    if i // 2 >= 1:
                        times_v(i // 2 - 1)
                if i == 5:
                    ada_columns(3)
            times_v(HEADS - 1)

            pe.wait_ge(s_aol, 4)
            pe.wait_ge(s_csl, 4)
            for b in range(B_O, B_F):
                block_product(b)
                if b == B_O:
                    ada_columns(4)

            def ffn(l):
                def gate_up(f, fv, fresh=None):
                    wait(pe, s_flo, f + (l * NF + 1))
                    wait(pe, s_fm, f + (l * NF - 1))
                    for half in range(2):
                        for j in range(DJ):
                            if fresh is not None:
                                pe.wait_ge(s_hl, DJ * fresh + j + 1)
                            w0 = (fv % 2) * FA + half * D + j * P
                            o = ps[fv % 2][:, half * T:(half + 1) * T]
                            mm(o, wh[:, w0:w0 + P], ah3[:, j, 0:T], start=(j == 0), stop=False)
                            mm(o, wh[:, w0:w0 + P], al3[:, j, 0:T], start=False, stop=False)
                            last = mm(o, wl[:, w0:w0 + P], ah3[:, j, 0:T], start=False, stop=(j == DJ - 1))
                    last.then_inc(s_fgu, 1)

                def down(f, fv, first=False, end=False):
                    wait(pe, s_fblo, f + (l * NF + 1))
                    wait(pe, s_fml, f + (l * NF + 1))
                    for j in range(DJ):
                        w0 = 2 * FA + (fv % 2) * D + j * P
                        o = ps[4 + j // 2][:, (j % 2) * T:(j % 2 + 1) * T]
                        a, b_ = mh[:, (fv % 2) * T:(fv % 2 + 1) * T], ml[:, (fv % 2) * T:(fv % 2 + 1) * T]
                        mm(o, wh[:, w0:w0 + P], a, start=first and j % 2 == 0, stop=False, skip_group_check=True)
                        mm(o, wh[:, w0:w0 + P], b_, start=False, stop=False, skip_group_check=True)
                        last = mm(o, wl[:, w0:w0 + P], a, start=False, stop=end, skip_group_check=True)
                    last.then_inc(s_fdn, 1)

                gate_up(0, 0, fresh=1 + l)
                gate_up(1, 1)
                down(0, 0, first=True)
                with pe.Fori(0, (NF - 2) // 4) as i:
                    f0 = pe.snap(i * 4)
                    for u in range(4):
                        gate_up(f0 + (2 + u), u)
                        if u == 2:
                            pe.wait_ge(s_ada, i * 8 + (8 * (5 + 6 * l)))
                            pe.wait_ge(s_mod, i + (6 + 6 * l))
                            for k in range(8):
                                last = mm(ps[2][:, k:k + 1], acc[:, k * P:(k + 1) * P], ones[:, 0:1], start=True, stop=True)
                            last.then_inc(s_acol, 1)
                        down(f0 + (1 + u), u + 1)
                down(NF - 1, NF - 1, end=True)

            norm_sums(1)
            ada_columns(5)
            ffn(0)

            norm_sums(2)
            pe.wait_ge(s_par, DFT_IN)
            for i in range(8):
                t, g = i // 4, i % 4
                if t == 0:
                    pe.wait_ge(s_h, DJ * 2 + 2 * g + 2)
                wait(pe, s_v1c, i - 3)
                for k in range(2):
                    last = mm(ps[4 + i % 4][:, :], work[:, 2 * g + k, t * P:(t + 1) * P],
                              tabs[:, k, 0:2, :].rearrange("p a n -> p (a n)"), start=(k == 0), stop=(k == 1))
                last.then_inc(s_v1, 1)
            for c in range(8):
                g, half = c // 2, c % 2
                if c == 0:
                    pe.wait_ge(s_v1c, 8)
                wait(pe, s_f2l, c - 1)
                for t in range(TT):
                    for part in range(2):
                        last = mm(ps[c % 2][:, 0:T], vdft[:, t, g, part * T + half * P:part * T + (half + 1) * P],
                                  tabs[:, t, 2 * part, :], start=(t + part == 0), stop=(t + part == 2))
                last.then_inc(s_f2, 1)
            ada_columns(11)
            pe.wait_ge(s_f2l, 8)
            for b in range(B_F, B_2):
                block_product(b)
            norm_sums(3)
            ffn(1)

            norm_sums(4)
            for b in range(B_2, B_V2):
                block_product(b, fresh=(s_hl, 3 * DJ) if b == B_2 else None)
                if b == B_2 + 2:
                    ada_columns(17)
            pe.wait_ge(s_par, LRU_IN)
            for c in range(4):
                pe.wait_ge(s_xcv, c + 1)
                wait(pe, s_sgm, 2 * (c - 1))
                mm(ps[2 + c % 2][:, 0:T], rga[:, c, :], xcv[:, c, :], start=True, stop=True)
                mm(ps[2 + c % 2][:, T:2 * T], rgx[:, c, :], xcv[:, c, :], start=True, stop=True).then_inc(s_rg1, 1)
            pe.wait_ge(s_lo, B_V2 + 1)
            pe.wait_ge(s_ev, B_V2 - 1)
            for t in range(TT):
                for j in range(DJ):
                    w = slice((B_V2 % NSPLIT) * D + j * P, (B_V2 % NSPLIT) * D + (j + 1) * P)
                    tok = slice(t * P, (t + 1) * P)
                    o = ps[B_V2 % 2][:, tok]
                    mm(o, ah3[:, j, tok], wh[:, w], start=(j == 0), stop=False)
                    mm(o, al3[:, j, tok], wh[:, w], start=False, stop=False)
                    last = mm(o, ah3[:, j, tok], wl[:, w], start=False, stop=(j == DJ - 1))
            last.then_inc(s_blk, 1)

            def win_scores(i):
                block_, heads = WIN[i]
                n = (1 + block_) * P
                kv = slice(64 * (heads[0] // 4), 64 * (heads[0] // 4) + 64)
                pe.wait_ge(s_ev, B_V2)
                wait(pe, s_ms2, i if i >= 2 else 0)
                for a, h in enumerate(heads):
                    last = mm(ps[4 + i % 2][:, a * n:(a + 1) * n], q2[kv, h % 4, block_ * P:(block_ + 1) * P], k2[kv, 0:n],
                              start=True, stop=True)
                last.then_inc(s_sc, 1)

            def win_turn(i):
                pe.wait_ge(s_dg, 2 * HEADS + i + 1)
                wait(pe, s_ptc, 2 * HEADS + i - 1)
                for k in range(4):
                    last = nc.tensor.transpose(ps[6 + i % 2][:, k * P:(k + 1) * P], p2[:, i % 2, k * P:(k + 1) * P], ident)
                last.then_inc(s_pt, 1)

            def win_pv(i):
                block_, heads = WIN[i]
                kv = slice(64 * (heads[0] // 4), 64 * (heads[0] // 4) + 64)
                pe.wait_ge(s_ptc, 2 * HEADS + i + 1)
                pe.wait_ge(s_ev, B_V2 + 1)
                pe.wait_ge(s_sgm, 8)
                wait(pe, s_at2, i - 1)
                for k in range(1 + block_):
                    src = pt2[:, i % 2, :] if block_ == 0 else \
                        pt2[:, i % 2, :].rearrange("p (h k q) -> p h k q", h=2, k=2)[:, :, k, :]
                    last = mm(ps[2 + i % 2][kv, 0:len(heads) * P], v2[:, k, kv], src, start=(k == 0), stop=(k == block_))
                last.then_inc(s_pv, 1)

            win_scores(0)
            win_scores(1)
            for i in range(len(WIN)):
                if i < 4:
                    block_product(B_XG + i)
                if i + 2 < len(WIN):
                    win_scores(i + 2)
                win_turn(i)
                if i >= 1:
                    win_pv(i - 1)
            win_pv(len(WIN) - 1)
            for half in range(2):
                for c in range(4):
                    pe.wait_ge(s_msq, 4 * half + c + 1)
                    last = mm(ps[2 + half][:, 0:T], ones, atsq[:, c, :] if half == 0 else work[:, 4 + c, T:2 * T],
                              start=(c == 0), stop=(c == 3))
                last.then_inc(s_msum, 1)
            pe.wait_ge(s_mnl, 8)
            for b in range(B_OUT2, NB):
                block_product(b)

            norm_sums(5)
            pe.wait_ge(s_ev, NB)
            pe.wait_ge(s_mod, NGRP)

            def h_turn(i):
                for k in range(4):
                    j = (i // 2) * 4 + k
                    pe.wait_ge(s_h, DJ * 5 + j + 1)
                    last = nc.tensor.transpose(ps[TOKEN_BANK[i]][:, k * P:(k + 1) * P], work[:, j, (i % 2) * P:(i % 2 + 1) * P], ident)
                last.then_inc(s_ht, 1)

            h_turn(0)
            h_turn(1)
            pe.wait_ge(s_par, EXP_IN)
            for t in range(TT):
                for j in range(DJ):
                    pe.wait_ge(s_h, DJ * 5 + j + 1)
                    last = mm(ps[4 + t][:, 0:NEXP], work[:, j, t * P:(t + 1) * P], rout[:, j, :], start=(j == 0),
                              stop=(j == DJ - 1))
                last.then_inc(s_lg, 1)
            h_turn(2)
            h_turn(3)
            pe.wait_ge(s_mask, 2)
            mm(ps[3][:, 0:NEXP], C("triu", P), mask_[:, 0, :], start=True, stop=True)
            mm(ps[3][:, 32:64], ones, mask_[:, 0, :], start=True, stop=False)
            mm(ps[3][:, 32:64], C("triu", P), mask_[:, 1, :], start=False, stop=True)
            mm(ps[3][:, 64:96], ones, mask_[:, 0, :], start=True, stop=False)
            mm(ps[3][:, 64:96], ones, mask_[:, 1, :], start=False, stop=True).then_inc(s_cum, 1)
            pe.wait_ge(s_bgl, 1)
            pe.wait_ge(s_flag, 1)

            def sum_start(k):
                if k == 2:
                    pe.wait_ge(s_route, 2)
                    for t in range(TT):
                        last = nc.tensor.transpose(ps[0][0:NEXP, t * P:(t + 1) * P], gatew[:, t, :], ident)
                    last.then_inc(s_gtt, 1)
                if k in (4, 6):
                    pe.wait_ge(s_gtc, 1)
                    if k == 6:
                        pe.wait_ge(s_oi, 2)
                    t = (k - 4) // 2
                    for n in range(2):
                        last = mm(ps[n][:, :], gT[:, t * P:(t + 1) * P], bdn[:, n * 512:(n + 1) * 512], start=True, stop=True)
                    last.then_inc(s_bd, 1)

            def experts(p_):
                if p_:
                    pe.wait_ge(m["added"], MOE["added"])

                def gather(e, half):
                    moe_wait(pe, p_, "onehot", e + 2)
                    if half == 0:
                        moe_wait(pe, p_, "at_lo", 2 * e)
                    else:
                        moe_wait(pe, p_, "xs_lo", 2 * e + 3)
                    for src, bank in ((hth, 2), (htl, 3)):
                        for k in range(4):
                            f = slice((4 * half + k) * P, (4 * half + k + 1) * P)
                            for t in range(TT):
                                last = mm(ps[bank][:, k * P:(k + 1) * P], src[:, t, f], sone[:, t, :], start=(t == 0),
                                          stop=(t == TT - 1))
                    last.then_inc(m["gathered"], 1)

                def chunk_ready(e, q):
                    d_, l_ = lo_before(q + 1)
                    if q % CH in POOL_LO:
                        moe_wait(pe, p_, "lo_pool", e * 4 + l_)
                    else:
                        moe_wait(pe, p_, "lo_dve", e * 8 + d_)

                def first_product(e, q, k):
                    chunk_ready(e, q)
                    w_h, w_l = mwh[q % MRAW], mwl[q % MRAW]
                    s = slice(k * P, (k + 1) * P)
                    for stat, mov, end in ((xsh, w_h, False), (xsh, w_l, False), (xsl, w_h, k == GU_CH - 1)):
                        for n in range(4):
                            last = mm(ps[4 + n][:, :], stat[:, s], mov[:, n * 512:(n + 1) * 512], start=False, stop=end)
                    last.then_inc(m["chunk"], 1)

                def second_product(e, q, c):
                    chunk_ready(e, q)
                    w_h, w_l = mwh[q % MRAW], mwl[q % MRAW]
                    for i in range(2):
                        k = 2 * c + i
                        s = slice(k * P, (k + 1) * P)
                        for step, (stat, mov) in enumerate(((ath, w_h), (ath, w_l), (atl, w_h))):
                            for n in range(2):
                                last = mm(ps[n][:, :], stat[:, s], mov[:, i * D + n * 512:i * D + (n + 1) * 512],
                                          start=(k == 0 and step == 0), stop=(k == 7 and step == 2))
                    last.then_inc(m["chunk"], 1)

                def combine(e, t):
                    if t == 0:
                        moe_wait(pe, p_, "stt", e - 1)
                        moe_wait(pe, p_, "y_lo", 2 * (e - 1))
                    else:
                        moe_wait(pe, p_, "added", 4 * (e - 1) - 2)
                    for n in range(2):
                        mm(ps[n][:, :], stt[:, t * P:(t + 1) * P], mh[:, n * 512:(n + 1) * 512], start=True, stop=False)
                        last = mm(ps[n][:, :], stt[:, t * P:(t + 1) * P], ml[:, n * 512:(n + 1) * 512], start=False,
                                  stop=True)
                    last.then_inc(m["combined"], 1)

                def slots(e, col):
                    moe_wait(pe, p_, "xs_lo", 2 * e + 4)
                    moe_wait(pe, p_, "onehot2", e)
                    for t in range(TT):
                        nc.tensor.transpose(ps[2][:, t * P:(t + 1) * P], stwo[:, t, :], ident)
                    for t in range(TT):
                        last = mm(ps[2][:, T:T + 1], stwo[:, t, :], gatew[:, t, col], start=(t == 0), stop=(t == TT - 1))
                    last.then_inc(m["slots"], 1)

                def body(e, gu=True, dn=True, cmb=True, first=False):
                    if gu:
                        moe_wait(pe, p_, "select", e + 1)
                        moe_wait(pe, p_, "xs_lo", 2 * e + 2)
                        moe_wait(pe, p_, "gu", e)
                        for n in range(4):
                            mm(ps[4 + n][:, :], sel[:, :], bgu[:, n * 512:(n + 1) * 512], start=True, stop=False)
                    for k in range(GU_CH):
                        if first and p_ == 0:
                            sum_start(k)
                        if gu:
                            first_product(e, k + 4 if first else k, k)
                        if cmb and k in (1, 4):
                            combine(e, 0 if k == 1 else 1)
                    if gu:
                        gather(e, 0)
                    if dn:
                        moe_wait(pe, p_, "at_lo", 2 * e)
                        if cmb:
                            moe_wait(pe, p_, "added", 4 * (e - 1))
                        shift = 0 if gu else GU_CH
                        second_product(e, 8 - shift, 0)
                        second_product(e, 9 - shift, 1)
                    if gu:
                        gather(e, 1)
                    if dn:
                        second_product(e, 10 - shift, 2)
                        if isinstance(e, int):
                            col = slice(e - 1, e)
                        else:
                            col = bass.ds(e - 1, 1)
                        if not gu:
                            moe_wait(pe, p_, "at_lo", 2 * e)
                        slots(e, col) if gu else slots_last(e, col)
                        second_product(e, 11 - shift, 3)
                    if gu:
                        moe_wait(pe, p_, "act", e + 1)
                        if dn:
                            moe_wait(pe, p_, "gcol", e)
                        else:
                            moe_wait(pe, p_, "xs_lo", 2 * e + 4)
                        for half in range(2):
                            for k in range(4):
                                f = (4 * half + k) * P
                                last = nc.tensor.transpose(ps[2 + half][:, k * P:(k + 1) * P], act_c[:, f:f + P], ident)
                            last.then_inc(m["turned"], 1)

                def slots_last(e, col):
                    moe_wait(pe, p_, "onehot2", e)
                    for t in range(TT):
                        nc.tensor.transpose(ps[2][:, t * P:(t + 1) * P], stwo[:, t, :], ident)
                    for t in range(TT):
                        last = mm(ps[2][:, T:T + 1], stwo[:, t, :], gatew[:, t, col], start=(t == 0), stop=(t == TT - 1))
                    last.then_inc(m["slots"], 1)

                if p_ == 0:
                    pe.wait_ge(s_htl, 2)
                gather(-1, 0)
                if p_ == 0:
                    pe.wait_ge(s_htl, 4)
                gather(-1, 1)
                body(0, dn=False, cmb=False, first=True)
                body(1, cmb=False)
                with pe.Fori(2, NEXP) as e:
                    body(e)
                body(NEXP, gu=False)
                combine(NEXP + 1, 0)
                combine(NEXP + 1, 1)
                pe.wait_ge(m["added"], (p_ + 1) * MOE["added"])

            experts(0)
            pe.wait_ge(s_flag, 1)
            over = pe.value_load(flag[0:1, 0:1], min_val=0, max_val=1)
            with pe.If(over > 0):
                experts(1)
            pe.end_ifs()
            for j in range(DJ):
                if j >= 4:
                    pe.wait_ge(s_x, 2 * DJ + j - 3)
                for t in range(TT):
                    last = nc.tensor.transpose(ps[4 + j % 4][:, t * P:(t + 1) * P], oacc[:, t, j * P:(j + 1) * P], ident)
                last.then_inc(s_ot, 1)
            norm_sums(6)

        @block.scalar
        def _(act):
            A = nc.scalar.activation
            chain = [0]

            def link(ins):
                chain[0] += 1
                ins.then_inc(s_act, 1)
                act.wait_ge(s_act, chain[0])

            def block_hi(b):
                act.wait_ge(s_raw[b % NRAW], 16 * (b // NRAW + 1))
                wait(act, s_blk, b - NSPLIT + 1)
                A(wh[:, (b % NSPLIT) * D:(b % NSPLIT + 1) * D], raw[:, (b % NRAW) * D:(b % NRAW + 1) * D], ACT.Copy
                  ).then_inc(s_hi, 1)

            def load_table(function):
                A(warm[:, :], V("eps", 0, 1), function)

            def norm_squares(n, ready):
                for j in range(DJ):
                    ready(j)
                    A(work[:, j, 0:T], x[:, j, :], ACT.Square).then_inc(s_sq, 1)
                    if n == 3 and j == 5:
                        ffn_hi(1, 0, 16)

            def norm_root(n, width=T):
                act.wait_ge(s_sum, n + 1)
                A(rt[:, 0:width], ps[3][:, 0:width], ACT.Sqrt, bias=V("eps"), scale=1.0 / D).then_inc(s_rt, 1)

            def h_hi(n, g_shift=None):
                for j in range(DJ):
                    act.wait_ge(s_h, DJ * n + j + 1)
                    if g_shift is None:
                        A(ah3[:, j, 0:T], work[:, j, 0:T], ACT.Copy).then_inc(s_hh, 1)
                    else:
                        A(ah3[:, j, 0:T], work[:, j, 0:T], ACT.Identity, bias=mod[:, 8 * g_shift + j:8 * g_shift + j + 1]
                          ).then_inc(s_hh, 1)

            act.wait_ge(s_vec, 16)
            A(csil[:, :], vec[:, 0:16], ACT.Sigmoid).then_inc(s_sil, 1)
            act.wait_ge(s_xin, 16)
            act.wait_ge(s_xcin, 16)
            for j in range(DJ):
                A(work[:, j, 0:T], x[:, j, :], ACT.Square)
                A(work[:, j, T:2 * T], xc[:, j * TC:(j + 1) * TC], ACT.Square).then_inc(s_sq, 1)
            norm_root(0, 2 * T)

            def ada_row(g):
                act.wait_ge(s_adp, 8 * (g + 1))
                A(arow[:, g * AG:(g + 1) * AG], psum[0:2, 4 + 2 * g:6 + 2 * g, :].rearrange("p a n -> p (a n)"), ACT.Copy
                  ).then_inc(s_arow, 1)

            ada_row(0)
            for b in range(3):
                block_hi(b)
            ada_row(1)
            h_hi(0)
            for b in range(3, 5):
                block_hi(b)
            for j in range(DJ):
                act.wait_ge(s_hx, j + 1)
                A(ah3[:, j, T:2 * T], work[:, j, T:2 * T], ACT.Copy).then_inc(s_hhx, 1)
            for b in range(5, 10):
                block_hi(b)
            for j in range(5):
                act.wait_ge(s_ev, j + 1)
                if j < 3:
                    A(sqf[:, j * T:(j + 1) * T], cq[:, j, :], ACT.Square).then_inc(s_cqs, 1)
                else:
                    A(pbuf[:, j - 3, :], ckv[:, j - 3, :], ACT.Square).then_inc(s_cqs, 1)
            for b in range(10, 13):
                block_hi(b)
            act.wait_ge(s_cqsum, 1)
            A(rt[:, 0:T], ps[3][:, 0:T], ACT.Sqrt, bias=V("eps"), scale=1.0 / QR).then_inc(s_cqrt, 1)
            act.wait_ge(s_cqsum, 2)
            act.wait_ge(s_cqn, 3)
            A(rt[:, :], ps[4][:, :], ACT.Sqrt, bias=V("eps"), scale=1.0 / KVR).then_inc(s_cqrt, 1)
            for b in range(13, B_O):
                block_hi(b)
            A(sqb[NOPE:QD, 0, :], kpe[NOPE:QD, :], ACT.Square).then_inc(s_qksq, 1)
            def pair_squares(u):
                act.wait_ge(s_qk, u)
                wait(act, s_qks8, u - 1)
                rows = slice(0, P if u <= PAIRS else QD)
                A(sqb[rows, u % 2, :], ps[PAIR_BANK[(u - 1) % PAIRS]][rows, :], ACT.Square).then_inc(s_qksq, 1)

            def v_copy(t):
                act.wait_ge(s_v, t + 1)
                A(vb[:, t, :], ps[t % 2][:, :], ACT.Copy).then_inc(s_vc, 1)

            for u in range(1, 2 * PAIRS + 1):
                pair_squares(u)
                if u == 2:
                    for c in range(CJ):
                        act.wait_ge(s_cs, c + 1)
                        act.wait_ge(s_blk, B_O)
                        A(ah3[:, 4 + c, 0:T], work[:, 4 + c, T:2 * T], ACT.Copy).then_inc(s_csh, 1)
                if u in (3, 4, 5):
                    block_hi(B_O + u - 3)
                if u == PAIRS + 1:
                    act.wait_ge(s_qks8, 1 + PAIRS)
                    A(kpe[0:8, :], ps[1][0:8, :], ACT.Sqrt, bias=V("eps", 0, 8), scale=1.0 / QD).then_inc(s_qk8r, 1)
                if u > PAIRS:
                    act.wait_ge(s_qrope, 1)
                    for h in (2 * (u - 5), 2 * (u - 5) + 1):
                        A(kb[NOPE:QD, h, :], pbuf[NOPE:QD, 0, :], ACT.Copy)
            act.wait_ge(s_qks8, 1 + 2 * PAIRS)
            act.wait_ge(s_cqn, 3)
            A(rstd[0:8, 0:T], ps[3][0:8, 0:T], ACT.Sqrt, bias=V("eps", 0, 8), scale=1.0 / QD).then_inc(s_qk8r, 1)
            for t in range(4):
                v_copy(t)
            for b in range(B_O + NRAW, B_O + NSPLIT):
                block_hi(b)

            def probs(i):
                act.wait_ge(s_nm, i + 1)
                wait(act, s_pt, i - 1)
                A(pbuf[:, i % 2, :], ps[4 + i % 2][:, :], ACT.Exp, bias=srow[:, i % 2, 1:2], scale=q_scale(i),
                  accum_out=srow[:, i % 2, 2:3]).then_inc(s_pe_, 1)

            def probs_copy(i):
                act.wait_ge(s_pt, i + 1)
                h = i // 2
                wait(act, s_pv, h - 1)
                A(pt[:, h % 2, :, (i % 2) * P:(i % 2 + 1) * P], ps[6 + i % 2][:, :].rearrange("p (k t) -> p k t", k=4),
                  ACT.Copy).then_inc(s_ptc, 1)

            def probs_divide(i):
                act.wait_ge(s_dg, i + 1)
                A(pbuf[:, i % 2, :], pbuf[:, i % 2, :], ACT.Copy, scale=srow[:, i % 2, 3:4]).then_inc(s_psc, 1)

            probs(0)
            for i in range(2 * HEADS):
                probs_divide(i)
                if i + 1 < 2 * HEADS:
                    probs(i + 1)
                probs_copy(i)
                if i % 4 == 3 and i >= 7:
                    attn_hi = (i - 7) // 4
                    act.wait_ge(s_pv, 2 * attn_hi + 2)
                    A(ah3[:, attn_hi, 0:T], ps[attn_hi % 2][:, 0:T], ACT.Copy).then_inc(s_ao, 1)
            act.wait_ge(s_pv, HEADS)
            A(ah3[:, 3, 0:T], ps[1][:, 0:T], ACT.Copy).then_inc(s_ao, 1)
            for b in range(B_O + NSPLIT, B_F):
                block_hi(b)

            def x_by_blocks(b):
                return lambda j: act.wait_ge(s_ev, b + j + 1)

            def x_by_ffn(k):
                return lambda j: act.wait_ge(s_x, DJ * k + j + 1)

            def ffn_hi(l, slot, loaded):
                act.wait_ge(s_fraw[slot], loaded + l * NF * 8)
                w = slice(slot * FA, (slot + 1) * FA)
                A(wh[:, w], raw[:, w], ACT.Copy).then_inc(s_fhi, 1)

            def ffn(l):
                def sigmoid(f, slot):
                    wait(act, s_fgu, f + (l * NF + 1))
                    A(sg[:, slot, :], ps[slot][:, 0:T], ACT.Sigmoid).then_inc(s_fsig, 1)

                def mul_hi(f, slot):
                    wait(act, s_fm, f + (l * NF + 1))
                    A(mh[:, slot * T:(slot + 1) * T], mm_[:, slot, :], ACT.Copy).then_inc(s_fmh, 1)

                def down_hi(f, slot, loaded):
                    act.wait_ge(s_fbraw[slot], loaded + l * NF * 8)
                    wait(act, s_fdn, f + l * NF)
                    w = slice(2 * FA + slot * D, 2 * FA + (slot + 1) * D)
                    A(wh[:, w], raw[:, w], ACT.Copy).then_inc(s_fbhi, 1)

                down_hi(0, 0, 16)
                with act.Fori(0, (NF - 2) // 4) as i:
                    f0 = act.snap(i * 4)
                    r0 = act.snap(i * 32)
                    for u in range(4):
                        sigmoid(f0 + u, u % 2)
                        ffn_hi(l, u % 2, r0 + 16 * (u // 2 + 2))
                        mul_hi(f0 + u, u % 2)
                        down_hi(f0 + (u + 1), (u + 1) % 2, r0 + 16 * ((u + 1) // 2 + 1))
                for f in (NF - 2, NF - 1):
                    sigmoid(f, f % 2)
                    mul_hi(f, f % 2)
                    if f == NF - 2:
                        down_hi(NF - 1, (NF - 1) % 2, 16 * ((NF - 1) // 2 + 1))

            norm_squares(1, x_by_blocks(B_O))
            norm_root(1)
            act.wait_ge(s_blk, B_F)
            ffn_hi(0, 0, 16)
            h_hi(1, 3)
            ffn_hi(0, 1, 16)
            ffn(0)

            load_table(ACT.Sqrt)
            norm_squares(2, x_by_ffn(0))
            norm_root(2)
            act.wait_ge(s_fdn, 1 + NF)
            for b in range(B_F, B_F + NRAW):
                block_hi(b)
            for i in range(8):
                act.wait_ge(s_v1, i + 1)
                A(vdft[:, i // 4, i % 4, :], ps[4 + i % 4][:, :], ACT.Copy).then_inc(s_v1c, 1)
            for c in range(8):
                act.wait_ge(s_f2, c + 1)
                A(ah3[:, c, 0:T], ps[c % 2][:, 0:T], ACT.Copy).then_inc(s_f2h, 1)
                if c in (2, 4, 6):
                    block_hi(B_F + NRAW + c // 2 - 1)
            for b in range(B_F + NSPLIT, B_2):
                block_hi(b)
            norm_squares(3, x_by_blocks(B_F))
            norm_root(3)
            act.wait_ge(s_blk, B_2)
            h_hi(3, 9)
            ffn_hi(1, 1, 16)
            ffn(1)

            load_table(ACT.Sqrt)
            norm_squares(4, x_by_ffn(1))
            act.wait_ge(s_fdn, 1 + 2 * NF)
            block_hi(B_2)
            norm_root(4)
            for b in range(B_2 + 1, B_2 + NRAW):
                block_hi(b)
            h_hi(4, 12)
            for b in range(B_2 + NRAW, B_2 + NSPLIT):
                block_hi(b)
            act.wait_ge(s_lru, 1)
            A(lam[:, 1, :], lam[:, 0, :], ACT.Exp, scale=-1.0).then_inc(s_lru, 1)
            for b in range(B_2 + NSPLIT, B_XG):
                block_hi(b)
            for c in range(4):
                act.wait_ge(s_rg1, c + 1)
                A(work[:, c, 0:T], ps[2 + c % 2][:, 0:T], ACT.Sigmoid, bias=V("ba", c)).then_inc(s_sgm, 1)
                A(work[:, 4 + c, 0:T], ps[2 + c % 2][:, T:2 * T], ACT.Sigmoid, bias=V("bx", c)).then_inc(s_sgm, 1)
            for b in range(B_XG, B_XG + 2):
                block_hi(b)
            act.wait_ge(s_lru, 3)
            for c in range(4):
                act.wait_ge(s_sgm, 8)
                A(work[:, c, T:2 * T], work[:, c, 0:T], ACT.Exp, scale=lam[:, 6, c:c + 1]).then_inc(s_ex, 1)
            for c in range(4):
                act.wait_ge(s_ex, 4)
                A(work[:, 4 + c, T:2 * T], work[:, c, 0:T], ACT.Tanh, scale=lam[:, 7, c:c + 1]).then_inc(s_th, 1)

            def win_probs(i):
                block_, heads = WIN[i]
                n = (1 + block_) * P
                act.wait_ge(s_nm, 2 * HEADS + i + 1)
                for a in range(len(heads)):
                    A(p2[:, i % 2, a * n:(a + 1) * n], p2[:, i % 2, a * n:(a + 1) * n], ACT.Exp, bias=wcol[:, i, 1, a:a + 1],
                      accum_out=wcol[:, i, 2, a:a + 1])
                A(wcol[:, i, 3, 0:len(heads)], wcol[:, i, 3, 0:len(heads)], ACT.Exp).then_inc(s_ex2, 1)

            def win_copy(i):
                act.wait_ge(s_pt, 2 * HEADS + i + 1)
                wait(act, s_pv, HEADS + i - 1)
                A(pt2[:, i % 2, :], ps[6 + i % 2][:, :], ACT.Copy).then_inc(s_ptc, 1)

            win_probs(0)
            win_probs(1)
            for b in range(B_XG + 2, B_OUT2):
                block_hi(b)
            for i in range(len(WIN)):
                win_copy(i)
                if i == 3:
                    act.wait_ge(s_th, 4)
                    for c in range(4):
                        act.wait_ge(s_gel, 3 * (c + 1))
                        A(work[:, c, 0:T], gl[:, c, :], ACT.Tanh, scale=0.7978845608028654).then_inc(s_gelt, 1)
                if i + 2 < len(WIN):
                    win_probs(i + 2)
                if i == 3:
                    for c in range(4):
                        act.wait_ge(s_mul2, 1)
                        A(work[:, 4 + c, T:2 * T], work[:, 4 + c, T:2 * T], ACT.Sqrt).then_inc(s_sq2, 1)
                block_hi(B_OUT2 + i)
            for half in range(2):
                for c in range(4):
                    if half == 0:
                        act.wait_ge(s_at2, len(WIN))
                        A(atsq[:, c, :], atn[:, c, :], ACT.Square).then_inc(s_msq, 1)
                    else:
                        act.wait_ge(s_lruo, c + 1)
                        A(work[:, 4 + c, T:2 * T], xcv[:, c, :], ACT.Square).then_inc(s_msq, 1)

            def merge_root(half):
                act.wait_ge(s_msum, half + 1)
                A(rt[:, half * T:(half + 1) * T], ps[2 + half][:, 0:T], ACT.Sqrt, bias=V("eps"), scale=1.0 / 512
                  ).then_inc(s_mrt, 1)

            merge_root(0)
            for c in range(8):
                if c == 2:
                    merge_root(1)
                act.wait_ge(s_mn, c + 1)
                act.wait_ge(s_blk, B_OUT2)
                A(ah3[:, c, 0:T], work[:, c, 0:T], ACT.Copy).then_inc(s_mnh, 1)
            for b in range(B_OUT2 + len(WIN), NB):
                block_hi(b)

            act.wait_ge(s_par, EXP_IN)
            A(bgu[:, :], bgr[:, :], ACT.Copy).then_inc(s_bgh, 1)
            norm_squares(5, x_by_blocks(B_OUT2))
            norm_root(5)
            load_table(ACT.Exp)

            def token_hi(i):
                act.wait_ge(s_ht, i + 1)
                A(hth[:, i % 2, (i // 2) * 512:(i // 2 + 1) * 512], ps[TOKEN_BANK[i]][:, :], ACT.Copy).then_inc(s_hth, 1)

            def top_exp(t):
                act.wait_ge(s_tk, t + 1)
                A(rsc[:, t * 32 + 8:t * 32 + 12], rsc[:, t * 32:t * 32 + 4], ACT.Exp, bias=rsc[:, t * 32 + 16:t * 32 + 17],
                  accum_out=rsc[:, t * 32 + 17:t * 32 + 18]).then_inc(s_tke, 1)

            def experts(p_):
                if p_:
                    act.wait_ge(m["added"], MOE["added"])
                else:
                    act.wait_ge(s_blk, NB)

                def hi(e, q):
                    n_ = e * 12 + (q - 4)
                    wait(act, s_mraw[q % MRAW], e * 48 + 16 * (q // 4) + p_ * MOE_RAW)
                    moe_wait(act, p_, "chunk", n_ - 3)
                    A(mwh[q % MRAW], raw[:, (q % MRAW) * 2048:(q % MRAW + 1) * 2048], ACT.Copy).then_inc(m["hi"], 1)

                def xs_hi(e, half):
                    moe_wait(act, p_, "gathered", 2 * e + 3 + half)
                    A(xsh[:, half * 512:(half + 1) * 512], ps[2][:, :], ACT.Copy).then_inc(m["xs_hi"], 1)

                def y_hi(e):
                    moe_wait(act, p_, "chunk", MOE["chunk"] if isinstance(e, int) and e > NEXP else 12 * (e - 1) + 8)
                    moe_wait(act, p_, "gcol", e - 1)
                    for n in range(2):
                        A(mh[:, n * 512:(n + 1) * 512], ps[n][:, :], ACT.Copy, scale=gcol[:, 0:1]).then_inc(m["y_hi"], 1)

                def body(e, gu=True, dn=True, cmb=True, q0=2):
                    if cmb:
                        y_hi(e)
                    for q in range(q0, 12 if gu else 4):
                        if q == 10 and dn and gu:
                            xs_hi(e, 0)
                        if q == 10 and not dn and p_ == 0:
                            act.wait_ge(s_gtt, 1)
                            A(gT[:, :], ps[0][0:NEXP, 0:T], ACT.Copy).then_inc(s_gtc, 1)
                        hi(e, q)
                    if gu:
                        if not dn:
                            xs_hi(e, 0)
                        moe_wait(act, p_, "gate", e + 1)
                        moe_wait(act, p_, "act", e)
                        A(sig_c, gate_c, ACT.Sigmoid, scale=ALPHA).then_inc(m["sig"], 1)
                        xs_hi(e, 1)
                        hi(e, 12)
                    if dn:
                        moe_wait(act, p_, "slots", e)
                        A(stt[:, :], ps[2][:, 0:T], ACT.Copy).then_inc(m["stt"], 1)
                    if gu:
                        hi(e, 13)
                        for half in range(2):
                            moe_wait(act, p_, "turned", 2 * e + 1 + half)
                            A(ath[:, half * 512:(half + 1) * 512], ps[2 + half][:, :], ACT.Copy).then_inc(m["at_hi"], 1)

                for q in range(4, 8):
                    if p_ == 0 and q == 6:
                        token_hi(0)
                        token_hi(1)
                    hi(0, q)
                if p_ == 0:
                    token_hi(2)
                    token_hi(3)
                xs_hi(-1, 0)
                xs_hi(-1, 1)
                if p_ == 0:
                    top_exp(0)
                    top_exp(1)
                body(0, dn=False, cmb=False, q0=8)
                body(1, cmb=False)
                with act.Fori(2, NEXP) as e:
                    body(e)
                body(NEXP, gu=False)
                y_hi(NEXP + 1)

            experts(0)
            act.wait_ge(s_flag, 1)
            over = act.value_load(flag[0:1, 0:1], min_val=0, max_val=1)
            with act.If(over > 0):
                experts(1)
            act.end_ifs()
            norm_squares(6, x_by_ffn(2))
            norm_root(6)

        @block.gpsimd
        def _(pool):
            sub = lambda o, a, b: nc.gpsimd.tensor_tensor(o, a, b.bitcast(F32), ALU.subtract)

            def block_lo(b):
                pool.wait_ge(s_hi, b + 1)
                s = slice((b % NSPLIT) * D, (b % NSPLIT + 1) * D)
                sub(wl[:, s], raw[:, (b % NRAW) * D:(b % NRAW + 1) * D], wh[:, s]).then_inc(s_lo, 1)

            def ffn(l):
                def lo(f, fv):
                    wait(pool, s_fhi, f + (l * NF + 1))
                    s = slice((fv % 2) * FA, (fv % 2 + 1) * FA)
                    sub(wl[:, s], raw[:, s], wh[:, s]).then_inc(s_flo, 1)

                lo(0, 0)
                lo(1, 1)
                with pool.Fori(0, (NF - 2) // 4) as i:
                    f0 = pool.snap(i * 4)
                    for u in range(4):
                        lo(f0 + (2 + u), u)

            for b in range(B_F):
                block_lo(b)
            ffn(0)
            for b in range(B_F, B_2):
                block_lo(b)
            ffn(1)
            pool.wait_ge(s_fml, 2 * NF)
            nc.gpsimd.memset(rga[:, :, :], 0.0).then_inc(s_zero, 1)
            nc.gpsimd.memset(rgx[:, :, :], 0.0).then_inc(s_zero, 1)
            nc.gpsimd.memset(xr[:, :, 0:3], 0.0).then_inc(s_zero, 1)
            def gelu_arg(c):
                pool.wait_ge(s_ev, B_XG + c + 1)
                g_, x_ = gl[:, c, :], xg[:, c, :]
                nc.gpsimd.tensor_tensor(g_, x_, x_, ALU.mult).then_inc(s_gel, 1)
                pool.wait_ge(s_gel, 3 * c + 1)
                nc.gpsimd.tensor_scalar(g_, g_, 0.044715, 1.0, ALU.mult, ALU.add).then_inc(s_gel, 1)
                pool.wait_ge(s_gel, 3 * c + 2)
                nc.gpsimd.tensor_tensor(g_, g_, x_, ALU.mult).then_inc(s_gel, 1)

            for b in range(B_2, NB):
                if B_OUT2 <= b < B_OUT2 + 4:
                    gelu_arg(b - B_OUT2)
                block_lo(b)

            def experts(p_):
                if p_:
                    pool.wait_ge(m["added"], MOE["added"])

                def lo(e, q):
                    moe_wait(pool, p_, "hi", e * 12 + (q - 3))
                    sub(mwl[q % MRAW], raw[:, (q % MRAW) * 2048:(q % MRAW + 1) * 2048], mwh[q % MRAW]
                        ).then_inc(m["lo_pool"], 1)

                for q in (4, 7, 10):
                    lo(0, q)
                with pool.Fori(1, NEXP) as e:
                    for q in POOL_LO:
                        lo(e, q)
                lo(NEXP, 1)

            experts(0)
            pool.wait_ge(s_flag, 1)
            over = pool.value_load(flag[0:1, 0:1], min_val=0, max_val=1)
            with pool.If(over > 0):
                experts(1)
            pool.end_ifs()

        @block.vector
        def _(dve):
            V_ = nc.vector
            TS, STT, TTn, COPY = V_.tensor_scalar, V_.scalar_tensor_tensor, V_.tensor_tensor, V_.tensor_copy
            chain = [0]

            def link(ins):
                chain[0] += 1
                ins.then_inc(s_dve, 1)
                dve.wait_ge(s_dve, chain[0])

            f32 = lambda a: a.bitcast(F32)

            def ada_step(dst, src, scalar, j):
                if j == 0:
                    return TS(dst, src, scalar, None, ALU.mult)
                return STT(dst, src, scalar, dst, ALU.mult, ALU.add)

            def ada(n):
                g, j = n // 8, n % 8
                dve.wait_ge(s_araw[n % 2], 16 * (n // 2 - 3))
                if j == 0:
                    dve.wait_ge(s_acol, g)
                else:
                    dve.wait_ge(s_ada, n - ADA_FIRST)
                ada_step(acc[:, :], araw[:, n % 2, :], csil[:, j:j + 1] if g < 12 else V("c2", j), j).then_inc(s_ada, 1)

            def bias(g):
                return vec[:, _V["ada_b"] + 8 * g:_V["ada_b"] + 8 * g + 8]

            def mod_ready(g):
                dve.wait_ge(s_acol, g + 1)
                cols = ps[2][:, 0:8]
                if g < 2:
                    both = ps[2][:, 0:16].rearrange("p (i a) -> p i a", a=2)
                    TTn(modx[:, 8 * g:8 * g + 8], both[:, :, 1], bias(g), ALU.add)
                    cols = both[:, :, 0]
                TTn(mod[:, 8 * g:8 * g + 8], cols, bias(g), ALU.add).then_inc(s_mod, 1)

            def m_col(g, j):
                return mod[:, 8 * g + j:8 * g + j + 1]

            def norm_gain(gain, g_shift):
                dve.wait_ge(s_mod, g_shift + 2)
                gcols = vec[:, gain:gain + 8]
                if g_shift == 0:
                    STT(gsx[:, :], modx[:, 8:16], 1.0, gcols, ALU.add, ALU.mult)
                link(STT(gs[:, :], mod[:, 8 * g_shift + 8:8 * g_shift + 16], 1.0, gcols, ALU.add, ALU.mult))

            def norm_split(n, gain, g_shift, hl):
                norm_gain(gain, g_shift)
                dve.wait_ge(s_rt, n + 1)
                link(V_.reciprocal(rstd[:, 0:T], rt[:, 0:T]))
                for j in range(DJ + 2):
                    if j < DJ:
                        STT(work[:, j, 0:T], x[:, j, :], gs[:, j:j + 1], rstd[:, 0:T], ALU.mult, ALU.mult).then_inc(s_h, 1)
                    if j >= 2:
                        k = j - 2
                        dve.wait_ge(s_hh, DJ * hl + k + 1)
                        STT(al3[:, k, 0:T], work[:, k, 0:T], m_col(g_shift, k), f32(ah3[:, k, 0:T]), ALU.add, ALU.subtract
                            ).then_inc(s_hl, 1)

            def norm(n, gain, g_shift, hl=None):
                ahead = DJ if n == 0 else 1
                scaled = DJ * {0: 0, 2: 1, 5: 2}[n]
                dve.wait_ge(s_rt, n + 1)
                link(V_.reciprocal(rstd[:, 0:T], rt[:, 0:T]))
                for j in range(ahead + DJ + 2):
                    if j < DJ:
                        TTn(work[:, j, 0:T], x[:, j, :], rstd[:, 0:T], ALU.mult).then_inc(s_nt, 1)
                    if j == ahead:
                        if n == 0:
                            link(V_.reciprocal(rstd[:, T:2 * T], rt[:, T:2 * T]))
                            for i in range(DJ):
                                TTn(work[:, i, T:2 * T], xc[:, i * TC:(i + 1) * TC], rstd[:, T:2 * T], ALU.mult
                                    ).then_inc(s_ntx, 1)
                            mod_ready(0)
                            mod_ready(1)
                        norm_gain(gain, g_shift)
                    k = j - ahead
                    if 0 <= k < DJ:
                        dve.wait_ge(s_nt, scaled + k + 1)
                        TS(work[:, k, 0:T], work[:, k, 0:T], gs[:, k:k + 1], m_col(g_shift, k), ALU.mult, ALU.add
                           ).then_inc(s_h, 1)
                    if k >= 2 and hl is not None:
                        k = k - 2
                        dve.wait_ge(s_hh, DJ * hl + k + 1)
                        TTn(al3[:, k, 0:T], work[:, k, 0:T], f32(ah3[:, k, 0:T]), ALU.subtract).then_inc(s_hl, 1)

            def evacuate(b, out, rows=slice(0, P), w=T):
                dve.wait_ge(s_blk, b + 1)
                COPY(out, ps[b % 2][rows, 0:w]).then_inc(s_ev, 1)

            def ctx_norm():
                for j in range(DJ + 2):
                    if j in (6, 8):
                        evacuate((j - 6) // 2, cq[:, (j - 6) // 2, :])
                    if j < DJ:
                        dve.wait_ge(s_ntx, j + 1)
                        TS(work[:, j, T:2 * T], work[:, j, T:2 * T], gsx[:, j:j + 1], modx[:, j:j + 1], ALU.mult, ALU.add
                           ).then_inc(s_hx, 1)
                    if j >= 2:
                        k = j - 2
                        dve.wait_ge(s_hhx, k + 1)
                        TTn(al3[:, k, T:2 * T], work[:, k, T:2 * T], f32(ah3[:, k, T:2 * T]), ALU.subtract).then_inc(s_hlx, 1)

            def residual(b, j, g):
                dve.wait_ge(s_blk, b + 1)
                STT(x[:, j, :], ps[b % 2][:, 0:T], m_col(g, j), x[:, j, :], ALU.mult, ALU.add).then_inc(s_ev, 1)

            dve.wait_ge(s_vec, 16)
            dve.wait_ge(s_sil, 1)
            link(TTn(csil[:, :], csil[:, :], vec[:, 0:16], ALU.mult))
            dve.wait_ge(s_sq, DJ)
            V_.reduce_sum(kpe[:, :], work[:, :, :].rearrange("p j t -> p t j"), AX).then_inc(s_sqx, 1)
            norm(0, _V["n1"], 0, hl=0)
            ctx_norm()

            V_.memset(czp[:, :, 0:1], 0.0)
            link(V_.memset(czp[:, :, T + 1:T + 2], 0.0))
            for b in range(B_O):
                if b < B_KV:
                    if b >= 2:
                        evacuate(b, cq[:, b, :])
                elif b < B_KPE:
                    evacuate(b, ckv[:, b - B_KV, :], w=2 * T)
                elif b == B_KPE:
                    evacuate(b, kpe[NOPE:QD, :], slice(NOPE, QD), 2 * T)
                elif b < B_CC:
                    evacuate(b, cbg[:, b - B_CB, :])
                elif b < B_CU:
                    evacuate(b, ccg[:, b - B_CC, :])
                else:
                    dve.wait_ge(s_blk, b + 1)
                    TTn(czp[:, b - B_CU, 1:T + 1], ps[b % 2][:, 0:T], ccg[:, b - B_CU, :], ALU.mult).then_inc(s_ev, 1)
                if b < 8:
                    ada(ADA_FIRST + b)
                if b == B_CC - 1:
                    dve.wait_ge(s_cqrt, 1)
                    link(V_.reciprocal(rstd[:, 0:T], rt[:, 0:T]))
                    for j in range(3):
                        STT(cq[:, j, :], cq[:, j, :], V("qg", j), rstd[:, 0:T], ALU.mult, ALU.mult).then_inc(s_cqn, 1)
                if b == B_CC:
                    dve.wait_ge(s_cqrt, 2)
                    dve.wait_ge(s_cqn, 3)
                    link(V_.reciprocal(rstd[:, :], rt[:, :]))
                    for j in range(2):
                        STT(ckv[:, j, :], ckv[:, j, :], V("kvg", j), rstd[:, :], ALU.mult, ALU.mult).then_inc(s_cqn, 1)
                    TS(pbuf[NOPE:QD, 0, :], kpe[NOPE:QD, :], vec[NOPE:QD, _V["kgain"]:_V["kgain"] + 1], None, ALU.mult
                       ).then_inc(s_qkc, 1)
            cos, sin = [con[NOPE:QD, _C[n]:_C[n] + T] for n in ("cos", "sin")]
            V_.memset(kgone[NOPE:QD, :], 1.0)
            COPY(kgone[0:NOPE, :], V("kgain", 0, NOPE))
            dve.wait_ge(s_rot, 1)
            dve.wait_ge(s_qkc, 1)
            TTn(pbuf[NOPE:QD, 1, 0:T], ps[4][NOPE:QD, 0:T], sin, ALU.mult)
            link(TTn(pbuf[NOPE:QD, 0, 0:T], pbuf[NOPE:QD, 0, 0:T], cos, ALU.mult))
            TTn(pbuf[NOPE:QD, 0, 0:T], pbuf[NOPE:QD, 0, 0:T], pbuf[NOPE:QD, 1, 0:T], ALU.add).then_inc(s_qrope, 1)
            dve.wait_ge(s_ev, B_O)
            for c in range(CJ):
                ins = TS(ccg[:, c, :], czp[:, c, 0:T], V("conv", c), None, ALU.mult)
            link(ins)
            for i in (1, 2):
                for c in range(CJ):
                    ins = STT(ccg[:, c, :], czp[:, c, i:i + T], V("conv", 4 * i + c), ccg[:, c, :], ALU.mult, ALU.add)
                link(ins)
            for c in range(CJ):
                TTn(work[:, 4 + c, T:2 * T], ccg[:, c, :], cbg[:, c, :], ALU.mult).then_inc(s_cs, 1)
            mod_ready(2)
            dve.wait_ge(s_cs, CJ)
            for j in range(PAIRS):
                dve.wait_ge(s_qksq, 2 + j)
                COPY(kb[0:NOPE, 2 * j, :], ps[PAIR_BANK[j]][0:NOPE, :])
                COPY(kb[0:NOPE, 2 * j + 1, :], ps[PAIR_BANK[j]][NOPE:P, :]).then_inc(s_qkc, 1)
            for c in range(CJ):
                dve.wait_ge(s_csh, c + 1)
                TTn(al3[:, 4 + c, 0:T], work[:, 4 + c, T:2 * T], f32(ah3[:, 4 + c, 0:T]), ALU.subtract).then_inc(s_csl, 1)

            def q_copy(j):
                dve.wait_ge(s_qksq, 2 + PAIRS + j)
                TS(qb[0:QD, 2 * j:2 * j + 2, :], ps[PAIR_BANK[j]][0:QD, :].rearrange("p (a t) -> p a t", a=2),
                   V("qgain", 0, QD), None, ALU.mult).then_inc(s_qkc, 1)

            sin2, cos2 = [tb.unsqueeze(1).to_broadcast([ROPE, 2, T]) for tb in (sin, cos)]
            turned_sin = pbuf[NOPE:QD, 1, :].rearrange("p (a t) -> p a t", a=2)

            def q_rope(j):
                dve.wait_ge(s_rot, 2 + j)
                dve.wait_ge(s_qrope, 1 + j)
                part = qb[NOPE:QD, 2 * j:2 * j + 2, :]
                TTn(turned_sin, ps[PAIR_BANK[j]][NOPE:QD, :].rearrange("p (a t) -> p a t", a=2), sin2, ALU.mult)
                link(TTn(part, part, cos2, ALU.mult))
                TTn(part, part, turned_sin, ALU.add).then_inc(s_qrope, 1)

            q_copy(0)
            ada(24)
            ada(25)
            q_copy(1)
            q_rope(0)
            q_copy(2)
            q_rope(1)
            q_copy(3)
            dve.wait_ge(s_qk8r, 1)
            V_.reciprocal(rt[0:8, :], kpe[0:8, :]).then_inc(s_qkr8, 1)
            q_rope(2)
            q_rope(3)

            def k_norm(h):
                dve.wait_ge(s_qkbc, h + 1)
                dve.wait_ge(s_qk8r, 2)
                STT(kb[0:QD, h, :], kb[0:QD, h, :], kgone[0:QD, :], ps[PAIR_BANK[h % PAIRS]][0:QD, :], ALU.mult, ALU.mult
                    ).then_inc(s_qkn, 1)

            for h in range(PAIRS):
                k_norm(h)
            dve.wait_ge(s_rot, 6)
            link(V_.reciprocal(qrs[:, :], ps[3][:, T:T + TT * HEADS]))
            link(TS(qrs[:, :], qrs[:, :], QK_SCALE, None, ALU.mult))
            for h in range(PAIRS, HEADS):
                k_norm(h)
            ada(26)

            def row_max(i):
                dve.wait_ge(s_sc, i + 1)
                link(V_.reduce_max(srow[:, i % 2, 0:1], ps[4 + i % 2][:, :], AX))
                TS(srow[:, i % 2, 1:2], srow[:, i % 2, 0:1], q_scale(i), -1.0, ALU.mult, ALU.mult).then_inc(s_nm, 1)

            def attn_lo(c):
                dve.wait_ge(s_ao, c + 1)
                TTn(al3[:, c, 0:T], ps[c % 2][:, 0:T], f32(ah3[:, c, 0:T]), ALU.subtract).then_inc(s_aol, 1)

            row_max(0)
            for i in range(2 * HEADS):
                if i + 1 < 2 * HEADS:
                    row_max(i + 1)
                dve.wait_ge(s_pe_, i + 1)
                V_.reciprocal(srow[:, i % 2, 3:4], srow[:, i % 2, 2:3]).then_inc(s_dg, 1)
                if i < 13:
                    ada(27 + i)
                if i == 10:
                    mod_ready(3)
                if i in (8, 12):
                    attn_lo((i - 8) // 4)
            attn_lo(2)
            attn_lo(3)
            for j in range(DJ):
                residual(B_O + j, j, 2)
                if j == 0:
                    mod_ready(4)
                    ada(40)
                if j < DJ - 1:
                    ada(41 + j)

            def ffn(l, g_gate):
                base_n, base_g = 48 + 48 * l, 6 + 6 * l

                def mul(f, slot):
                    wait(dve, s_fsig, f + (l * NF + 1))
                    TTn(sg[:, slot, :], ps[slot][:, 0:T], sg[:, slot, :], ALU.mult).then_inc(s_ft, 1)
                    wait(dve, s_ft, f + (l * NF + 1))
                    TTn(mm_[:, slot, :], ps[slot][:, T:2 * T], sg[:, slot, :], ALU.mult).then_inc(s_fm, 1)

                def mul_lo(f, slot):
                    wait(dve, s_fmh, f + (l * NF + 1))
                    s = slice(slot * T, (slot + 1) * T)
                    TTn(ml[:, s], mm_[:, slot, :], f32(mh[:, s]), ALU.subtract).then_inc(s_fml, 1)

                def down_lo(f, slot):
                    wait(dve, s_fbhi, f + (l * NF + 1))
                    w = slice(2 * FA + slot * D, 2 * FA + (slot + 1) * D)
                    TTn(wl[:, w], raw[:, w], f32(wh[:, w]), ALU.subtract).then_inc(s_fblo, 1)

                down_lo(0, 0)
                with dve.Fori(0, (NF - 2) // 4) as i:
                    f0 = dve.snap(i * 4)
                    n0 = dve.snap(i * 8 + (base_n - ADA_FIRST))
                    loaded = dve.snap(i * 64 + 16 * (base_n // 2 - 3))
                    col = dve.snap(i * 8 + 8 * (base_g - 1))
                    cols = dve.snap(i + base_g)
                    for u in range(4):
                        mul(f0 + u, u % 2)
                        if u == 0:
                            dve.wait_ge(s_acol, cols)
                            TTn(mod[:, bass.ds(col, 8)], ps[2][:, 0:8], vec[:, bass.ds(col + _V["ada_b"], 8)], ALU.add
                                ).then_inc(s_mod, 1)
                        for j in (2 * u, 2 * u + 1):
                            dve.wait_ge(s_araw[j % 2], loaded + 16 * (j // 2))
                            if j == 0:
                                dve.wait_ge(s_acol, cols)
                            else:
                                dve.wait_ge(s_ada, n0 + j)
                            ada_step(acc[:, :], araw[:, j % 2, :], csil[:, j:j + 1] if l == 0 else V("c2", j), j
                                     ).then_inc(s_ada, 1)
                            if j % 2 == 0:
                                mul_lo(f0 + u, u % 2)
                        down_lo(f0 + (u + 1), (u + 1) % 2)
                mul(NF - 2, 0)
                mod_ready(base_g + 4)
                mul_lo(NF - 2, 0)
                down_lo(NF - 1, 1)
                for j in range(2):
                    ada(base_n + 40 + j)
                mul(NF - 1, 1)
                mul_lo(NF - 1, 1)
                for j in range(2, 4):
                    ada(base_n + 40 + j)
                dve.wait_ge(s_fdn, 1 + (l + 1) * NF)
                for j in range(DJ):
                    STT(x[:, j, :], ps[4 + j // 2][:, (j % 2) * T:(j % 2 + 1) * T], m_col(g_gate, j), x[:, j, :],
                        ALU.mult, ALU.add).then_inc(s_x, 1)
                for j in range(4, 6):
                    ada(base_n + 40 + j)

            norm_split(1, _V["n2"], 3, hl=1)
            ffn(0, 5)
            norm(2, _V["n1"] + 8, 6)
            ada(94)
            ada(95)
            for c in range(8):
                dve.wait_ge(s_f2h, c + 1)
                TTn(al3[:, c, 0:T], ps[c % 2][:, 0:T], f32(ah3[:, c, 0:T]), ALU.subtract).then_inc(s_f2l, 1)
            for j in range(DJ):
                residual(B_F + j, j, 8)
            norm_split(3, _V["n2"] + 8, 9, hl=2)
            ffn(1, 11)

            lam_in = vec[:, _V["lam"]:_V["lam"] + 4]
            STT(lam[:, 0, :], lam_in, -1.0, lam_in, ALU.mult, ALU.max).then_inc(s_lru, 1)
            norm_split(4, _V["gmix"], 12, hl=3)
            ada(142)
            ada(143)
            TS(nsink[:, :], vec[:, _V["sink"]:_V["sink"] + 8], -1.0, None, ALU.mult).then_inc(s_ms2, 1)
            dve.wait_ge(s_zero, 3)
            for b in range(B_2, B_XG):
                if b < B_Q2:
                    evacuate(b, xr[:, b - B_XR, 3:T + 3])
                    if b == B_2 + 3:
                        mod_ready(17)
                elif b < B_K2:
                    evacuate(b, q2[:, b - B_Q2, :])
                elif b == B_K2:
                    evacuate(b, k2[:, :])
                else:
                    evacuate(b, v2[:, :, :].rearrange("p a n -> p (a n)"))
                if B_Q2 <= b < B_K2:
                    i = b - B_Q2
                    dve.wait_ge(s_ev, B_Q2)
                    for c in range(4):
                        if i == 0:
                            ins = TS(xcv[:, c, :], xr[:, c, 0:T], V("conv2", c), V("conv2b", c), ALU.mult, ALU.add)
                        else:
                            ins = STT(xcv[:, c, :], xr[:, c, i:i + T], V("conv2", 4 * i + c), xcv[:, c, :], ALU.mult, ALU.add)
                        if i == 3:
                            ins.then_inc(s_xcv, 1)
                    if i < 3:
                        link(ins)
                if b == B_K2:
                    dve.wait_ge(s_lru, 2)
                    e_, z_, zz, q_, m8 = [lam[:, k, :] for k in (1, 2, 3, 4, 5)]
                    link(TS(z_, e_, 2.0, None, ALU.add))
                    link(V_.reciprocal(z_, z_))
                    link(TTn(z_, e_, z_, ALU.mult))
                    link(TTn(zz, z_, z_, ALU.mult))
                    link(TS(q_, zz, 1.0 / 17, None, ALU.mult))
                    for k in range(7, 0, -1):
                        link(STT(q_, q_, 1.0 / (2 * k + 1), zz, ALU.add, ALU.mult))
                    link(STT(q_, q_, 1.0, z_, ALU.add, ALU.mult))
                    link(TS(m8, vec[:, _V["lam"]:_V["lam"] + 4], 0.0, 8.0, ALU.min, ALU.mult))
                    link(STT(lam[:, 6, :], q_, -16.0, m8, ALU.mult, ALU.add))
                    TS(lam[:, 7, :], lam[:, 6, :], -1.0, None, ALU.mult).then_inc(s_lru, 1)

            def win_max(i):
                block_, heads = WIN[i]
                nh, n = len(heads), (1 + block_) * P
                sl = slice(heads[0], heads[0] + nh)
                dve.wait_ge(s_sc, 2 * HEADS + i + 1)
                wait(dve, s_pt, 2 * HEADS + i - 1 if i >= 2 else 0)
                mask = con[:, _C["mask"] + 2 * P - n:_C["mask"] + 2 * P].unsqueeze(1).to_broadcast([P, nh, n])
                p_ = p2[:, i % 2, :].rearrange("p (h n) -> p h n", h=nh)
                STT(p_, ps[4 + i % 2][:, :].rearrange("p (h n) -> p h n", h=nh), Q_SCALE2, mask, ALU.mult, ALU.add
                    ).then_inc(s_ms2, 1)
                dve.wait_ge(s_ms2, i + 2)
                link(V_.reduce_max(wcol[:, i, 0, 0:nh], p_, AX))
                link(STT(wcol[:, i, 1, 0:nh], wcol[:, i, 0, 0:nh], -1.0, nsink[:, sl], ALU.mult, ALU.min))
                TTn(wcol[:, i, 3, 0:nh], wcol[:, i, 1, 0:nh], vec[:, _V["sink"] + heads[0]:_V["sink"] + heads[0] + nh], ALU.add
                    ).then_inc(s_nm, 1)

            def win_scale(i):
                block_, heads = WIN[i]
                nh, n = len(heads), (1 + block_) * P
                dve.wait_ge(s_ex2, i + 1)
                link(TTn(wcol[:, i, 2, 0:nh], wcol[:, i, 2, 0:nh], wcol[:, i, 3, 0:nh], ALU.add))
                link(V_.reciprocal(wcol[:, i, 4, 0:nh], wcol[:, i, 2, 0:nh]))
                for a in range(nh):
                    ins = TS(p2[:, i % 2, a * n:(a + 1) * n], p2[:, i % 2, a * n:(a + 1) * n], wcol[:, i, 4, a:a + 1], None, ALU.mult)
                ins.then_inc(s_dg, 1)

            def win_out(i):
                block_, heads = WIN[i]
                nh = len(heads)
                kv = slice(64 * (heads[0] // 4), 64 * (heads[0] // 4) + 64)
                dve.wait_ge(s_pv, HEADS + i + 1)
                COPY(atn[kv, heads[0] % 4:heads[0] % 4 + nh, block_ * P:(block_ + 1) * P],
                     ps[2 + i % 2][kv, 0:nh * P].rearrange("p (h q) -> p h q", h=nh)).then_inc(s_at2, 1)

            a_, th, ig = work[:, 0:4, T:2 * T], work[:, 4:8, T:2 * T], work[:, 4:8, 0:T]
            sq_ = xr[:, :, 0:T]
            dve.wait_ge(s_sgm, 8)
            TTn(ig, ig, xcv[:, :, :], ALU.mult)
            win_max(0)
            win_max(1)
            for i in range(len(WIN)):
                if i < 4:
                    evacuate(B_XG + i, xg[:, i, :])
                win_scale(i)
                if i + 2 < len(WIN):
                    win_max(i + 2)
                if i == 1:
                    dve.wait_ge(s_th, 4)
                    link(TTn(sq_, a_, a_, ALU.mult))
                    link(STT(th, sq_, 1.0, th, ALU.add, ALU.mult))
                    TS(th, th, 0.0, None, ALU.max).then_inc(s_mul2, 1)
                if i == 5:
                    dve.wait_ge(s_gelt, 4)
                    STT(xg[:, :, :], work[:, 0:4, 0:T], 1.0, xg[:, :, :], ALU.add, ALU.mult)
                    dve.wait_ge(s_sq2, 4)
                    link(TTn(ig, th, ig, ALU.mult))
                if i >= 1:
                    win_out(i - 1)
            win_out(len(WIN) - 1)
            dve.wait_ge(s_at2, len(WIN))
            for c in range(4):
                ins = V_.tensor_tensor_scan(gl[:, c, :], work[:, c, T:2 * T], work[:, 4 + c, 0:T], 0.0, ALU.mult, ALU.add)
            link(ins)
            for c in range(4):
                STT(xcv[:, c, :], gl[:, c, :], 0.5, xg[:, c, :], ALU.mult, ALU.mult).then_inc(s_lruo, 1)
            for c in range(10):
                if c in (0, 4):
                    dve.wait_ge(s_mrt, c // 4 + 1)
                    half = slice((c // 4) * T, (c // 4 + 1) * T)
                    link(V_.reciprocal(rstd[:, half], rt[:, half]))
                if c < 8:
                    src = atn[:, c, :] if c < 4 else xcv[:, c - 4, :]
                    STT(work[:, c, 0:T], src, V("gattn", c) if c < 4 else V("glru", c - 4), rstd[:, half], ALU.mult, ALU.mult
                        ).then_inc(s_mn, 1)
                if c >= 2:
                    k = c - 2
                    dve.wait_ge(s_mnh, k + 1)
                    TTn(al3[:, k, 0:T], work[:, k, 0:T], f32(ah3[:, k, 0:T]), ALU.subtract).then_inc(s_mnl, 1)
            for j in range(DJ):
                residual(B_OUT2 + j, j, 14)
                if j == 3:
                    dve.wait_ge(s_bgh, 1)
                    TTn(bgu[NEXP:2 * NEXP, :], bgr[NEXP:2 * NEXP, :], f32(bgu[NEXP:2 * NEXP, :]), ALU.subtract
                        ).then_inc(s_bgl, 1)

            norm(5, _V["gffn"], 15)
            V_.memset(pos[:, :, :], -1.0).then_inc(s_pos, 1)
            iota32 = C("iota32", NEXP)
            for t in range(TT):
                r = lambda a, n=1: rsc[:, 32 * t + a:32 * t + a + n]
                dve.wait_ge(s_lg, t + 1)
                link(TTn(logit[:, t, :], ps[4 + t][:, 0:NEXP], vec[:, _V["brout"]:_V["brout"] + NEXP], ALU.add))
                link(V_.max(r(0, 8), logit[:, t, :]))
                TS(r(16), r(0), -1.0, None, ALU.mult).then_inc(s_tk, 1)
                link(V_.max_index(ridx[:, t, :], r(0, 8), logit[:, t, :]))
                link(COPY(r(20, TOPK), ridx[:, t, 0:TOPK]))
                for k in range(TOPK):
                    if k == 0:
                        ins = TS(mask_[:, t, :], iota32, r(20), None, ALU.is_equal)
                    else:
                        ins = STT(mask_[:, t, :], iota32, r(20 + k), mask_[:, t, :], ALU.is_equal, ALU.add)
                    if k < TOPK - 1:
                        link(ins)
                ins.then_inc(s_mask, 1)

            def token_lo(i):
                dve.wait_ge(s_hth, i + 1)
                f = slice((i // 2) * 512, (i // 2 + 1) * 512)
                TTn(htl[:, i % 2, f], ps[TOKEN_BANK[i]][:, :], f32(hth[:, i % 2, f]), ALU.subtract).then_inc(s_htl, 1)

            for i in range(4):
                token_lo(i)
            dve.wait_ge(s_cum, 1)
            dve.wait_ge(s_pos, 1)
            dve.wait_ge(s_mask, 2)
            for t in range(TT):
                link(STT(pos[:, t, 0:NEXP], ps[3][:, 32 * t:32 * t + 32], 1.0, mask_[:, t, :], ALU.add, ALU.mult))
                link(TS(pos[:, t, 0:NEXP], pos[:, t, 0:NEXP], -1.0, None, ALU.add))
            V_.reduce_max(rsc[:, 31:32], ps[3][:, 64:96], AX).then_inc(s_cumr, 1)
            dve.wait_ge(s_cumr, 1)
            TS(flag[0:1, 0:1], rsc[0:1, 31:32], CAP + 0.5, None, ALU.is_gt).then_inc(s_flag, 1)

            def gates():
                for t in range(TT):
                    r = lambda a, n=1: rsc[:, 32 * t + a:32 * t + a + n]
                    dve.wait_ge(s_tke, t + 1)
                    link(V_.reciprocal(r(18), r(17)))
                    link(TS(r(24, TOPK), r(8, TOPK), r(18), None, ALU.mult))
                    for k in range(TOPK):
                        dst = gatew[:, t, :] if k == 0 else logit[:, t, :]
                        ins = TS(dst, iota32, r(20 + k), r(24 + k), ALU.is_equal, ALU.mult)
                        if k:
                            link(ins)
                            ins = TTn(gatew[:, t, :], gatew[:, t, :], logit[:, t, :], ALU.add)
                        if k < TOPK - 1:
                            link(ins)
                    ins.then_inc(s_route, 1)

            def sum_start(t):
                dve.wait_ge(s_bd, t + 1)
                for n in range(2):
                    COPY(oacc[:, t, n * 512:(n + 1) * 512], ps[n][:, :]).then_inc(s_oi, 1)

            def experts(p_):
                if p_:
                    dve.wait_ge(m["added"], MOE["added"])
                    TS(pos[:, :, :], pos[:, :, :], -float(CAP), None, ALU.add).then_inc(s_pos, 1)
                    dve.wait_ge(s_pos, p_ + 1)

                def col(e):
                    return slice(e, e + 1) if isinstance(e, int) else bass.ds(e, 1)

                def onehot(dst, e, done):
                    for t in range(TT):
                        ins = TS(dst[:, t, :], C("iota", CAP), pos[:, t, col(e)], None, ALU.is_equal)
                    ins.then_inc(done, 1)

                def select(e):
                    TS(sel[:, :], ones[0:64, :], con[0:64, _C["eye64"]:_C["eye64"] + NEXP + 1][:, col(e)], None, ALU.mult
                       ).then_inc(m["select"], 1)

                def lo(e, q):
                    if q % CH in POOL_LO:
                        return
                    moe_wait(dve, p_, "hi", e * 12 + (q - 3))
                    TTn(mwl[q % MRAW], raw[:, (q % MRAW) * 2048:(q % MRAW + 1) * 2048], f32(mwh[q % MRAW]), ALU.subtract
                        ).then_inc(m["lo_dve"], 1)

                def xs_lo(e, half):
                    moe_wait(dve, p_, "xs_hi", 2 * e + 3 + half)
                    COPY(xsl[:, half * 512:(half + 1) * 512], ps[3][:, :]).then_inc(m["xs_lo"], 1)

                def y_lo(e):
                    for n in range(2):
                        moe_wait(dve, p_, "y_hi", 2 * (e - 2) + n + 1)
                        s = slice(n * 512, (n + 1) * 512)
                        STT(ml[:, s], ps[n][:, :], gcol[:, 0:1], f32(mh[:, s]), ALU.mult, ALU.subtract
                            ).then_inc(m["y_lo"], 1)

                def add(e, t):
                    moe_wait(dve, p_, "combined", 2 * (e - 2) + t + 1)
                    for n in range(2):
                        o = oacc[:, t, n * 512:(n + 1) * 512]
                        TTn(o, ps[n][:, :], o, ALU.add).then_inc(m["added"], 1)

                def body(e, gu=True, dn=True, cmb=True, q0=0):
                    def lo_(q):
                        if q >= q0 and (gu or q < 4):
                            lo(e, q)

                    if gu:
                        moe_wait(dve, p_, "xs_lo", 2 * e + 2)
                        onehot(sone, e + 1, m["onehot"])
                    if dn:
                        onehot(stwo, e - 1, m["onehot2"])
                    if cmb:
                        y_lo(e)
                    lo_(2)
                    lo_(3)
                    if cmb:
                        add(e, 0)
                    for q in (5, 6):
                        lo_(q)
                    if cmb:
                        add(e, 1)
                    for q in (8, 9):
                        lo_(q)
                        if not dn and p_ == 0:
                            sum_start(q - 8)
                    if gu:
                        if not dn:
                            if p_ == 0:
                                dve.wait_ge(s_oi, 4)
                            lo_(11)
                        moe_wait(dve, p_, "chunk", 12 * e + 4 if dn else 8)
                        xs_lo(e, 0)
                        moe_wait(dve, p_, "turned", 2 * e)
                        TS(gate_c, ps45, LIMIT, None, ALU.min).then_inc(m["gate"], 1)
                        TS(up_c, ps67, LIMIT, -LIMIT, ALU.min, ALU.max).then_inc(m["gu"], 1)
                        select(e + 1 if not isinstance(e, int) or e < NEXP - 1 else e)
                        if dn:
                            lo_(11)
                        moe_wait(dve, p_, "sig", e + 1)
                        TTn(sig_c, gate_c, sig_c, ALU.mult).then_inc(m["glu"], 1)
                        moe_wait(dve, p_, "glu", e + 1)
                        STT(act_c, up_c, 1.0, sig_c, ALU.add, ALU.mult).then_inc(m["act"], 1)
                        xs_lo(e, 1)
                        lo(e, 12)
                    if dn:
                        moe_wait(dve, p_, "stt", e)
                        COPY(gcol[:, :], ps[2][:, T:T + 1]).then_inc(m["gcol"], 1)
                    if gu:
                        for half in range(2):
                            moe_wait(dve, p_, "at_hi", 2 * e + 1 + half)
                            s = slice(half * 512, (half + 1) * 512)
                            TTn(atl[:, s], ps[2 + half][:, :], f32(ath[:, s]), ALU.subtract).then_inc(m["at_lo"], 1)

                onehot(sone, 0, m["onehot"])
                select(0)
                for half in range(2):
                    lo(0, 5 + half)
                    xs_lo(-1, half)
                if p_ == 0:
                    gates()
                body(0, dn=False, cmb=False, q0=8)
                body(1, cmb=False, q0=2)
                with dve.Fori(2, NEXP) as e:
                    body(e, q0=2)
                body(NEXP, gu=False, q0=2)
                y_lo(NEXP + 1)
                add(NEXP + 1, 0)
                add(NEXP + 1, 1)

            experts(0)
            over = dve.value_load(flag[0:1, 0:1], min_val=0, max_val=1)
            with dve.If(over > 0):
                experts(1)
            dve.end_ifs()
            for j in range(DJ):
                dve.wait_ge(s_ot, j + 1)
                STT(x[:, j, :], ps[4 + j % 4][:, 0:T], m_col(17, j), x[:, j, :], ALU.mult, ALU.add).then_inc(s_x, 1)
            dve.wait_ge(s_rt, 7)
            link(V_.reciprocal(rstd[:, 0:T], rt[:, 0:T]))
            for j in range(DJ):
                STT(work[:, j, 0:T], x[:, j, :], V("gfin", j), rstd[:, 0:T], ALU.mult, ALU.mult).then_inc(s_fy, 1)


def constants():
    c = np.zeros((P, NC_), np.float32)

    def put(name, a):
        c[:a.shape[0], _C[name]:_C[name] + a.shape[1]] = a

    r = np.arange(P)
    put("ident", np.eye(P))
    put("ones", np.ones((P, P)))
    put("triu", (r[:, None] < r[None, :]) * 1.0)
    put("iota", np.broadcast_to(np.arange(P), (P, P)))
    put("iota32", np.broadcast_to(np.arange(NEXP), (P, NEXP)))
    put("pair8", np.repeat(np.eye(HEADS).reshape(4, 2, HEADS).transpose(1, 0, 2).reshape(2, 32), NOPE, axis=0))
    put("head8", np.broadcast_to(np.eye(HEADS).reshape(1, 64), (P, 64)))
    put("bcast8", np.repeat(np.eye(HEADS), QD, axis=1))
    put("eye64", np.eye(NEXP, NEXP + 1)[np.arange(2 * NEXP) % NEXP])
    put("mask", np.concatenate([np.where(r[None, :] > r[:, None], 0, NEG), np.where(r[None, :] <= r[:, None], 0, NEG)], 1))
    t = np.arange(T)
    half = ROPE // 2
    inv = (1.0 / (np.float32(10000.0) ** (np.arange(0, half, 2, dtype=np.float32) / np.float32(half)))).astype(np.float32)
    rows, cols = (t // 64).astype(np.float32), (t % 64).astype(np.float32)
    ang = np.concatenate([np.tile(rows[None] * inv[:, None], (2, 1)), np.tile(cols[None] * inv[:, None], (2, 1))])
    c[NOPE:QD, _C["cos"]:_C["cos"] + T] = np.cos(ang.astype(np.float64))
    c[NOPE:QD, _C["sin"]:_C["sin"] + T] = np.sin(ang.astype(np.float64))
    rot = np.zeros((ROPE, ROPE))
    for base in (0, half):
        for i in range(half // 2):
            rot[base + half // 2 + i, base + i] = -1.0
            rot[base + i, base + half // 2 + i] = 1.0
    c[NOPE:QD, _C["rot"]:_C["rot"] + ROPE] = rot
    phase = 2 * np.pi * ((t[:, None] * t[None, :]) % T) / T
    tab = np.stack([np.cos(phase), np.sin(phase), -np.sin(phase)], 1) / np.sqrt(float(T))
    tab = np.ascontiguousarray(tab.reshape(2, P, 3, T).transpose(1, 0, 2, 3)).astype(np.float32)
    return c, tab


def kernel(**inp):
    import concourse.bacc as bacc
    from concourse.bass_utils import run_bass_kernel_spmd

    a = {k: np.asarray(v) for k, v in inp.items()}

    def cols(v):
        return np.reshape(v, (-1, P)).T

    def feature_major(v):
        return v.T.reshape(DJ, P, -1).transpose(1, 0, 2)

    def blocks(w):
        return w.reshape(DJ, P, -1, P).transpose(2, 1, 0, 3).reshape(-1, P, D)

    perm = np.arange(512).reshape(2, 4, HD).transpose(1, 0, 2).reshape(512)
    v = np.zeros((P, NV), np.float32)

    def put(name, x):
        x = np.asarray(x)
        v[:x.shape[0], _V[name]:_V[name] + x.shape[1]] = x

    put("c", cols(a["c"][0])); put("cx", cols(a["c_ctx"])); put("c2", cols(a["c_2"][0]))
    put("ada_b", np.concatenate([cols(a["ada_b"][0]), cols(a["ada_b"][1]), cols(a["b_ada_2"][0])], 1))
    put("n1", cols(a["norm1_g"])); put("n2", cols(a["norm2_g"]))
    put("gmix", cols(a["g_mix_2"][0])); put("gffn", cols(a["g_ffn_2"][0])); put("gfin", cols(a["g_final_2"]))
    put("qg", cols(a["q_norm_g"][0])); put("kvg", cols(a["kv_norm_g"][0]))
    put("qgain", a["q_gain"][0][:, None]); put("kgain", a["k_gain"][0][:, None])
    put("conv", cols(a["conv_w"][0])); put("conv2", cols(a["conv_w_2"][0])); put("conv2b", cols(a["conv_b_2"][0]))
    put("ba", cols(a["b_rg_a_2"][0])); put("bx", cols(a["b_rg_x_2"][0])); put("lam", cols(a["lru_lambda_2"][0]))
    put("gattn", cols(a["g_attn_out_2"][0][perm])); put("glru", cols(a["g_lru_out_2"][0]))
    put("sink", np.broadcast_to(a["sinks_2"][0], (P, 8)))
    put("eps", np.full((P, 1), EPS, np.float32))
    put("brout", np.broadcast_to(a["b_router_2"][0], (P, NEXP)))

    w = a["w_in"][0]
    kp = np.zeros((D, P), np.float32)
    kp[:, NOPE:QD] = w[:, QR + KVR:QR + KVR + ROPE]
    w2 = a["w_in_2"][0]
    wo2 = a["w_out_2"][0]
    blk = np.concatenate([
        blocks(w[:, 0:QR + KVR]), blocks(kp), blocks(w[:, QR + KVR + ROPE:]), blocks(a["w_o"][0]),
        blocks(a["w_fourier"][0]), blocks(w2[:, 768:1280]), blocks(w2[:, 0:512][:, perm]), blocks(w2[:, 512:640]),
        blocks(w2[:, 640:768]), blocks(w2[:, 1280:1792]), blocks(np.concatenate([wo2[0:512][perm], wo2[512:]]))])
    uq = a["w_uq"][0].reshape(3, P, HEADS * QD).transpose(1, 0, 2)
    uk = a["w_ukv"][0].reshape(2, P, HEADS, 2, NOPE).transpose(1, 0, 3, 2, 4).reshape(P, 2, 2 * HEADS * NOPE)
    ffa = np.stack([np.stack([a[n][l].reshape(DJ, P, NF, P).transpose(2, 1, 0, 3).reshape(NF, P, D)
                              for n in ("ffn_w1", "ffn_w3")], 2).reshape(NF, P, FA) for l in range(2)])
    con, tab = constants()
    arrays = {
        "xT": feature_major(a["x"][0]), "xc": feature_major(a["ctx"][0]).reshape(P, -1), "vec": v, "con": con, "tab": tab,
        "ada": np.concatenate([a["ada_w"], a["w_ada_2"]]), "blk": blk, "uq": uq, "uk": uk, "ffa": ffa,
        "ffb": a["ffn_w2"].reshape(2, NF, P, D), "rga": a["w_rg_a_2"][0], "rgx": a["w_rg_x_2"][0],
        "rout": a["w_router_2"][0].reshape(DJ, P, NEXP).transpose(1, 0, 2), "gu": a["w_gu_2"][0], "bgu": a["b_gu_2"][0],
        "dn": a["w_down_2"][0], "bdn": a["b_down_2"][0],
    }
    arrays = {k + "_dram": np.ascontiguousarray(x) for k, x in arrays.items()}
    nc = bacc.Bacc("TRN2", target_bir_lowering=False, num_devices=1)
    args = [nc.dram_tensor(k, x.shape, mybir.dt.from_np(x.dtype), kind="ExternalInput").ap() for k, x in arrays.items()]
    args.append(nc.dram_tensor("out_dram", (P, DJ, T), mybir.dt.float32, kind="ExternalOutput").ap())
    build(nc, *args)
    r = run_bass_kernel_spmd(nc, [arrays], core_ids=[0])
    out = r.results[0]["out_dram"]
    return np.ascontiguousarray(np.asarray(out).transpose(2, 1, 0).reshape(1, T, D))
```
